# Optimizing a Trainium2 kernel written in Bass

```python
import jax, jax.numpy as jnp
from jax import lax
import numpy as np

D_MODEL = 1024
BATCH = 1
SEQ = 128
DEPTH = 2
DEC_BATCH = 1
DEC_SEQ = 256
PAST_LEN = 128

GRID_W = 64
N_MIXERS = 2
N_RWKV_LAYERS = (DEPTH + 1) // 2
N_NA_LAYERS = DEPTH // 2
HEAD_DIM = 64
N_HEADS = D_MODEL // HEAD_DIM
DECAY_LORA = 64
ICLR_LORA = 64
GATE_LORA = 128
WIN_ROWS = 8
WIN_COLS = 16
N_GROUPS = 4
EXPERTS_PER_GROUP = 4
N_EXPERTS = N_GROUPS * EXPERTS_PER_GROUP
TOP_K_IN_GROUP = 2
D_EXPERT = 256
N_MOD = 6
NORM_EPS = 1e-6
GN_EPS = 64e-5
ATTN_BLOCK = 128

kernel_name = 'bidir_rwkv7_natten_hmoe_step'

def rmsnorm(x, g):
    xf = x.astype(jnp.float32)
    y = xf * lax.rsqrt(jnp.mean(xf * xf, axis=-1, keepdims=True) + NORM_EPS)
    return (y * g.astype(jnp.float32)).astype(x.dtype)

def modulation(cvec, ada_w, ada_b):
    m = jax.nn.silu(cvec) @ ada_w + ada_b
    return jnp.split(jnp.expand_dims(m, -2), N_MOD, axis=-1)

def modulate(x, g, shift, scale):
    return rmsnorm(x, g) * (1 + scale) + shift

def centred_shift(x):
    xp = jnp.pad(x, ((0, 0), (1, 1), (0, 0)))
    return 0.5 * (xp[:, :-2] + xp[:, 2:])

def wkv_scan(r, w, k, v, a, b, s0, reverse):
    def step(S, inp):
        r_t, w_t, k_t, v_t, a_t, b_t = inp
        sa = jnp.einsum('bhij,bhj->bhi', S, a_t)
        S = (S * w_t[..., None, :] + v_t[..., :, None] * k_t[..., None, :]
             + sa[..., :, None] * b_t[..., None, :])
        return S, jnp.einsum('bhij,bhj->bhi', S, r_t)
    xs = tuple(jnp.swapaxes(t.astype(jnp.float32), 0, 1) for t in (r, w, k, v, a, b))
    S, ys = lax.scan(step, s0.astype(jnp.float32), xs, reverse=reverse)
    return jnp.swapaxes(ys, 0, 1), S

def rwkv_time_mix(h, s0, mu, w_r, w_k, w_v, w_o, w0, w1, w2, a0, a1, a2,
                  g1, g2, k_k, k_a, r_k, lnx_g, lnx_b):
    B, T, D = h.shape

    def heads(t):
        return t.reshape(B, T, N_HEADS, HEAD_DIM)

    dx = centred_shift(h) - h
    xr, xw, xk, xv, xa, xg = [h + dx * mu[n] for n in range(6)]
    r = heads(xr @ w_r)
    k_raw = xk @ w_k
    k = heads(k_raw)
    v = heads(xv @ w_v)
    g = jax.nn.sigmoid(xg @ g1) @ g2
    kk = heads(k_raw * k_k).astype(jnp.float32)
    kk = (kk / jnp.maximum(jnp.sqrt(jnp.sum(kk * kk, -1, keepdims=True)), 1e-12)).astype(h.dtype)
    k_a_h = k_a.reshape(N_HEADS, HEAD_DIM)
    y_sum = jnp.zeros((B, T, N_HEADS, HEAD_DIM), jnp.float32)
    bonus = jnp.zeros((B, T, N_HEADS, HEAD_DIM), jnp.float32)
    finals = []
    for d in range(2):
        logw = -jax.nn.softplus(-(w0[d] + jnp.tanh(xw @ w1[d]) @ w2[d]).astype(jnp.float32)) - 0.5
        decay = heads(jnp.exp(-jnp.exp(logw)))
        a = heads(jax.nn.sigmoid(a0[d] + (xa @ a1[d]) @ a2[d]))
        k_d = k * (1 + (a - 1) * k_a_h)
        y_d, s_d = wkv_scan(r, decay, k_d, v, -kk, kk * a, s0[:, d], reverse=(d == 1))
        y_sum = y_sum + y_d
        bonus = bonus + jnp.sum((r * k_d * r_k).astype(jnp.float32), -1, keepdims=True) * v.astype(jnp.float32)
        finals.append(s_d)
    mean = jnp.mean(y_sum, -1, keepdims=True)
    var = jnp.mean(jnp.square(y_sum - mean), -1, keepdims=True)
    yn = ((y_sum - mean) * lax.rsqrt(var + GN_EPS)).reshape(B, T, D) * lnx_g + lnx_b
    y = (yn + bonus.reshape(B, T, D)).astype(h.dtype)
    return (y * g) @ w_o, jnp.stack(finals, axis=1)

def na_qkv(h, w_qkv):
    B, T, _ = h.shape
    q, k, v = jnp.split(h @ w_qkv, 3, axis=-1)
    shp = (B, T, N_HEADS, HEAD_DIM)
    return q.reshape(shp), k.reshape(shp), v.reshape(shp)

def ctx_attention(q, k, v):
    B, L = q.shape[:2]
    nb = L // ATTN_BLOCK
    qb = jnp.moveaxis(q.reshape(B, nb, ATTN_BLOCK, N_HEADS, HEAD_DIM), 1, 0)
    scale = HEAD_DIM ** -0.5

    def block(qi):
        s = jnp.einsum('bqhd,blhd->bhql', qi, k).astype(jnp.float32) * scale
        p = jax.nn.softmax(s, axis=-1).astype(v.dtype)
        return jnp.einsum('bhql,blhd->bqhd', p, v)

    o = lax.map(block, qb)
    return jnp.moveaxis(o, 0, 1).reshape(B, L, N_HEADS * HEAD_DIM)

def latent_neighbourhood_attention(q, k, v, k_ctx, v_ctx, rpb):
    B, T = q.shape[:2]
    rows = T // GRID_W
    kr = min(WIN_ROWS, rows)
    kc = WIN_COLS
    qb = WIN_COLS
    cb = 2 * WIN_COLS
    nqb = GRID_W // qb
    scale = HEAD_DIM ** -0.5
    q5 = q.reshape(B, rows, nqb, qb, N_HEADS, HEAD_DIM)
    k4 = k.reshape(B, rows, GRID_W, N_HEADS, HEAD_DIM)
    v4 = v.reshape(B, rows, GRID_W, N_HEADS, HEAD_DIM)
    r_ar = jnp.arange(rows)
    row_idx = jnp.clip(r_ar - kr // 2, 0, rows - kr)[:, None] + jnp.arange(kr)
    col_band = jnp.clip(jnp.arange(nqb) * qb - kc // 2, 0, GRID_W - cb)[:, None] + jnp.arange(cb)
    qcol = jnp.arange(GRID_W).reshape(nqb, qb)
    q_cstart = jnp.clip(qcol - kc // 2, 0, GRID_W - kc)
    col_mask = ((col_band[:, None, :] >= q_cstart[..., None])
                & (col_band[:, None, :] < q_cstart[..., None] + kc))
    ridx = row_idx[:, None, :, None]
    cidx = col_band[None, :, None, :]
    k_blk = k4[:, ridx, cidx]
    v_blk = v4[:, ridx, cidx]
    dr = row_idx - r_ar[:, None]
    dc = jnp.clip(col_band[:, None, :] - qcol[..., None], -(kc - 1), kc - 1)
    bias = rpb[:, dr[:, None, None, :, None] + WIN_ROWS - 1,
               dc[None, :, :, None, :] + WIN_COLS - 1].astype(jnp.float32)
    s_loc = jnp.einsum('brjqhd,brjkwhd->bhrjqkw', q5, k_blk).astype(jnp.float32) * scale + bias
    s_loc = jnp.where(col_mask[:, :, None, :], s_loc, -jnp.inf)
    s_ctx = jnp.einsum('brjqhd,blhd->bhrjql', q5, k_ctx).astype(jnp.float32) * scale
    n_loc = kr * cb
    s = jnp.concatenate([s_loc.reshape(B, N_HEADS, rows, nqb, qb, n_loc), s_ctx], axis=-1)
    p = jax.nn.softmax(s, axis=-1).astype(v.dtype)
    p_loc = p[..., :n_loc].reshape(B, N_HEADS, rows, nqb, qb, kr, cb)
    p_ctx = p[..., n_loc:]
    o = (jnp.einsum('bhrjqkw,brjkwhd->brjqhd', p_loc, v_blk)
         + jnp.einsum('bhrjql,blhd->brjqhd', p_ctx, v_ctx))
    return o.reshape(B, T, N_HEADS * HEAD_DIM)

def hier_moe(x, w_grp, b_grp, w_exp, b_exp, w1, w3, w2):
    shp = x.shape
    xt = x.reshape(-1, shp[-1])
    pg = jax.nn.softmax((xt @ w_grp + b_grp).astype(jnp.float32), axis=-1)
    p_sel, g_sel = lax.top_k(pg, 1)
    le = (xt @ w_exp + b_exp).astype(jnp.float32).reshape(-1, N_GROUPS, EXPERTS_PER_GROUP)
    le_g = jnp.take_along_axis(le, g_sel[:, :, None], axis=1)[:, 0]
    vals, idx = lax.top_k(jax.nn.softmax(le_g, axis=-1), TOP_K_IN_GROUP)
    wts = p_sel * vals / jnp.sum(vals, -1, keepdims=True)
    eidx = g_sel * EXPERTS_PER_GROUP + idx
    gate = jnp.sum(jax.nn.one_hot(eidx, N_EXPERTS, dtype=jnp.float32) * wts[..., None], axis=1).astype(x.dtype)
    hid = jax.nn.silu(jnp.einsum('nd,edf->nef', xt, w1)) * jnp.einsum('nd,edf->nef', xt, w3)
    y = jnp.einsum('nef,efd->nd', hid * gate[..., None], w2)
    return y.reshape(shp)

def setup_inputs(seed: int = 0) -> dict:
    key = jax.random.key(seed)
    keys = iter(jax.random.split(key, 64))
    f32 = jnp.float32
    D, H, N = D_MODEL, N_HEADS, HEAD_DIM
    NA, NB = N_RWKV_LAYERS, N_NA_LAYERS

    def nrm(shape, scale):
        return scale * jax.random.normal(next(keys), shape, f32)

    def unif(shape, lo, hi):
        return jax.random.uniform(next(keys), shape, f32, lo, hi)

    return {
        'x_prompt': nrm((BATCH, SEQ, D), 1.0),
        'x_sample': nrm((DEC_BATCH, DEC_SEQ, D), 1.0),
        'c': nrm((DEC_BATCH, D), 1.0),
        'state_rwkv': nrm((DEC_BATCH, NA, 2, H, N, N), 0.5),
        'cache_na_k': nrm((DEC_BATCH, NB, PAST_LEN, H, N), 1.0),
        'cache_na_v': nrm((DEC_BATCH, NB, PAST_LEN, H, N), 1.0),
        'c_ctx': nrm((D,), 1.0),
        'norm_mix': 1.0 + nrm((DEPTH, D), 0.1),
        'norm_ffn': 1.0 + nrm((DEPTH, D), 0.1),
        'ada_w': nrm((DEPTH, D, N_MOD * D), 0.5 * D ** -0.5),
        'ada_b': nrm((DEPTH, N_MOD * D), 0.02),
        'rwkv_mu': unif((NA, 6, D), 0.0, 1.0),
        'rwkv_w_r': nrm((NA, D, D), D ** -0.5),
        'rwkv_w_k': nrm((NA, D, D), D ** -0.5),
        'rwkv_w_v': nrm((NA, D, D), D ** -0.5),
        'rwkv_w_o': nrm((NA, D, D), D ** -0.5),
        'rwkv_w0': unif((NA, 2, D), -5.0, 0.0),
        'rwkv_w1': nrm((NA, 2, D, DECAY_LORA), D ** -0.5),
        'rwkv_w2': nrm((NA, 2, DECAY_LORA, D), 0.5 * DECAY_LORA ** -0.5),
        'rwkv_a0': nrm((NA, 2, D), 0.5),
        'rwkv_a1': nrm((NA, 2, D, ICLR_LORA), D ** -0.5),
        'rwkv_a2': nrm((NA, 2, ICLR_LORA, D), ICLR_LORA ** -0.5),
        'rwkv_g1': nrm((NA, D, GATE_LORA), D ** -0.5),
        'rwkv_g2': nrm((NA, GATE_LORA, D), GATE_LORA ** -0.5),
        'rwkv_k_k': 0.85 + nrm((NA, D), 0.05),
        'rwkv_k_a': 1.0 + nrm((NA, D), 0.05),
        'rwkv_r_k': nrm((NA, H, N), 0.1),
        'rwkv_lnx_g': 1.0 + nrm((NA, D), 0.1),
        'rwkv_lnx_b': nrm((NA, D), 0.01),
        'na_w_qkv': nrm((NB, D, 3 * D), D ** -0.5),
        'na_w_o': nrm((NB, D, D), D ** -0.5),
        'na_rpb': nrm((NB, H, 2 * WIN_ROWS - 1, 2 * WIN_COLS - 1), 0.5),
        'moe_w_grp': nrm((DEPTH, D, N_GROUPS), D ** -0.5),
        'moe_b_grp': nrm((DEPTH, N_GROUPS), 0.01),
        'moe_w_exp': nrm((DEPTH, D, N_EXPERTS), D ** -0.5),
        'moe_b_exp': nrm((DEPTH, N_EXPERTS), 0.01),
        'moe_w1': nrm((DEPTH, N_EXPERTS, D, D_EXPERT), D ** -0.5),
        'moe_w3': nrm((DEPTH, N_EXPERTS, D, D_EXPERT), D ** -0.5),
        'moe_w2': nrm((DEPTH, N_EXPERTS, D_EXPERT, D), D_EXPERT ** -0.5),
        'final_norm': 1.0 + nrm((D,), 0.1),
    }

def reference(x_prompt, x_sample, c, state_rwkv, cache_na_k, cache_na_v, c_ctx,
              norm_mix, norm_ffn, ada_w, ada_b,
              rwkv_mu, rwkv_w_r, rwkv_w_k, rwkv_w_v, rwkv_w_o, rwkv_w0, rwkv_w1, rwkv_w2,
              rwkv_a0, rwkv_a1, rwkv_a2, rwkv_g1, rwkv_g2, rwkv_k_k, rwkv_k_a, rwkv_r_k,
              rwkv_lnx_g, rwkv_lnx_b,
              na_w_qkv, na_w_o, na_rpb,
              moe_w_grp, moe_b_grp, moe_w_exp, moe_b_exp, moe_w1, moe_w3, moe_w2,
              final_norm):
    y_p, y_s = x_prompt, x_sample
    new_states, new_k, new_v = [], [], []
    for i in range(DEPTH):
        j = i // N_MIXERS
        sh_p, sc_p, gt_p, sh2_p, sc2_p, gt2_p = modulation(c_ctx, ada_w[i], ada_b[i])
        sh_s, sc_s, gt_s, sh2_s, sc2_s, gt2_s = modulation(c, ada_w[i], ada_b[i])
        h_p = modulate(y_p, norm_mix[i], sh_p, sc_p)
        h_s = modulate(y_s, norm_mix[i], sh_s, sc_s)
        if i % N_MIXERS == 0:
            rw = (rwkv_mu[j], rwkv_w_r[j], rwkv_w_k[j], rwkv_w_v[j], rwkv_w_o[j],
                  rwkv_w0[j], rwkv_w1[j], rwkv_w2[j], rwkv_a0[j], rwkv_a1[j], rwkv_a2[j],
                  rwkv_g1[j], rwkv_g2[j], rwkv_k_k[j], rwkv_k_a[j], rwkv_r_k[j],
                  rwkv_lnx_g[j], rwkv_lnx_b[j])
            s_zero = jnp.zeros((y_p.shape[0], 2, N_HEADS, HEAD_DIM, HEAD_DIM), jnp.float32)
            o_p, st = rwkv_time_mix(h_p, s_zero, *rw)
            o_s, _ = rwkv_time_mix(h_s, state_rwkv[:, j], *rw)
            new_states.append(st)
        else:
            q_p, k_p, v_p = na_qkv(h_p, na_w_qkv[j])
            o_p = ctx_attention(q_p, k_p, v_p) @ na_w_o[j]
            q_s, k_s, v_s = na_qkv(h_s, na_w_qkv[j])
            o_s = latent_neighbourhood_attention(q_s, k_s, v_s, cache_na_k[:, j], cache_na_v[:, j],
                                                 na_rpb[j]) @ na_w_o[j]
            new_k.append(k_p)
            new_v.append(v_p)
        y_p = y_p + gt_p * o_p
        y_s = y_s + gt_s * o_s
        moe = (moe_w_grp[i], moe_b_grp[i], moe_w_exp[i], moe_b_exp[i], moe_w1[i], moe_w3[i], moe_w2[i])
        y_p = y_p + gt2_p * hier_moe(modulate(y_p, norm_ffn[i], sh2_p, sc2_p), *moe)
        y_s = y_s + gt2_s * hier_moe(modulate(y_s, norm_ffn[i], sh2_s, sc2_s), *moe)
    y_prompt = rmsnorm(y_p, final_norm)
    y_sample = rmsnorm(y_s, final_norm)
    new_state_rwkv = jnp.stack(new_states, axis=1)
    new_cache_na_k = jnp.stack(new_k, axis=1)
    new_cache_na_v = jnp.stack(new_v, axis=1)
    return (y_prompt, y_sample, new_state_rwkv, new_cache_na_k, new_cache_na_v)


_drawn_inputs = setup_inputs


def setup_inputs(seed=0):
    import zlib

    import numpy as np

    out = dict(_drawn_inputs(seed))
    spreads = {}
    factors = {'rwkv_lnx_g': 2.713,
     'rwkv_lnx_b': 24.014,
     'na_rpb': 13.297,
     'moe_b_grp': 16.513,
     'moe_b_exp': 29.573,
     'cache_na_k': 3.292,
     'cache_na_v': 2.688}
    for name, (base, spread) in spreads.items():
        noise = np.random.default_rng([zlib.crc32(name.encode()), seed]).standard_normal(out[name].shape)
        drawn = base * np.exp(spread * noise) if base else spread * noise
        out[name] = __import__('jax').numpy.asarray(drawn.astype(out[name].dtype))
    for name, factor in factors.items():
        out[name] = (out[name] * factor).astype(out[name].dtype)
    return out
```

```python
from contextlib import ExitStack

import numpy as np
import concourse.bass as bass
from concourse import mybir

F32 = mybir.dt.float32
BF16 = mybir.dt.bfloat16
ALU = mybir.AluOpType
ACT = mybir.ActivationFunctionType
AX = mybir.AxisListType

P = 128
D = 1024
DC = D // P
CTX, LAT = 128, 256
T = CTX + LAT
NT = T // P
H, HD = 16, 64
NS = 6
PIECE = 2048
NE, DE = 16, 256
NG, EPG = 4, 4
LEVELS = 6
DECAY = float(np.exp(-0.5))
EPS, GN_EPS = 1e-6, 64e-5
GRID, ROWS = 64, LAT // 64
WIN_C = 16
BIG = 1e30

V_NMIX, V_NFFN, V_FIN, V_C, V_CCTX, V_MU, V_KK, V_KA, V_RK = 0, 16, 32, 40, 48, 56, 104, 112, 120
V_W0, V_A0, V_LG, V_LB, V_ADAB = 128, 144, 160, 168, 176
NV = 272

SLAB = 3096
S_Y, S_PF, S_PB, S_AF, S_AB, S_R, S_K, S_V, S_NKK = range(9)
NSLAB = 9


def constants():
    s = np.arange(P)
    same = (s[:, None] // HD) == (s[None, :] // HD)
    out = {
        "c_ident": np.eye(P),
        "c_mean": np.full((P, P), 1.0 / D),
        "c_block": same * 1.0,
    }
    hs = np.zeros((P, DC, H))
    for c in range(DC):
        for p in range(P):
            hs[p, c, 2 * c + p // HD] = 1.0
    out["c_headsum"] = hs.reshape(P, DC * H)
    out["c_headcast"] = np.ascontiguousarray(hs.transpose(2, 1, 0)).reshape(H, DC * P)
    reset = np.ones((P, NT, P + 1))
    reset[:, :, 0] = 0.0
    out["c_reset"] = reset.reshape(P, NT * (P + 1))
    earlier = s[:, None] < s[None, :]
    causal = np.zeros((P, 2, 2, P))
    causal[:, 0, 0], causal[:, 0, 1] = earlier, earlier | np.eye(P, dtype=bool)
    causal[:, 1, 0], causal[:, 1, 1] = earlier.T, earlier.T | np.eye(P, dtype=bool)
    out["c_causal"] = causal.reshape(P, 4 * P)
    level = np.zeros((P, 2, LEVELS + 1, HD))
    for l in range(LEVELS + 1):
        m = 1 << l
        for d in range(2):
            early = [n for n in range(P) if (n // m) % 2 == d]
            for j, n in enumerate(early):
                for t in range(P):
                    level[t, d, l, j] = float(t // (2 * m) == n // (2 * m) and (t // m) % 2 != d)
    out["c_level"] = level.reshape(P, 2 * (LEVELS + 1) * HD)
    col = np.arange(GRID)
    start = np.clip(col - WIN_C // 2, 0, GRID - WIN_C)[:, None]
    cap = np.where((col[None] >= start) & (col[None] < start + WIN_C), 3e38, -BIG)
    out["c_cap"] = np.concatenate([cap[::-1], cap[::-1]])
    out["c_order"] = np.tile(np.arange(EPG, 0, -1.0), (P, NT)).reshape(P, NT * EPG)
    return {k: np.ascontiguousarray(v, dtype=np.float32) for k, v in out.items()}


class Kernel:

    def __init__(self, nc, a, ctx):
        self.nc, self.a, self.ctx = nc, a, ctx
        self.taken = 0
        self.arrival = []
        self.used = {}
        self.plan = []
        sb = self.sb
        self.slab = sb("slab", [P, NSLAB, SLAB])
        self.ring = sb("ring", [P, NS, PIECE])
        self.ws = sb("ws", [P, 9984])
        self.ident = sb("ident", [P, P])
        self.mean = sb("mean", [P, P])
        self.vec = sb("vec", [P, NV])
        self.mod = sb("mod", [P, 48, 2])
        self.silu_c = sb("silu_c", [P, DC, 2])
        self.omka = sb("omka", [P, DC])
        self.sgate = sb("sgate", [P, T])
        self.s0t = sb("s0t", [P, 2, DC, HD])
        self.ep0 = sb("ep0", [P, 2, DC, NT])
        self.epe = sb("epe", [P, 2, DC, NT])
        self.headsum = sb("headsum", [P, DC, H])
        self.causal = sb("causal", [P, 2, 2, P], BF16)
        self.level = sb("level", [P, 2, LEVELS + 1, HD], BF16)
        self.psum = ctx.enter_context(nc.psum_tensor("psum", [P, 8, 512], F32))
        self.ring_in = [nc.alloc_semaphore(name=f"ring_in{i}") for i in range(NS)]
        self.phase_sems = []

    def sb(self, name, shape, dt=F32):
        return self.ctx.enter_context(self.nc.sbuf_tensor(name, shape, dt))

    def sem(self, name):
        self.phase_sems.append(self.nc.alloc_semaphore(name=name))
        return self.phase_sems[-1]

    def block(self):
        def run(body):
            with self.nc.Block() as block:
                body(block)
            self.nc.clear_and_free_semaphores(self.phase_sems)
            self.nc.all_engine_barrier()
            self.phase_sems = []
        return run

    def act3(self, s):
        return self.slab[:, s, 0:DC * T].rearrange("p (c t) -> p c t", c=DC)

    def tok3(self, s):
        return self.slab[:, s, 0:NT * D].rearrange("p (n d) -> p n d", n=NT)

    def p4(self, s):
        return self.slab[:, s, :].rearrange("p (c n t) -> p c n t", c=DC, n=NT)


def cols(w, j):
    return w[:, j * 256:(j + 1) * 256].rearrange("(c p) n -> p c n", p=P)


def add_pieces(k):
    a = k.a

    def whole(src, parts=DC):
        return lambda slot: [(k.ring[:, slot, :].rearrange("p (c n) -> p c n", c=parts), src)]

    def lora_in(slot):
        w = k.ring[:, slot, :].rearrange("p (g c n) -> p g c n", g=2, c=DC)
        return ([(w[:, 0, :, 64 * d:64 * d + 64], a["rwkv_w1"][0, d].rearrange("(c p) n -> p c n", p=P))
                 for d in range(2)]
                + [(w[:, 1, :, 64 * d:64 * d + 64], a["rwkv_a1"][0, d].rearrange("(c p) n -> p c n", p=P))
                   for d in range(2)])

    def gate_in(slot):
        w = k.ring[:, slot, 0:D].rearrange("p (c n) -> p c n", c=DC)
        return [(w, a["rwkv_g1"][0].rearrange("(c p) n -> p c n", p=P))]

    def lora_out(slot):
        return [(k.ring[:, slot, 0:D], a["rwkv_w2"][0].rearrange("d r n -> (d r) n")),
                (k.ring[:, slot, D:2 * D], a["rwkv_a2"][0].rearrange("d r n -> (d r) n"))]

    def gate_out(slot):
        return [(k.ring[:, slot, 0:D], a["rwkv_g2"][0])]

    plan = [whole(cols(a["ada_w"][0], j)) for j in range(24)]
    plan += [lora_in, gate_in]
    for n in ("rwkv_w_r", "rwkv_w_k", "rwkv_w_v"):
        plan += [whole(cols(a[n][0], j)) for j in range(4)]
    plan += [lora_out, gate_out] + [whole(cols(a["rwkv_w_o"][0], j)) for j in range(4)] + [None] * 4

    def experts(layer):
        w1, w3 = ([whole(cols(a[n][layer, e], 0)) for e in range(NE)] for n in ("moe_w1", "moe_w3"))
        w2 = [whole(a["moe_w2"][layer, e].rearrange("(f p) n -> p f n", p=P), 2) for e in range(NE)]
        out = [w1[0], w3[0]]
        for e in range(NE):
            out += ([w1[e + 1], w3[e + 1]] if e + 1 < NE else []) + [w2[e]]
        return out

    plan += experts(0) + [whole(cols(a["ada_w"][1], j)) for j in range(24)]
    plan += [whole(cols(a["na_w_qkv"][0], j)) for j in range(12)]
    plan += [whole(cols(a["na_w_o"][0], j)) for j in range(4)] + [None] * 2 + experts(1)
    k.plan = plan
    raised = [0] * NS
    for n, piece in enumerate(plan):
        raised[n % NS] += 16 * len(piece(n % NS)) if piece else 0
        k.arrival.append(raised[n % NS])


def load_piece(k, eng, n):
    if n >= len(k.plan) or k.plan[n] is None:
        return
    slot = n % NS
    if n - NS in k.used:
        sem, value = k.used[n - NS]
        eng.wait_ge(sem, value)
    for dst, src in k.plan[n](slot):
        eng.dma_start(dst, src).then_inc(k.ring_in[slot], 16)


def take_piece(k, eng, n):
    eng.wait_ge(k.ring_in[n % NS], k.arrival[n])
    return k.ring[:, n % NS, :]


def prefetch(k, eng, first, last):
    for n in range(first + NS, last + NS):
        load_piece(k, eng, n)


def piece_cols(w):
    return w.rearrange("p (c n) -> p c n", c=DC)
def load_tokens(k, eng, dst, sem):
    eng.dma_start(dst[:, 0, :], k.a["x_prompt"][0]).then_inc(sem, 16)
    eng.dma_start(dst[:, 1:NT, :], k.a["x_sample"][0].rearrange("(n p) d -> p n d", p=P)).then_inc(sem, 16)


def phase_inputs(k):
    nc, a = k.nc, k.a
    consts_in, vec_in, x_in = k.sem("consts_in"), k.sem("vec_in"), k.sem("x_in")
    vec_t, vec_ok, x_t, x_half = k.sem("vec_t"), k.sem("vec_ok"), k.sem("x_t"), k.sem("x_half")
    sig_c, masks_in = k.sem("sig_c"), k.sem("masks_in")
    rows = [k.ws[0:n, 128 * i:128 * i + 128] for i, n in enumerate((128, 48, 96))]
    masks = k.ws[:, 512:512 + 4 * P + 2 * (LEVELS + 1) * HD]
    xt = k.tok3(S_R)
    x3 = k.act3(S_Y)
    vp = k.psum[:, 0, 0:NV]
    pieces = NS

    @k.block()
    def _(block):
        @block.sync
        def _(sp):
            sp.dma_start(k.ident[:], a["c_ident"]).then_inc(consts_in, 16)
            rvecs = [("norm_mix", 0, 16), ("norm_ffn", 16, 16), ("final_norm", 32, 8), ("c", 40, 8), ("c_ctx", 48, 8),
                     ("rwkv_mu", 56, 48), ("rwkv_k_k", 104, 8), ("rwkv_k_a", 112, 8), ("rwkv_r_k", 120, 8)]
            for n, at, m in rvecs:
                sp.dma_start(rows[0][at:at + m, :], flat(a[n])).then_inc(vec_in, 16)
            for n, at, m in (("rwkv_w0", 0, 16), ("rwkv_a0", 16, 16), ("rwkv_lnx_g", 32, 8), ("rwkv_lnx_b", 40, 8)):
                sp.dma_start(rows[1][at:at + m, :], flat(a[n])).then_inc(vec_in, 16)
            sp.dma_start(rows[2], flat(a["ada_b"])).then_inc(vec_in, 16)
            for n in range(pieces):
                load_piece(k, sp, n)

        @block.scalar
        def _(act):
            load_tokens(k, act, xt, x_in)
            act.dma_start(k.mean[:], a["c_mean"]).then_inc(masks_in, 16)
            act.dma_start(k.headsum[:], a["c_headsum"].rearrange("p (c h) -> p c h", c=DC)).then_inc(masks_in, 16)
            act.dma_start(masks[:, 0:4 * P], a["c_causal"]).then_inc(masks_in, 16)
            act.dma_start(masks[:, 4 * P:], a["c_level"]).then_inc(masks_in, 16)
            act.wait_ge(vec_ok, 1)
            c2 = k.vec[:, V_C:V_C + 16].rearrange("p (s c) -> p c s", s=2)
            nc.scalar.activation(k.silu_c[:, :, 0:1], c2[:, :, 1:2], ACT.Silu).then_inc(sig_c, 1)
            nc.scalar.activation(k.silu_c[:, :, 1:2], c2[:, :, 0:1], ACT.Silu).then_inc(sig_c, 1)
            act.wait_ge(x_t, 4)
            nc.scalar.copy(x3[:, 4:8, :], k.psum[:, 4:8, 0:T]).then_inc(x_half, 1)

        @block.gpsimd
        def _(pool):
            pool.wait_ge(masks_in, 64)
            nc.gpsimd.tensor_copy(k.causal[:].rearrange("p d k t -> p (d k t)"), masks[:, 0:4 * P]).then_inc(sig_c, 1)
            nc.gpsimd.tensor_copy(k.level[:].rearrange("p d l t -> p (d l t)"), masks[:, 4 * P:]).then_inc(sig_c, 1)

        @block.tensor
        def _(pe):
            pe.wait_ge(consts_in, 16)
            pe.wait_ge(vec_in, 16 * 14)
            at = 0
            for r in rows:
                n = r.shape[0]
                last = nc.tensor.transpose(vp[:, at:at + n], r, k.ident[0:n, 0:n])
                at += n
            last.then_inc(vec_t, 1)
            pe.wait_ge(x_in, 32)
            for c in range(DC - 1, -1, -1):
                if c == 0:
                    pe.wait_ge(vec_ok, 1)
                for n in range(NT):
                    last = nc.tensor.transpose(k.psum[:, c, n * P:(n + 1) * P], xt[:, n, c * P:(c + 1) * P], k.ident[:])
                last.then_inc(x_t, 1)

        @block.vector
        def _(dve):
            dve.wait_ge(vec_t, 1)
            nc.vector.tensor_copy(k.vec[:], vp).then_inc(vec_ok, 1)
            dve.wait_ge(vec_ok, 1)
            nc.vector.tensor_scalar(k.omka[:], k.vec[:, V_KA:V_KA + 8], -1.0, 1.0, ALU.mult, ALU.add).then_inc(x_half, 1)
            dve.wait_ge(x_t, 8)
            nc.vector.tensor_copy(x3[:, 0:4, :], k.psum[:, 0:4, 0:T]).then_inc(x_half, 1)


def flat(ap):
    names = "abcdef"[:len(ap.shape)]
    s = " ".join(names)
    if len(ap.shape) > 1:
        ap = ap.rearrange(f"{s} -> ({s})")
    return ap.rearrange("(r q) -> r q", q=P)


def phase_ada(k, layer):
    nc = k.nc
    first = k.taken
    k.taken += 24
    multiplied = k.sem(f"ada{layer}_multiplied")
    added = k.sem(f"ada{layer}_added")
    acc = k.psum[:, 0, 0:96]

    @k.block()
    def _(block):
        @block.tensor
        def _(pe):
            base = [k.arrival[first + u] for u in range(NS)]
            with pe.Fori(0, 4) as i:
                for u in range(NS):
                    pe.wait_ge(k.ring_in[u], 16 * i + base[u])
                    w = piece_cols(k.ring[:, u, :])
                    for m in range(2):
                        out = acc[:, bass.ds(4 * NS * i + 4 * u + 2 * m, 2)]
                        for c in range(DC):
                            last = nc.tensor.matmul(out, w[:, c, m * P:(m + 1) * P], k.silu_c[:, c, :],
                                                    start=c == 0, stop=c == DC - 1)
                    last.then_inc(multiplied, 1)
            for u in range(NS):
                k.used[first + 18 + u] = (multiplied, 19 + u)

        @block.sync
        def _(sp):
            with sp.Fori(0, 3) as i:
                for u in range(NS):
                    sp.wait_ge(multiplied, NS * i + u + 1)
                    src = k.a["ada_w"][layer][:, bass.ds(256 * NS * i + 256 * (NS + u), 256)]
                    sp.dma_start(piece_cols(k.ring[:, u, :]), src.rearrange("(c p) n -> p c n", p=P)).then_inc(k.ring_in[u], 16)
            prefetch(k, sp, first + 18, first + 24)

        @block.vector
        def _(dve):
            dve.wait_ge(multiplied, 24)
            bias = k.vec[:, V_ADAB + 48 * layer:V_ADAB + 48 * layer + 48]
            nc.vector.tensor_tensor(k.mod[:], acc.rearrange("p (j s) -> p j s", s=2),
                                    bias.unsqueeze(2).to_broadcast([P, 48, 2]), ALU.add).then_inc(added, 1)


def phase_norm(k, name, x_slab, h_slab, tmp_slab, v_gain, mod_at):
    nc = k.nc
    squared, summed, meaned, rooted, scaled = (k.sem(f"{name}_{s}") for s in ("squared", "summed", "meaned", "rooted", "scaled"))
    step, out_act = k.sem(f"{name}_step"), k.sem(f"{name}_act")
    x, h, tmp = k.act3(x_slab), k.act3(h_slab), k.act3(tmp_slab)
    acc = k.psum[:, 0, 0:T]
    ms, root, rstd = k.ws[:, 0:T], k.ws[:, T:2 * T], k.ws[:, 2 * T:3 * T]
    gs = k.ws[:, 3 * T:3 * T + 16].rearrange("p (c s) -> p c s", s=2)
    gain = k.vec[:, v_gain:v_gain + DC]

    @k.block()
    def _(block):
        @block.scalar
        def _(act):
            for g in range(4):
                nc.scalar.activation(tmp[:, 2 * g:2 * g + 2, :], x[:, 2 * g:2 * g + 2, :], ACT.Square).then_inc(squared, 1)
            act.wait_ge(meaned, 1)
            nc.scalar.activation(root, ms, ACT.Sqrt).then_inc(rooted, 1)
            if mod_at is not None:
                for c in range(4, DC):
                    act.wait_ge(scaled, c - 3)
                    for s, (t0, t1) in enumerate(((0, CTX), (CTX, T))):
                        nc.scalar.activation(h[:, c, t0:t1], tmp[:, c, t0:t1], ACT.Identity,
                                             bias=k.mod[:, mod_at + c, s:s + 1], scale=gs[:, c, s:s + 1]).then_inc(out_act, 1)

        @block.tensor
        def _(pe):
            for c in range(DC):
                pe.wait_ge(squared, c // 2 + 1)
                last = nc.tensor.matmul(acc, k.mean[:], tmp[:, c, :], start=c == 0, stop=c == DC - 1)
            last.then_inc(summed, 1)

        @block.vector
        def _(dve):
            if mod_at is not None:
                nc.vector.scalar_tensor_tensor(gs, k.mod[:, mod_at + DC:mod_at + 2 * DC, :], 1.0,
                                               gain.unsqueeze(2).to_broadcast([P, DC, 2]), ALU.add, ALU.mult).then_inc(step, 1)
            else:
                nc.vector.tensor_copy(gs[:, :, 0], gain).then_inc(step, 1)
            dve.wait_ge(summed, 1)
            nc.vector.tensor_scalar(ms, acc, EPS, None, ALU.add).then_inc(meaned, 1)
            dve.wait_ge(rooted, 1)
            nc.vector.reciprocal(rstd, root).then_inc(step, 1)
            dve.wait_ge(step, 2)
            for c in list(range(4, DC)) + list(range(4)):
                nc.vector.tensor_tensor(tmp[:, c, :], x[:, c, :], rstd, ALU.mult).then_inc(scaled, 1)
            for c in range(4):
                dve.wait_ge(scaled, c + 5)
                if mod_at is None:
                    nc.vector.tensor_scalar(h[:, c, :], tmp[:, c, :], gs[:, c, 0:1], None, ALU.mult).then_inc(step, 1)
                    nc.vector.tensor_scalar(h[:, c + 4, :], tmp[:, c + 4, :], gs[:, c + 4, 0:1], None, ALU.mult).then_inc(step, 1)
                else:
                    for s, (t0, t1) in enumerate(((0, CTX), (CTX, T))):
                        nc.vector.tensor_scalar(h[:, c, t0:t1], tmp[:, c, t0:t1], gs[:, c, s:s + 1],
                                                k.mod[:, mod_at + c, s:s + 1], ALU.mult, ALU.add).then_inc(step, 1)


def phase_rwkv_project(k):
    nc = k.nc
    first = k.taken
    k.taken += 14
    mixed = k.sem("mixed")
    proj, read_out = k.sem("proj"), k.sem("proj_read")
    step = k.sem("shift_step")
    h, dx = k.act3(S_PF), k.act3(S_PB)
    mix = [k.act3(S_AF), k.act3(S_AB)]
    r3, k3, v3 = k.act3(S_R), k.act3(S_K), k.tok3(S_V)
    t1, t2 = k.ws[:, 0:T], k.ws[:, T:2 * T]
    MIX_ORDER = [1, 4, 5, 0, 2, 3]

    def bank(o):
        return k.psum[:, o % 8, :]

    @k.block()
    def _(block):
        @block.vector
        def _(dve):
            n = 0
            for t0, t1_ in ((0, CTX), (CTX, T)):
                nc.vector.tensor_tensor(dx[:, :, t0 + 1:t1_ - 1], h[:, :, t0:t1_ - 2], h[:, :, t0 + 2:t1_], ALU.add).then_inc(step, 1)
                nc.vector.tensor_copy(dx[:, :, t0:t0 + 1], h[:, :, t0 + 1:t0 + 2]).then_inc(step, 1)
                nc.vector.tensor_copy(dx[:, :, t1_ - 1:t1_], h[:, :, t1_ - 2:t1_ - 1]).then_inc(step, 1)
            dve.wait_ge(step, 6)
            for g in range(2):
                nc.vector.scalar_tensor_tensor(dx[:, 4 * g:4 * g + 4, :], dx[:, 4 * g:4 * g + 4, :], 0.5,
                                               h[:, 4 * g:4 * g + 4, :], ALU.mult, ALU.subtract).then_inc(step, 1)
            dve.wait_ge(step, 8)
            for i, mu in enumerate(MIX_ORDER):
                if i >= 2:
                    dve.wait_ge(proj, i - 1 if i < 5 else 11)
                for c in range(DC):
                    nc.vector.scalar_tensor_tensor(mix[i % 2][:, c, :], dx[:, c, :], k.vec[:, V_MU + 8 * mu + c:V_MU + 8 * mu + c + 1],
                                                   h[:, c, :], ALU.mult, ALU.add).then_inc(mixed, 1)

        @block.tensor
        def _(pe):
            for i in range(3):
                if i != 1:
                    piece = take_piece(k, pe, first + i // 2)
                w = piece_cols(piece[:, D * (i % 2):D * (i % 2) + D])
                for c in range(DC):
                    pe.wait_ge(mixed, 8 * i + c + 1)
                    last = nc.tensor.matmul(bank(i)[:, 0:T], w[:, c, :], mix[i % 2][:, c, :], start=c == 0, stop=c == DC - 1)
                last.then_inc(proj, 1)
            k.used[first], k.used[first + 1] = (proj, 2), (proj, 3)
            o = 3
            for i in range(3, 5):
                for j in range(4):
                    n = first + 2 + 4 * (i - 3) + j
                    w = piece_cols(take_piece(k, pe, n))
                    for m in range(2):
                        if o >= 8:
                            pe.wait_ge(read_out, o - 7)
                        for c in range(DC):
                            if j == 0 and m == 0:
                                pe.wait_ge(mixed, 8 * i + c + 1)
                            last = nc.tensor.matmul(bank(o)[:, 0:T], w[:, c, m * P:(m + 1) * P], mix[i % 2][:, c, :],
                                                    start=c == 0, stop=c == DC - 1)
                        last.then_inc(proj, 1)
                        o += 1
                    k.used[n] = (proj, o)
            for j in range(4):
                w = piece_cols(take_piece(k, pe, first + 10 + j))
                for n in range(NT):
                    pe.wait_ge(read_out, o - 7)
                    for c in range(DC):
                        if j == 0 and n == 0:
                            pe.wait_ge(mixed, 40 + c + 1)
                        last = nc.tensor.matmul(bank(o)[:, 0:256], mix[1][:, c, n * P:(n + 1) * P], w[:, c, :],
                                                start=c == 0, stop=c == DC - 1)
                    last.then_inc(proj, 1)
                    o += 1
                k.used[first + 10 + j] = (proj, o)

        @block.sync
        def _(sp):
            prefetch(k, sp, first, first + 14)

        @block.scalar
        def _(act):
            act.wait_ge(proj, 1)
            nc.scalar.activation(t1, bank(0)[:, 0:T], ACT.Tanh).then_inc(read_out, 1)
            act.wait_ge(proj, 2)
            nc.scalar.copy(t2, bank(1)[:, 0:T]).then_inc(read_out, 1)
            act.wait_ge(proj, 3)
            nc.scalar.activation(k.sgate[:], bank(2)[:, 0:T], ACT.Sigmoid).then_inc(read_out, 1)
            o = 3
            for dst in (r3, k3):
                for c in range(DC):
                    act.wait_ge(proj, o + 1)
                    nc.scalar.copy(dst[:, c, :], bank(o)[:, 0:T]).then_inc(read_out, 1)
                    o += 1
            for j in range(4):
                for n in range(NT):
                    act.wait_ge(proj, o + 1)
                    nc.scalar.copy(v3[:, n, 256 * j:256 * j + 256], bank(o)[:, 0:256]).then_inc(read_out, 1)
                    o += 1


def phase_rwkv_rates(k):
    nc = k.nc
    first = k.taken
    k.taken += 1
    names = ("z_done", "z_read", "consts2_in", "scanned", "kk_scaled", "kk_squared", "kk_summed", "kk_copied", "kk_rooted",
             "kk_floored", "kk_inverse", "cast_done", "nkk_ok", "state_in", "state_turned", "state_ok", "edges_ok", "mid_ok",
             "centred", "edge_zero")
    (z_done, z_read, consts2, scanned, kk_scaled, kk_squared, kk_summed, kk_copied, kk_rooted, kk_floored, kk_inverse,
     cast_done, nkk_ok, state_in, state_turned, state_ok, edges_ok, mid_ok, centred, edge_zero) = (k.sem(n) for n in names)
    t1, t2 = k.ws[:, 0:T], k.ws[:, T:2 * T]
    reset = k.ws[:, 768:768 + NT * (P + 1)]
    cast = k.ws[0:H, 1160:1160 + D].rearrange("h (c p) -> h c p", c=DC)
    norm2, norm, inverse = (k.ws[0:H, 2200 + T * i:2200 + T * i + T] for i in range(3))
    mid = [k.ws[:, 3356 + 24 * d:3356 + 24 * d + 24] for d in range(2)]
    state = k.ws[0:HD, 3410:3410 + 2 * D]
    k3, kk, sq = k.act3(S_K), k.act3(S_NKK), k.act3(S_AF)
    rates = k.p4(S_Y)

    def z_bank(d, c):
        return k.psum[:, 3 * d + c % 3, 0:T]

    @k.block()
    def _(block):
        @block.tensor
        def _(pe):
            w = take_piece(k, pe, first)

            def outer(i, src):
                for d in range(2):
                    rows = slice(HD * d, HD * d + HD)
                    for c in range(DC):
                        o = 16 * i + 8 * d + c
                        if c >= 3:
                            pe.wait_ge(z_read, o - 2)
                        elif i:
                            pe.wait_ge(z_read, 8 * (2 * i + d - 1))
                        nc.tensor.matmul(z_bank(d, c), w[rows, D * i + c * P:D * i + c * P + P], src[rows, :],
                                         start=True, stop=True).then_inc(z_done, 1)

            outer(0, t1)
            pe.wait_ge(consts2, 32)
            for c in range(DC):
                pe.wait_ge(kk_squared, c + 1)
                last = nc.tensor.matmul(k.psum[0:H, 6, 0:T], k.headsum[:, c, :], sq[:, c, :], start=c == 0, stop=c == DC - 1)
            last.then_inc(kk_summed, 1)
            outer(1, t2)
            k.used[first] = (z_done, 32)
            pe.wait_ge(z_read, 32)
            pe.wait_ge(state_in, 16)
            for d in range(2):
                for c in range(DC):
                    last = nc.tensor.transpose(k.psum[:, d, HD * c:HD * c + HD], state[:, D * d + c * P:D * d + c * P + P],
                                               k.ident[0:HD, 0:HD])
            last.then_inc(state_turned, 1)
            pe.wait_ge(kk_inverse, 1)
            for c in range(DC):
                if c >= 4:
                    pe.wait_ge(nkk_ok, c - 3)
                nc.tensor.matmul(k.psum[:, 2 + c % 4, 0:T], cast[:, c, :], inverse, start=True, stop=True).then_inc(cast_done, 1)

        @block.sync
        def _(sp):
            sp.dma_start(reset, k.a["c_reset"]).then_inc(consts2, 16)
            sp.dma_start(k.ws[0:H, 1160:1160 + D], k.a["c_headcast"]).then_inc(consts2, 16)
            sp.dma_start(state.rearrange("i (e h j) -> i e h j", e=2, h=H),
                         k.a["state_rwkv"][0, 0].rearrange("e h i j -> i e h j")).then_inc(state_in, 16)
            prefetch(k, sp, first, first + 1)

        @block.scalar
        def _(act):
            act.wait_ge(edge_zero, 1)
            for d in range(2):
                if d == 1:
                    act.wait_ge(scanned, 8)
                for c in range(DC):
                    act.wait_ge(z_done, 8 * d + c + 1)
                    nc.scalar.activation(rates[:, c, :, 1:P + 1], z_bank(d, c).rearrange("p (n t) -> p n t", n=NT),
                                         ACT.Sigmoid, bias=k.vec[:, V_W0 + 8 * d + c:V_W0 + 8 * d + c + 1]).then_inc(z_read, 1)
            for c in range(DC):
                act.wait_ge(kk_scaled, c + 1)
                nc.scalar.activation(sq[:, c, :], kk[:, c, :], ACT.Square).then_inc(kk_squared, 1)
            act.wait_ge(kk_summed, 1)
            for d in range(2):
                dst = k.act3((S_AF, S_AB)[d])
                for c in range(DC):
                    act.wait_ge(z_done, 16 + 8 * d + c + 1)
                    nc.scalar.activation(dst[:, c, :], z_bank(d, c), ACT.Sigmoid,
                                         bias=k.vec[:, V_A0 + 8 * d + c:V_A0 + 8 * d + c + 1]).then_inc(z_read, 1)
            act.wait_ge(kk_copied, 1)
            nc.scalar.activation(norm, norm2, ACT.Sqrt).then_inc(kk_rooted, 1)
            act.wait_ge(centred, 2)
            for d in range(2):
                p = k.p4((S_PF, S_PB)[d])
                nc.scalar.activation(k.ep0[:, d, :, :], p[:, :, :, 0], ACT.Exp, scale=DECAY).then_inc(edges_ok, 1)
                nc.scalar.activation(k.epe[:, d, :, :], p[:, :, :, P], ACT.Exp, scale=-DECAY).then_inc(edges_ok, 1)

        @block.vector
        def _(dve):
            nc.vector.memset(rates[:, :, :, 0:1], 0.0).then_inc(edge_zero, 1)
            for c in range(DC):
                nc.vector.tensor_scalar(kk[:, c, :], k3[:, c, :], k.vec[:, V_KK + c:V_KK + c + 1], None, ALU.mult).then_inc(kk_scaled, 1)
            dve.wait_ge(consts2, 32)
            for d in range(2):
                p = k.slab[:, (S_PF, S_PB)[d], :].rearrange("p (c t) -> p c t", c=DC)
                src = k.slab[:, S_Y, :].rearrange("p (c t) -> p c t", c=DC)
                for c in range(DC):
                    dve.wait_ge(z_read, 8 * d + c + 1)
                    nc.vector.tensor_tensor_scan(p[:, c, :], reset, src[:, c, :], 0.0, ALU.mult, ALU.add).then_inc(scanned, 1)
            for d in range(2):
                p = k.slab[:, (S_PF, S_PB)[d], :].rearrange("p (n t) -> p n t", t=P + 1)
                dve.wait_ge(scanned, 8 * d + 8)
                nc.vector.tensor_copy(mid[d], p[:, :, P // 2]).then_inc(mid_ok, 1)
                dve.wait_ge(mid_ok, d + 1)
                nc.vector.tensor_tensor(p, p, mid[d].unsqueeze(2).to_broadcast([P, DC * NT, P + 1]), ALU.subtract).then_inc(centred, 1)
            dve.wait_ge(kk_summed, 1)
            nc.vector.tensor_copy(norm2, k.psum[0:H, 6, 0:T]).then_inc(kk_copied, 1)
            dve.wait_ge(kk_rooted, 1)
            nc.vector.tensor_scalar(norm2, norm, 1e-12, -1.0, ALU.max, ALU.mult).then_inc(kk_floored, 1)
            dve.wait_ge(kk_floored, 1)
            nc.vector.reciprocal(inverse, norm2).then_inc(kk_inverse, 1)
            dve.wait_ge(state_turned, 1)
            dve.wait_ge(edges_ok, 4)
            for d, (e, n) in enumerate(((k.ep0, 1), (k.epe, 2))):
                nc.vector.tensor_tensor(k.s0t[:, d, :, :], k.psum[:, d, :].rearrange("p (c i) -> p c i", c=DC),
                                        e[:, d, :, n:n + 1].to_broadcast([P, DC, HD]), ALU.mult).then_inc(state_ok, 1)
            for c in range(DC):
                dve.wait_ge(cast_done, c + 1)
                nc.vector.tensor_tensor(kk[:, c, :], kk[:, c, :], k.psum[:, 2 + c % 4, 0:T], ALU.mult).then_inc(nkk_ok, 1)


def phase_scan(k):
    nc = k.nc
    WORDS = 4992

    def pair(name):
        return [k.sem(f"scan_{name}{d}") for d in range(2)]

    exp_ok, staged, rate_ok, ar_ok, tmp_ok, kb_ok = (pair(n) for n in ("exp_ok", "staged", "rate_ok", "ar_ok", "tmp_ok", "kb_ok"))
    a_done, a_ok, t_done, t_ok, x_done, x_ok, xt_done, xt_ok = (
        pair(n) for n in ("a_done", "a_ok", "t_done", "t_ok", "x_done", "x_ok", "xt_done", "xt_ok"))
    x_init, r_done, r_ok, u_done, u_ok, y_done, y_ok = (
        pair(n) for n in ("x_init", "r_done", "r_ok", "u_done", "u_ok", "y_done", "y_ok"))
    khat_ok, kt_done, kt_ok, s_done, s_copied, s_out, s_step, s_ok = (
        pair(n) for n in ("khat_ok", "kt_done", "kt_ok", "s_done", "s_copied", "s_out", "s_step", "s_ok"))
    zero_ok = k.sem("scan_zero_ok")

    NL = LEVELS + 1
    TILE = [(0, 0), (1, 2), (2, 1)]

    def at(step, q, per, local):
        return q * per + (4 * per * step + local)

    class Dir:
        def __init__(self, d):
            w = k.ws[:, WORDS * d:WORDS * (d + 1)]
            self.ar = w[:, 0:512].rearrange("p (c g t) -> p c g t", c=2, g=2)
            self.kb = w[:, 512:1024].rearrange("p (g c t) -> p g c t", g=2, c=2)
            self.ak = w[:, 1024:2048].rearrange("p (e c g t) -> p e c g t", e=2, c=2, g=2)
            self.ab = w[:, 2048:3072].rearrange("p (e c g t) -> p e c g t", e=2, c=2, g=2)
            self.x = w[:, 3072:3584].rearrange("p (u t) -> p u t", u=4)
            self.kt = w[:, 3072:3584].rearrange("p (g c f) -> p g c f", g=2, c=2)
            self.xt = w[:, 3584:4096].rearrange("p (u t) -> p u t", u=4)
            self.tmp = w[:, 3584:3840].rearrange("p (c t) -> p c t", c=2)
            self.rate = w[:, 3840:4096].rearrange("p (c t) -> p c t", c=2)
            self.t1 = w[:, 4096:4352].rearrange("p (u n) -> p u n", u=4)
            self.r = self.t1
            self.s = w[:, 4096:4224].rearrange("p (c n) -> p c n", c=2)
            self.u = w[:, 4352:4608].rearrange("p (u n) -> p u n", u=4)
            self.v = w[:, 4608:4864].rearrange("p (c e n) -> p c e n", c=2, e=2)
            self.s0 = w[:, 4864:4992].rearrange("p (c n) -> p c n", c=2)
            self.p = k.p4((S_PF, S_PB)[d])
            self.a = k.act3((S_AF, S_AB)[d])
            self.bank = 4 * d
            self.w_end = (k.epe, k.ep0)[d][:, d]
            self.w_mid = (k.ep0, k.epe)[d][:, d]
            self.late = slice(64, 128) if d == 0 else slice(0, 64)
            self.early = slice(0, 64) if d == 0 else slice(64, 128)

        def halves(self, x, level):
            return x.rearrange("p u (b h m) -> p u b h m", h=2, m=1 << level)

    D2 = [Dir(0), Dir(1)]

    @k.block()
    def _(block):
        @block.tensor
        def _(pe):
            pe.wait_ge(zero_ok, 4)
            for step in range(3):
                with pe.Fori(0, 4) as q:
                    for d, b in enumerate(D2):
                        pe.wait_ge(kb_ok[d], at(step, q, 2, 2))
                        pe.wait_ge(ar_ok[d], at(step, q, 2, 2))
                        pe.wait_ge(y_ok[d], at(step, q, 2, 0))
                        if step < 2:
                            pe.wait_ge((s_copied, s_ok)[step][d], q)
                        else:
                            pe.wait_ge(s_ok[d], 4)
                        for g in range(2):
                            for e in range(2):
                                rows = slice(64 * e, 64 * e + 64)
                                out = k.psum[:, b.bank + 2 * g + e, :].rearrange("p (c g t) -> p c g t", c=2, g=2)
                                for c in range(2):
                                    nc.tensor.matmul(out[:, c, :, b.late], b.kb[rows, g, c, :], b.ar[rows, c, :, b.late],
                                                     start=True, stop=True)
                                    last = nc.tensor.matmul(out[b.early, c, :, b.early], b.kb[rows, g, c, b.early],
                                                            b.ar[rows, c, :, b.early], start=True, stop=True)
                            last.then_inc(a_done[d], 1)
                    for l in range(NL):
                        for d, b in enumerate(D2):
                            if l == 0:
                                pe.wait_ge(a_ok[d], at(step, q, 4, 4))
                            else:
                                pe.wait_ge(x_ok[d], at(step, q, NL, l))
                            for u in range(4):
                                src = k.ident[:].unsqueeze(1) if l == 0 else b.x[:, u:u + 1, :]
                                last = nc.tensor.matmul(k.psum[:, b.bank, 64 * u:64 * u + 64], b.ab[:, u // 2, u % 2, 0, :],
                                                        b.halves(src, l)[:, 0, :, d, :], start=True, stop=True)
                            last.then_inc(t_done[d], 1)
                        if l:
                            for d, b in enumerate(D2):
                                pe.wait_ge(t_ok[d], at(step, q, NL, l + 1))
                                pe.wait_ge(xt_ok[d], at(step, q, NL, l))
                                for u in range(4):
                                    last = nc.tensor.matmul(k.psum[:, b.bank + 1, 64 * u:64 * u + 64], b.xt[:, u, :], b.t1[:, u, :],
                                                            start=True, stop=True)
                                last.then_inc(x_done[d], 1)
                        for d, b in enumerate(D2):
                            pe.wait_ge(x_ok[d], at(step, q, NL, l + 1))
                            for u in range(4):
                                last = nc.tensor.transpose(k.psum[:, b.bank + 2, P * u:P * u + P], b.x[:, u, :], k.ident[:])
                            last.then_inc(xt_done[d], 1)
                    for d, b in enumerate(D2):
                        pe.wait_ge(staged[d], at(step, q, 2, 2))
                        pe.wait_ge(xt_ok[d], at(step, q, NL, NL))
                        for u in range(4):
                            e, c = u // 2, u % 2
                            rows = slice(64 * e, 64 * e + 64)
                            out = k.psum[:, b.bank + e, 64 * c:64 * c + 64]
                            if step:
                                nc.tensor.matmul(out, b.ar[rows, c, 0, :], b.s0[rows, c, :], start=True, stop=False)
                            last = nc.tensor.matmul(out, b.ak[:, e, c, 0, :], b.v[:, c, e, :], start=step == 0, stop=True)
                        last.then_inc(r_done[d], 1)
                    if step < 2:
                        for d, b in enumerate(D2):
                            pe.wait_ge(khat_ok[d], at(step, q, 2, 2))
                            for g in range(2):
                                for c in range(2):
                                    last = nc.tensor.transpose(k.psum[:, b.bank + 3, P * (2 * g + c):P * (2 * g + c) + P],
                                                               b.kb[:, g, c, :], k.ident[:])
                            last.then_inc(kt_done[d], 1)
                    for d, b in enumerate(D2):
                        pe.wait_ge(r_ok[d], at(step, q, 1, 1))
                        for u in range(4):
                            last = nc.tensor.matmul(k.psum[:, b.bank + 2, 64 * u:64 * u + 64], b.xt[:, u, :], b.r[:, u, :],
                                                    start=True, stop=True)
                        last.then_inc(u_done[d], 1)
                    for d, b in enumerate(D2):
                        pe.wait_ge(u_ok[d], at(step, q, 1, 1))
                        if step < 2:
                            pe.wait_ge(kt_ok[d], at(step, q, 1, 1))
                            for u in range(4):
                                e, c = u // 2, u % 2
                                out = k.psum[64 * e:64 * e + 64, b.bank + 1, 64 * c:64 * c + 64]
                                kj, bj = (b.kt[:, g, c, 64 * e:64 * e + 64] for g in range(2))
                                if step == 0:
                                    nc.tensor.matmul(out, b.v[:, c, e, :], kj, start=True, stop=False)
                                    last = nc.tensor.matmul(out, b.u[:, u, :], bj, start=False, stop=True)
                                else:
                                    nc.tensor.matmul(out, kj, b.v[:, c, e, :], start=True, stop=False)
                                    last = nc.tensor.matmul(out, bj, b.u[:, u, :], start=False, stop=True)
                            last.then_inc(s_done[d], 1)
                    for d, b in enumerate(D2):
                        for u in range(4):
                            e, c = u // 2, u % 2
                            rows = slice(64 * e, 64 * e + 64)
                            out = k.psum[rows, b.bank + 3 * e, P * c:P * c + P]
                            nc.tensor.matmul(out, b.v[:, c, e, :], b.ak[:, e, c, 1, :], start=True, stop=False)
                            if step:
                                nc.tensor.matmul(out, b.s0[rows, c, :], b.ar[rows, c, 1, :], start=False, stop=False)
                            last = nc.tensor.matmul(out, b.u[:, u, :], b.ab[:, e, c, 1, :], start=False, stop=True)
                        last.then_inc(y_done[d], 1)

        @block.scalar
        def _(act):
            for step in range(3):
                with act.Fori(0, 4) as q:
                    for d, b in enumerate(D2):
                        n = TILE[step][d]
                        act.wait_ge(y_done[d], at(step, q, 1, 0))
                        inc, exc = (b.p[:, bass.ds(2 * q, 2), n, lo:lo + P] for lo in (1, 0))
                        ins = (exc, inc, inc) if d == 0 else (inc, exc, exc)
                        for dst, src, sign in zip((b.ar[:, :, 0, :], b.ar[:, :, 1, :], b.kb[:, 0, :, :]), ins, (-1, -1, 1)):
                            nc.scalar.activation(dst, src, ACT.Exp, scale=DECAY * (sign if d == 0 else -sign)).then_inc(exp_ok[d], 1)
                    for l in range(NL):
                        for d, b in enumerate(D2):
                            act.wait_ge(xt_done[d], at(step, q, NL, l + 1))
                            if l == 0:
                                nc.scalar.copy(b.xt, k.psum[:, b.bank + 2, :].rearrange("p (u t) -> p u t", u=4)).then_inc(xt_ok[d], 1)
                            else:
                                nc.scalar.copy(b.halves(b.xt, l)[:, :, :, 1 - d, :],
                                               b.halves(k.psum[:, b.bank + 2, :].rearrange("p (u t) -> p u t", u=4), l)[:, :, :, 1 - d, :]).then_inc(xt_ok[d], 1)
                    for d, b in enumerate(D2):
                        act.wait_ge(r_done[d], at(step, q, 1, 1))
                        nc.scalar.copy(b.r.rearrange("p (e c) n -> p e (c n)", e=2), k.psum[:, b.bank:b.bank + 2, 0:P]).then_inc(r_ok[d], 1)
                    if step < 2:
                        for d, b in enumerate(D2):
                            act.wait_ge(kt_done[d], at(step, q, 1, 1))
                            nc.scalar.copy(b.kt.rearrange("p g c f -> p (g c f)"), k.psum[:, b.bank + 3, :]).then_inc(kt_ok[d], 1)
                    for d, b in enumerate(D2):
                        act.wait_ge(u_done[d], at(step, q, 1, 1))
                        nc.scalar.copy(b.u.rearrange("p u n -> p (u n)"), k.psum[:, b.bank + 2, 0:256]).then_inc(u_ok[d], 1)
                    if step == 0:
                        for d, b in enumerate(D2):
                            act.wait_ge(s_done[d], at(step, q, 1, 1))
                            nc.scalar.copy(b.s.rearrange("p c n -> p (c n)"), k.psum[:, b.bank + 1, 0:P]).then_inc(s_copied[d], 1)

        @block.vector
        def _(dve):
            for b in D2:
                nc.vector.memset(b.ak[b.late, :, :, :, b.early], 0.0).then_inc(zero_ok, 1)
                nc.vector.memset(b.ab[b.late, :, :, :, b.early], 0.0).then_inc(zero_ok, 1)
            for step in range(3):
                with dve.Fori(0, 4) as q:
                    for d, b in enumerate(D2):
                        n = TILE[step][d]
                        toks = slice(P * n, P * n + P)
                        dve.wait_ge(y_done[d], at(step, q, 1, 0))
                        for c in range(2):
                            nc.vector.tensor_scalar(b.tmp[:, c, :], b.a[:, bass.ds(2 * q + c, 1), toks].squeeze(1),
                                                    k.vec[:, bass.ds(2 * q + (V_KA + c), 1)], k.omka[:, bass.ds(2 * q + c, 1)],
                                                    ALU.mult, ALU.add).then_inc(tmp_ok[d], 1)
                    for d, b in enumerate(D2):
                        n = TILE[step][d]
                        toks = slice(P * n, P * n + P)
                        dve.wait_ge(exp_ok[d], at(step, q, 3, 3))
                        nkk, r = (k.act3(i)[:, bass.ds(2 * q, 2), toks] for i in (S_NKK, S_R))
                        nc.vector.tensor_tensor(b.ar[:, :, 0, :], b.ar[:, :, 0, :], nkk, ALU.mult).then_inc(ar_ok[d], 1)
                        nc.vector.tensor_tensor(b.ar[:, :, 1, :], b.ar[:, :, 1, :], r, ALU.mult).then_inc(ar_ok[d], 1)
                        dve.wait_ge(rate_ok[d], at(step, q, 1, 1))
                        nc.vector.scalar_tensor_tensor(b.kb[:, 1, :, :], b.rate, -1.0, b.kb[:, 0, :, :], ALU.mult, ALU.mult).then_inc(kb_ok[d], 1)
                        dve.wait_ge(tmp_ok[d], at(step, q, 3, 2))
                        nc.vector.tensor_tensor(b.tmp, b.tmp, k.act3(S_K)[:, bass.ds(2 * q, 2), toks], ALU.mult).then_inc(tmp_ok[d], 1)
                        dve.wait_ge(tmp_ok[d], at(step, q, 3, 3))
                        dve.wait_ge(kb_ok[d], at(step, q, 2, 1))
                        nc.vector.tensor_tensor(b.kb[:, 0, :, :], b.kb[:, 0, :, :], b.tmp, ALU.mult).then_inc(kb_ok[d], 1)
                    for d, b in enumerate(D2):
                        for g, dst in enumerate((b.ak, b.ab)):
                            dve.wait_ge(a_done[d], at(step, q, 2, g + 1))
                            src = k.psum[:, b.bank + 2 * g:b.bank + 2 * g + 2, :].rearrange("p e (c g t) -> p (e c) g t", c=2, g=2)
                            dst = dst.rearrange("p e c g t -> p (e c) g t")
                            for part, cols in ((slice(0, P), b.late), (b.early, b.early)):
                                mask = k.causal[part, d, :, cols].unsqueeze(1).to_broadcast([part.stop - part.start, 4, 2, 64])
                                nc.vector.tensor_tensor(dst[part, :, :, cols], src[part, :, :, cols], mask, ALU.mult).then_inc(a_ok[d], 1)
                    for l in range(NL):
                        for d, b in enumerate(D2):
                            dve.wait_ge(t_done[d], at(step, q, NL, l + 1))
                            if l == 0 and step < 2:
                                dve.wait_ge(s_out[d], 32 * q if step == 0 else 128)
                            mask = k.level[:, d, l, :].unsqueeze(1).to_broadcast([P, 4, 64])
                            nc.vector.tensor_tensor(b.t1, k.psum[:, b.bank, 0:256].rearrange("p (u n) -> p u n", u=4), mask,
                                                    ALU.mult).then_inc(t_ok[d], 1)
                        for d, b in enumerate(D2):
                            early = b.halves(b.x, l)[:, :, :, d, :]
                            if l == 0:
                                dve.wait_ge(x_init[d], at(step, q, 1, 1))
                                dve.wait_ge(t_ok[d], at(step, q, NL, 1))
                                src = b.t1.rearrange("p u (b m) -> p u b m", m=1)
                            else:
                                dve.wait_ge(x_done[d], at(step, q, NL - 1, l))
                                dve.wait_ge(x_ok[d], at(step, q, NL, l))
                                src = k.psum[:, b.bank + 1, 0:256].rearrange("p (u b m) -> p u b m", u=4, m=1 << l)
                            nc.vector.tensor_tensor(early, early, src, ALU.add).then_inc(x_ok[d], 1)
                    if step == 1:
                        for d, b in enumerate(D2):
                            n, nxt = TILE[1][d], TILE[2][d]
                            w_end, w_mid = (w[:, bass.ds(2 * q, 2), i:i + 1].to_broadcast([P, 2, 64])
                                            for w, i in ((b.w_end, n), (b.w_mid, nxt)))
                            dve.wait_ge(s_done[d], at(1, q, 1, 1))
                            nc.vector.tensor_tensor(b.s, b.s0, w_end, ALU.mult).then_inc(s_step[d], 1)
                            dve.wait_ge(s_step[d], 2 * q + 1)
                            nc.vector.tensor_tensor(b.s, b.s, k.psum[:, b.bank + 1, 0:P].rearrange("p (c n) -> p c n", c=2),
                                                    ALU.add).then_inc(s_step[d], 1)
                            dve.wait_ge(s_step[d], 2 * q + 2)
                            nc.vector.tensor_tensor(k.s0t[:, d, bass.ds(2 * q, 2), :], b.s, w_mid, ALU.mult).then_inc(s_ok[d], 1)
                    for d, b in enumerate(D2):
                        n = TILE[step][d]
                        dve.wait_ge(y_done[d], at(step, q, 1, 1))
                        if step == 0 and d == 1:
                            dve.wait_ge(y_ok[0], at(step, q, 2, 2))
                        for e in range(2):
                            rows = slice(64 * e, 64 * e + 64)
                            y = k.act3(S_Y)[rows, bass.ds(2 * q, 2), P * n:P * n + P]
                            src = k.psum[rows, b.bank + 3 * e, 0:256].rearrange("p (c t) -> p c t", c=2)
                            if step == 1 or (step, d) == (0, 0):
                                nc.vector.tensor_copy(y, src).then_inc(y_ok[d], 1)
                            else:
                                nc.vector.tensor_tensor(y, y, src, ALU.add).then_inc(y_ok[d], 1)

        @block.gpsimd
        def _(pool):
            for step in range(3):
                with pool.Fori(0, 4) as q:
                    for d, b in enumerate(D2):
                        n = TILE[step][d]
                        toks = slice(P * n, P * n + P)
                        pool.wait_ge(y_done[d], at(step, q, 1, 0))
                        nkk = k.act3(S_NKK)[:, bass.ds(2 * q, 2), toks]
                        nc.gpsimd.tensor_tensor(b.rate, nkk, b.a[:, bass.ds(2 * q, 2), toks], ALU.mult).then_inc(rate_ok[d], 1)
                        nc.gpsimd.tensor_copy(b.x, k.ident[:].unsqueeze(1).to_broadcast([P, 4, P])).then_inc(x_init[d], 1)
                    for d, b in enumerate(D2):
                        n = TILE[step][d]
                        nc.gpsimd.tensor_copy(b.v.rearrange("p c e n -> p (c e n)"),
                                              k.tok3(S_V)[:, n, bass.ds(256 * q, 256)]).then_inc(staged[d], 1)
                        if step:
                            pool.wait_ge(s_ok[d], q if step == 1 else 4)
                        nc.gpsimd.tensor_copy(b.s0, k.s0t[:, d, bass.ds(2 * q, 2), :]).then_inc(staged[d], 1)
                    if step < 2:
                        for d, b in enumerate(D2):
                            n = TILE[step][d]
                            pool.wait_ge(a_done[d], at(step, q, 2, 2))
                            w_end = b.w_end[:, bass.ds(2 * q, 2), n:n + 1].to_broadcast([P, 2, P])
                            for g in range(2):
                                nc.gpsimd.tensor_tensor(b.kb[:, g, :, :], b.kb[:, g, :, :], w_end, ALU.mult).then_inc(khat_ok[d], 1)

        @block.sync
        def _(sp):
            new = k.a["new_state"][0, 0]
            with sp.Fori(0, 4) as q:
                for d, b in enumerate(D2):
                    sp.wait_ge(s_copied[d], q + 1)
                    dst = new[d][bass.ds(4 * q, 4)]
                    for e in range(2):
                        sp.dma_start(dst.rearrange("(c e) i j -> e i c j", e=2)[e], b.s[64 * e:64 * e + 64]).then_inc(s_out[d], 16)


def residual(k, dve, x, c, acc, gate_at, sem):
    for s, (t0, t1) in enumerate(((0, CTX), (CTX, T))):
        k.nc.vector.scalar_tensor_tensor(x[:, c, t0:t1], acc[:, t0:t1], k.mod[:, gate_at + c, s:s + 1], x[:, c, t0:t1],
                                         ALU.mult, ALU.add).then_inc(sem, 1)


def phase_rwkv_out(k):
    nc = k.nc
    first = k.taken
    k.taken += 9
    names = ("block_in", "cast_in", "x_in2", "rates_sum", "bonus_a", "bonus_b", "bonus_t", "mean_done", "less_mean", "y_squared",
             "var_done", "var_eps", "var_root", "rstd_ok", "bonus_done", "bonus_read", "vt_done", "bonus_ok", "rs_done", "y_scaled",
             "y_affine", "y_bonus", "g_done", "y_gated", "x_turned", "x_read", "o_done", "o_read", "omka2_ok")
    (block_in, cast_in, x_in, rates_sum, bonus_a, bonus_b, bonus_t, mean_done, less_mean, y_squared, var_done, var_eps, var_root,
     rstd_ok, bonus_done, bonus_read, vt_done, bonus_ok, rs_done, y_scaled, y_affine, y_bonus, g_done, y_gated, x_turned, x_read,
     o_done, o_read, omka2_ok) = (k.sem("post_" + n) for n in names)
    ones = k.ws[:, 0:P]
    cast = k.ws[0:H, 1160:1160 + D].rearrange("h (c p) -> h c p", c=DC)
    var, root, rstd = (k.ws[0:H, 2200 + T * i:2200 + T * i + T] for i in range(3))
    omka2 = k.ws[:, 130:138]
    y, sq, tb = k.act3(S_Y), k.act3(S_PF), k.act3(S_PB)
    af, ab, r3, k3, v3, xt, x = (k.act3(S_AF), k.act3(S_AB), k.act3(S_R), k.act3(S_K), k.tok3(S_V), k.tok3(S_NKK), k.act3(S_AB))

    @k.block()
    def _(block):
        @block.tensor
        def _(pe):
            pe.wait_ge(block_in, 16)
            for c in range(DC):
                if c >= 2:
                    pe.wait_ge(less_mean, c - 1)
                nc.tensor.matmul(k.psum[:, c % 2, 0:T], ones, y[:, c, :], start=True, stop=True).then_inc(mean_done, 1)
            for c in range(DC):
                pe.wait_ge(bonus_t, c + 1)
                if c >= 2:
                    pe.wait_ge(bonus_read, c - 1)
                nc.tensor.matmul(k.psum[:, 3 + c % 2, 0:T], ones, tb[:, c, :], start=True, stop=True).then_inc(bonus_done, 1)
            for c in range(DC):
                if c >= 2:
                    pe.wait_ge(bonus_ok, c - 1)
                for n in range(NT):
                    last = nc.tensor.transpose(k.psum[:, 5 + c % 2, P * n:P * n + P], v3[:, n, P * c:P * c + P], k.ident[:])
                last.then_inc(vt_done, 1)
            for c in range(DC):
                pe.wait_ge(y_squared, c + 1)
                last = nc.tensor.matmul(k.psum[0:H, 2, 0:T], k.headsum[:, c, :], sq[:, c, :], start=c == 0, stop=c == DC - 1)
            last.then_inc(var_done, 1)
            pe.wait_ge(x_in, 32)
            for c in range(DC):
                if c >= 2:
                    pe.wait_ge(x_read, c - 1)
                else:
                    pe.wait_ge(bonus_read, 8)
                for n in range(NT):
                    last = nc.tensor.transpose(k.psum[:, 3 + c % 2, P * n:P * n + P], xt[:, n, P * c:P * c + P], k.ident[:])
                last.then_inc(x_turned, 1)
            pe.wait_ge(rstd_ok, 1)
            pe.wait_ge(cast_in, 16)
            g2 = take_piece(k, pe, first)
            for c in range(DC):
                if c >= 2:
                    pe.wait_ge(y_scaled, c - 1)
                else:
                    pe.wait_ge(less_mean, 8)
                nc.tensor.matmul(k.psum[:, c % 2, 0:T], cast[:, c, :], rstd, start=True, stop=True).then_inc(rs_done, 1)
                if c >= 2:
                    pe.wait_ge(y_gated, c - 1)
                nc.tensor.matmul(k.psum[:, (7, 2)[c % 2], 0:T], g2[:, P * c:P * c + P], k.sgate[:], start=True, stop=True).then_inc(g_done, 1)
            k.used[first] = (g_done, 8)
            for o in range(DC):
                if o % 2 == 0:
                    w = piece_cols(take_piece(k, pe, first + 1 + o // 2))
                if o < 2:
                    pe.wait_ge(bonus_ok, 8)
                else:
                    pe.wait_ge(o_read, 2 * (o - 1))
                for c in range(DC):
                    pe.wait_ge(y_gated, c + 1)
                    last = nc.tensor.matmul(k.psum[:, 5 + o % 2, 0:T], w[:, c, P * (o % 2):P * (o % 2) + P], y[:, c, :],
                                            start=c == 0, stop=c == DC - 1)
                last.then_inc(o_done, 1)
                k.used[first + 1 + o // 2] = (o_done, o + 1)

        @block.sync
        def _(sp):
            load_tokens(k, sp, xt, x_in)
            sp.dma_start(ones, k.a["c_block"]).then_inc(block_in, 16)
            sp.dma_start(k.ws[0:H, 1160:1160 + D], k.a["c_headcast"]).then_inc(cast_in, 16)
            prefetch(k, sp, first, first + 9)

        @block.gpsimd
        def _(pool):
            for g in range(4):
                nc.gpsimd.tensor_tensor(tb[:, 2 * g:2 * g + 2, :], af[:, 2 * g:2 * g + 2, :], ab[:, 2 * g:2 * g + 2, :], ALU.add).then_inc(rates_sum, 1)

        @block.scalar
        def _(act):
            for c in range(DC):
                act.wait_ge(less_mean, c + 1)
                nc.scalar.activation(sq[:, c, :], y[:, c, :], ACT.Square).then_inc(y_squared, 1)
                act.wait_ge(bonus_done, c + 1)
                act.wait_ge(rates_sum, 4)
                nc.scalar.copy(af[:, c, :], k.psum[:, 3 + c % 2, 0:T]).then_inc(bonus_read, 1)
            act.wait_ge(var_eps, 1)
            nc.scalar.activation(root, var, ACT.Sqrt).then_inc(var_root, 1)
            for c in range(DC):
                act.wait_ge(x_turned, c + 1)
                nc.scalar.copy(x[:, c, :], k.psum[:, 3 + c % 2, 0:T]).then_inc(x_read, 1)
            for c in range(DC):
                act.wait_ge(y_scaled, c + 1)
                nc.scalar.activation(y[:, c, :], y[:, c, :], ACT.Identity, bias=k.vec[:, V_LB + c:V_LB + c + 1],
                                     scale=k.vec[:, V_LG + c:V_LG + c + 1]).then_inc(y_affine, 1)

        @block.vector
        def _(dve):
            nc.vector.tensor_scalar(omka2, k.omka[:], 2.0, None, ALU.mult).then_inc(omka2_ok, 1)
            dve.wait_ge(omka2_ok, 1)
            for c in range(DC):
                dve.wait_ge(mean_done, c + 1)
                nc.vector.scalar_tensor_tensor(y[:, c, :], k.psum[:, c % 2, 0:T], -1.0 / HD, y[:, c, :], ALU.mult, ALU.add).then_inc(less_mean, 1)
                dve.wait_ge(rates_sum, c // 2 + 1)
                nc.vector.tensor_scalar(tb[:, c, :], tb[:, c, :], k.vec[:, V_KA + c:V_KA + c + 1], omka2[:, c:c + 1],
                                        ALU.mult, ALU.add).then_inc(bonus_a, 1)
                dve.wait_ge(bonus_a, c + 1)
                nc.vector.tensor_tensor(tb[:, c, :], tb[:, c, :], k3[:, c, :], ALU.mult).then_inc(bonus_b, 1)
                dve.wait_ge(bonus_b, c + 1)
                nc.vector.scalar_tensor_tensor(tb[:, c, :], r3[:, c, :], k.vec[:, V_RK + c:V_RK + c + 1], tb[:, c, :],
                                               ALU.mult, ALU.mult).then_inc(bonus_t, 1)
            for c in range(DC):
                dve.wait_ge(vt_done, c + 1)
                dve.wait_ge(bonus_read, c + 1)
                nc.vector.tensor_tensor(af[:, c, :], af[:, c, :], k.psum[:, 5 + c % 2, 0:T], ALU.mult).then_inc(bonus_ok, 1)
            dve.wait_ge(var_done, 1)
            nc.vector.tensor_scalar(var, k.psum[0:H, 2, 0:T], 1.0 / HD, GN_EPS, ALU.mult, ALU.add).then_inc(var_eps, 1)
            dve.wait_ge(var_root, 1)
            nc.vector.reciprocal(rstd, root).then_inc(rstd_ok, 1)
            for c in range(DC + 1):
                if c < DC:
                    dve.wait_ge(rs_done, c + 1)
                    nc.vector.tensor_tensor(y[:, c, :], y[:, c, :], k.psum[:, c % 2, 0:T], ALU.mult).then_inc(y_scaled, 1)
                if c:
                    b = c - 1
                    dve.wait_ge(y_affine, b + 1)
                    nc.vector.tensor_tensor(y[:, b, :], y[:, b, :], af[:, b, :], ALU.add).then_inc(y_bonus, 1)
                    dve.wait_ge(g_done, b + 1)
                    dve.wait_ge(y_bonus, b + 1)
                    nc.vector.tensor_tensor(y[:, b, :], y[:, b, :], k.psum[:, (7, 2)[b % 2], 0:T], ALU.mult).then_inc(y_gated, 1)
            dve.wait_ge(x_read, 8)
            for o in range(DC):
                dve.wait_ge(o_done, o + 1)
                residual(k, dve, x, o, k.psum[:, 5 + o % 2, 0:T], 16, o_read)


def phase_router(k, layer, h_slab):
    nc, a = k.nc, k.a
    w_in, b_in, logit_done, step, exps = (k.sem(f"router{layer}_{n}") for n in ("w_in", "b_in", "logit_done", "step", "exps"))
    h = k.act3(h_slab)
    w = k.ws[:, 0:DC * 20].rearrange("p (c n) -> p c n", c=DC)
    bias, order = k.ws[:, 160:180], k.ws[:, 180:192].rearrange("p (n j) -> p n j", n=NT)
    at = [192]

    def buf(*shape):
        n = int(np.prod(shape))
        v = k.ws[:, at[0]:at[0] + n]
        at[0] += n
        names = "abc"[:len(shape)]
        return v if len(shape) == 1 else v.rearrange(f"p ({' '.join(names)}) -> p {' '.join(names)}",
                                                     **dict(zip(names, shape)))

    lg, gmax, rel, gexp, gsum, one_g, top = buf(NT, 20), buf(NT), buf(NT, 4), buf(NT, 4), buf(NT), buf(NT, 4), buf(NT)
    sel, le, m1, d1, one1, d2, m2, one2, e2, w1, w2, wj = (buf(NT, 4, 4), buf(NT, 4), buf(NT), buf(NT, 4), buf(NT, 4), buf(NT, 4),
                                                           buf(NT), buf(NT, 4), buf(NT), buf(NT), buf(NT), buf(NT, 4))
    den, t4 = buf(NT), buf(NT, 4)
    gate = k.ws[:, 700:700 + NT * NE].rearrange("p (n g j) -> p n g j", n=NT, g=NG)

    def wide(v, n=4):
        return v.unsqueeze(2).to_broadcast([P, NT, n])

    @k.block()
    def _(block):
        @block.sync
        def _(sp):
            for n, lo, hi in (("grp", 0, 4), ("exp", 4, 20)):
                sp.dma_start(w[:, :, lo:hi], a["moe_w_" + n][layer].rearrange("(c p) n -> p c n", p=P)).then_inc(w_in, 16)
                sp.dma_start(bias[:, lo:hi], a["moe_b_" + n][layer].partition_broadcast(P)).then_inc(b_in, 16)
            sp.dma_start(k.ws[:, 180:192], a["c_order"]).then_inc(b_in, 16)

        @block.tensor
        def _(pe):
            pe.wait_ge(w_in, 32)
            for n in range(NT):
                for c in range(DC):
                    last = nc.tensor.matmul(k.psum[:, n, 0:20], h[:, c, P * n:P * n + P], w[:, c, :], start=c == 0, stop=c == DC - 1)
            last.then_inc(logit_done, 1)

        @block.scalar
        def _(act):
            act.wait_ge(step, 3)
            nc.scalar.activation(gexp, rel, ACT.Exp).then_inc(exps, 1)
            act.wait_ge(step, SECOND)
            nc.scalar.activation(e2, m2, ACT.Exp).then_inc(exps, 1)

        @block.vector
        def _(dve):
            n = [0]

            def then(ins):
                n[0] += 1
                ins.then_inc(step, 1)
                dve.wait_ge(step, n[0])

            def first_of(dst, flags):
                then(nc.vector.tensor_tensor(t4, flags, order, ALU.mult))
                then(nc.vector.tensor_reduce(top, t4, AX.X, ALU.max))
                then(nc.vector.tensor_tensor(dst, t4, wide(top), ALU.is_equal))

            dve.wait_ge(logit_done, 1)
            dve.wait_ge(b_in, 48)
            then(nc.vector.tensor_tensor(lg, k.psum[:, 0:NT, 0:20], bias.unsqueeze(1).to_broadcast([P, NT, 20]), ALU.add))
            then(nc.vector.tensor_reduce(gmax, lg[:, :, 0:4], AX.X, ALU.max))
            then(nc.vector.tensor_tensor(rel, lg[:, :, 0:4], wide(gmax), ALU.subtract))
            then(nc.vector.tensor_scalar(d1, rel, 0.0, None, ALU.is_ge))
            first_of(one_g, d1)
            then(nc.vector.tensor_tensor(sel, lg[:, :, 4:20].rearrange("p n (g j) -> p n g j", g=4),
                                         one_g.unsqueeze(3).to_broadcast([P, NT, 4, 4]), ALU.mult))
            then(nc.vector.tensor_reduce(le, sel.rearrange("p n g j -> p n j g"), AX.X, ALU.add))
            then(nc.vector.tensor_reduce(m1, le, AX.X, ALU.max))
            then(nc.vector.tensor_tensor(d1, le, wide(m1), ALU.subtract))
            then(nc.vector.tensor_scalar(d2, d1, 0.0, None, ALU.is_ge))
            first_of(one1, d2)
            then(nc.vector.scalar_tensor_tensor(d2, one1, -BIG, d1, ALU.mult, ALU.add))
            then(nc.vector.tensor_reduce(m2, d2, AX.X, ALU.max))
            assert n[0] == SECOND
            then(nc.vector.tensor_tensor(d1, d2, wide(m2), ALU.is_ge))
            first_of(one2, d1)
            dve.wait_ge(exps, 2)
            then(nc.vector.tensor_reduce(gsum, gexp, AX.X, ALU.add))
            then(nc.vector.scalar_tensor_tensor(den, e2, 1.0, gsum, ALU.add, ALU.mult))
            then(nc.vector.reciprocal(w1, den))
            then(nc.vector.tensor_tensor(w2, w1, e2, ALU.mult))
            then(nc.vector.tensor_tensor(wj, one1, wide(w1), ALU.mult))
            then(nc.vector.tensor_tensor(t4, one2, wide(w2), ALU.mult))
            then(nc.vector.tensor_tensor(wj, wj, t4, ALU.add))
            then(nc.vector.tensor_tensor(gate, one_g.unsqueeze(3).to_broadcast([P, NT, 4, 4]),
                                         wj.unsqueeze(2).to_broadcast([P, NT, 4, 4]), ALU.mult))


SECOND = 17


def phase_moe(k, layer, h_slab, y_slab):
    nc = k.nc
    first = k.taken
    k.taken += 48
    h_done, silu_ok, hid_ok, y_done, y_added = (
        k.sem(f"moe{layer}_{n}") for n in ("h_done", "silu_ok", "hid_ok", "y_done", "y_added"))
    h, y = k.act3(h_slab), k.tok3(y_slab)
    gate = k.ws[:, 700:700 + NT * NE].rearrange("p (n e) -> p n e", n=NT)
    silu = [k.ws[:, 1024 + T * f:1024 + T * f + T] for f in range(2)]
    hid = [[k.ws[:, 2048 + T * (2 * b + f):2048 + T * (2 * b + f) + T] for f in range(2)] for b in range(2)]

    def w1_at(e):
        return 3 * e - 1 if e else 0

    def w3_at(e):
        return 3 * e if e else 1

    def w2_at(e):
        return 3 * e + 4 if e < NE - 1 else 47

    @k.block()
    def _(block):
        @block.tensor
        def _(pe):
            def arrived(i, place):
                pe.wait_ge(k.ring_in[place % NS], i * 16 + k.arrival[first + place])
                return k.ring[:, place % NS, :]

            def inner(i, e):
                w1, w3 = piece_cols(arrived(i, w1_at(e))), piece_cols(arrived(i, w3_at(e)))
                for f in range(2):
                    if e:
                        pe.wait_ge(hid_ok, 4 * i + (2 * e - 1 + f))
                    for w, bank in ((w1, f), (w3, 2 + f)):
                        for c in range(DC):
                            last = nc.tensor.matmul(k.psum[:, bank, 0:T], w[:, c, P * f:P * f + P], h[:, c, :],
                                                    start=c == 0, stop=c == DC - 1)
                        last.then_inc(h_done, 1)

            def outer(i, e):
                w2 = arrived(i, w2_at(e)).rearrange("p (f n) -> p f n", f=2)
                pe.wait_ge(hid_ok, 4 * i + (2 * e + 2))
                for j in range(2 * NT):
                    n, half = j // 2, j % 2
                    pe.wait_ge(y_added, 12 * i + (6 * e + j + 1))
                    for f in range(2):
                        last = nc.tensor.matmul(k.psum[:, 4 + (2 * e + j) % 4, :], hid[e % 2][f][:, P * n:P * n + P],
                                                w2[:, f, 512 * half:512 * half + 512], start=f == 0, stop=f == 1)
                    last.then_inc(y_done, 1)

            inner(0, 0)
            with pe.Fori(0, NE // 2 - 1) as i:
                inner(i, 1)
                outer(i, 0)
                inner(i, 2)
                outer(i, 1)
            inner(0, NE - 1)
            outer(0, NE - 2)
            outer(0, NE - 1)
            for e in range(NE):
                k.used[first + w1_at(e)] = k.used[first + w3_at(e)] = (h_done, 4 * e + 4)
                k.used[first + w2_at(e)] = (y_done, 6 * e + 6)

        @block.sync
        def _(sp):
            body = [(6, "moe_w3", 2, [(h_done, 8, 4)]), (7, "moe_w2", 1, [(h_done, 8, 4), (y_done, 12, 0)]),
                    (8, "moe_w1", 3, [(h_done, 8, 8)]), (9, "moe_w3", 3, [(h_done, 8, 8)]),
                    (10, "moe_w2", 2, [(y_done, 12, 6)]), (11, "moe_w1", 4, [(h_done, 8, 12)])]
            with sp.Fori(0, 6) as i:
                for place, name, e, waits in body:
                    sp.wait_ge(h_done, 4)
                    for sem, per, value in waits:
                        sp.wait_ge(sem, i * per + value)
                    src = k.a[name][layer][bass.ds(2 * i + e, 1)].rearrange("e r n -> (e r) n").rearrange("(c p) n -> p c n", p=P)
                    dst = k.ring[:, place % NS, :].rearrange("p (c n) -> p c n", c=2 if name == "moe_w2" else DC)
                    sp.dma_start(dst, src).then_inc(k.ring_in[place % NS], 16)
            prefetch(k, sp, first + 36, first + 48)

        @block.scalar
        def _(act):
            def silus(i, e):
                for f in range(2):
                    act.wait_ge(h_done, 8 * i + (4 * e + 2 * f + 1))
                    if e:
                        act.wait_ge(hid_ok, 4 * i + (2 * e - 1 + f))
                    nc.scalar.activation(silu[f], k.psum[:, f, 0:T], ACT.Silu).then_inc(silu_ok, 1)

            silus(0, 0)
            with act.Fori(0, NE // 2 - 1) as i:
                silus(i, 1)
                silus(i, 2)
            silus(0, NE - 1)

        @block.vector
        def _(dve):
            def hidden(i, e):
                if e >= 2:
                    dve.wait_ge(y_done, 12 * i + 6 * (e - 1))
                for f in range(2):
                    dve.wait_ge(silu_ok, 4 * i + (2 * e + f + 1))
                    dve.wait_ge(h_done, 8 * i + (4 * e + 2 * f + 2))
                    nc.vector.tensor_tensor(hid[e % 2][f], silu[f], k.psum[:, 2 + f, 0:T], ALU.mult).then_inc(hid_ok, 1)

            def add(i, e):
                for j in range(2 * NT):
                    n, half = j // 2, j % 2
                    dve.wait_ge(y_done, 12 * i + (6 * e + j + 1))
                    acc = y[:, n, 512 * half:512 * half + 512]
                    nc.vector.scalar_tensor_tensor(acc, k.psum[:, 4 + (2 * e + j) % 4, :], gate[:, n, bass.ds(2 * i + e, 1)],
                                                   acc, ALU.mult, ALU.add).then_inc(y_added, 1)

            nc.vector.memset(k.slab[:, y_slab, 0:NT * D], 0.0).then_inc(y_added, 4)
            dve.wait_ge(y_added, 4)
            hidden(0, 0)
            with dve.Fori(0, NE // 2 - 1) as i:
                hidden(i, 1)
                add(i, 0)
                hidden(i, 2)
                add(i, 1)
            hidden(0, NE - 1)
            add(0, NE - 2)
            add(0, NE - 1)


def phase_moe_out(k, layer, y_slab, x_slab):
    nc = k.nc
    y_turned, x_added = k.sem(f"moe{layer}_y_turned"), k.sem(f"moe{layer}_x_added")
    y, x = k.tok3(y_slab), k.act3(x_slab)

    @k.block()
    def _(block):
        @block.tensor
        def _(pe):
            for c in range(DC):
                for n in range(NT):
                    last = nc.tensor.transpose(k.psum[:, c, P * n:P * n + P], y[:, n, P * c:P * c + P], k.ident[:])
                last.then_inc(y_turned, 1)

        @block.vector
        def _(dve):
            for c in range(DC):
                dve.wait_ge(y_turned, c + 1)
                residual(k, dve, x, c, k.psum[:, c, 0:T], 40, x_added)


def phase_qkv(k):
    nc, a = k.nc, k.a
    first = k.taken
    k.taken += 12
    proj, read_out, kt_done, kt_ok, stored = (k.sem("qkv_" + n) for n in ("done", "read", "kt_done", "kt_ok", "stored"))
    padded, rpb_in, pad_out, cap_in, bias_in, capped = (
        k.sem("bias_" + n) for n in ("padded", "rpb_in", "pad_out", "cap_in", "in", "capped"))
    q_lat = k.sem("q_lat_ok")
    ctx_in, kc_done, kc_ok = (k.sem("ctx_" + n) for n in ("in", "kc_done", "kc_ok"))
    h, q3, k3, v3 = k.act3(S_Y), k.act3(S_PF), k.act3(S_PB), k.tok3(S_V)
    new_k = k.ws[:, 0:D]
    pad = k.ws[0:H, 1024:1024 + 15 * P].rearrange("h (r n) -> h r n", r=15)
    cap = k.ws[:, 3000:3064]
    MID = GRID - WIN_C
    slabs = k.slab[:, S_R:S_K + 1, :].rearrange("p s n -> p (s n)")
    bias = slabs[:, 0:H * 6 * GRID].rearrange("p (h e n) -> p h e n", h=H, e=6)
    k_tok, v_tok = k.slab[:, S_NKK, 0:D], k.slab[:, S_NKK, D:2 * D]
    kc = k.slab[:, S_NKK, 2 * D:3 * D].rearrange("p (c t) -> p c t", c=DC)

    def bank(o):
        return k.psum[:, o % 6, :]

    @k.block()
    def _(block):
        @block.tensor
        def _(pe):
            o = 0
            for j in range(12):
                w = piece_cols(take_piece(k, pe, first + j))
                for m in range(2 if j < 8 else NT):
                    if o >= 6:
                        pe.wait_ge(read_out, o - 5)
                    for c in range(DC):
                        if j < 8:
                            last = nc.tensor.matmul(bank(o)[:, 0:T], w[:, c, P * m:P * m + P], h[:, c, :], start=c == 0, stop=c == DC - 1)
                        else:
                            last = nc.tensor.matmul(bank(o)[:, 0:256], h[:, c, P * m:P * m + P], w[:, c, :], start=c == 0, stop=c == DC - 1)
                    last.then_inc(proj, 1)
                    o += 1
                k.used[first + j] = (proj, o)
                if j == 8:
                    pe.wait_ge(read_out, 16)
                    for c in range(DC):
                        last = nc.tensor.transpose(k.psum[:, 6 + c // 4, P * (c % 4):P * (c % 4) + P], k3[:, c, 0:CTX], k.ident[:])
                    last.then_inc(kt_done, 1)
            pe.wait_ge(kt_ok, 1)
            pe.wait_ge(ctx_in, 32)
            for c in range(DC):
                last = nc.tensor.transpose(k.psum[:, 6 + c // 4, P * (c % 4):P * (c % 4) + P], k_tok[:, P * c:P * c + P], k.ident[:])
            last.then_inc(kc_done, 1)

        @block.sync
        def _(sp):
            sp.dma_start(k_tok, a["cache_na_k"][0, 0].rearrange("t h d -> t (h d)")).then_inc(ctx_in, 16)
            sp.dma_start(v_tok, a["cache_na_v"][0, 0].rearrange("t h d -> t (h d)")).then_inc(ctx_in, 16)
            prefetch(k, sp, first, first + 12)
            sp.wait_ge(kt_ok, 1)
            sp.dma_start(a["new_k"][0, 0].rearrange("t h d -> t (h d)"), new_k).then_inc(stored, 16)
            sp.wait_ge(read_out, 28)
            sp.dma_start(a["new_v"][0, 0].rearrange("t h d -> t (h d)"), v3[:, 0, :]).then_inc(stored, 16)
            sp.wait_ge(stored, 32)

        @block.scalar
        def _(act):
            act.wait_ge(padded, 1)
            act.dma_start(pad[:, :, MID:MID + 31], a["na_rpb"][0]).then_inc(rpb_in, 16)
            act.wait_ge(rpb_in, 16)
            act.dma_start(a["scratch"], pad).then_inc(pad_out, 16)
            act.dma_start(cap, a["c_cap"]).then_inc(cap_in, 16)
            act.wait_ge(pad_out, 16)
            for half in range(2):
                for e in range(6):
                    row = e + 5 - half
                    src = bass.AP(tensor=a["scratch"].tensor, offset=row * P, ap=[[1, GRID], [15 * P, H], [1, GRID]])
                    act.dma_start(bias[64 * half:64 * half + 64, :, e, :], src).then_inc(bias_in, 16)
            for o in range(28):
                act.wait_ge(proj, o + 1)
                if o < 8:
                    nc.scalar.mul(q3[:, o, CTX:T].rearrange("p (r n) -> p r n", n=GRID),
                                  bank(o)[:, CTX:T].rearrange("p (r n) -> p r n", n=GRID)[:, :, ::-1], HD ** -0.5).then_inc(q_lat, 1)
                    nc.scalar.mul(q3[:, o, 0:CTX], bank(o)[:, 0:CTX], HD ** -0.5).then_inc(read_out, 1)
                elif o < 16:
                    nc.scalar.copy(k3[:, o - 8, :], bank(o)[:, 0:T]).then_inc(read_out, 1)
                else:
                    j, n = divmod(o - 16, NT)
                    nc.scalar.copy(v3[:, n, 256 * j:256 * j + 256], bank(o)[:, 0:256]).then_inc(read_out, 1)

        @block.vector
        def _(dve):
            nc.vector.memset(k.ws[0:H, 1024:1024 + 15 * P], 0.0).then_inc(padded, 1)
            dve.wait_ge(kt_done, 1)
            nc.vector.tensor_copy(new_k.rearrange("p (b n) -> p b n", b=2), k.psum[:, 6:8, :]).then_inc(kt_ok, 1)
            dve.wait_ge(bias_in, 192)
            dve.wait_ge(cap_in, 16)
            for g in range(4):
                part = bias[:, 4 * g:4 * g + 4].rearrange("p h e n -> p (h e) n")
                nc.vector.tensor_tensor(part, part, cap.unsqueeze(1).to_broadcast([P, 24, GRID]), ALU.min).then_inc(capped, 1)
            dve.wait_ge(kc_done, 1)
            nc.vector.tensor_copy(kc.rearrange("p c t -> p (c t)").rearrange("p (b n) -> p b n", b=2), k.psum[:, 6:8, :]).then_inc(kc_ok, 1)


def phase_attention(k):
    nc = k.nc
    staged, s_done, s_ok, m_ok, e_ok, pt_done, pt_ok, o_done, r_ok, o_ok = (
        k.sem("att_" + n) for n in ("staged", "s_done", "s_ok", "m_ok", "e_ok", "pt_done", "pt_ok", "o_done", "r_ok", "o_ok"))
    q3, k3, v3, o3 = k.act3(S_PF), k.act3(S_PB), k.tok3(S_V), k.tok3(S_AF)
    slabs = k.slab[:, S_R:S_K + 1, :].rearrange("p s n -> p (s n)")
    bias = slabs[:, 0:H * 6 * GRID].rearrange("p (h n) -> p h n", h=H)
    v_ctx = k.slab[:, S_NKK, D:2 * D]
    kc = k.slab[:, S_NKK, 2 * D:3 * D].rearrange("p (c t) -> p c t", c=DC)
    qs, ks, kcs = k.ws[:, 0:T], k.ws[:, T:2 * T], k.ws[:, 2 * T:2 * T + P]
    LK = LAT + CTX
    UNITS = [(e, n) for n in (1, 2, 0) for e in range(2)]
    probs = [k.ws[:, 1024 + LK * i:1024 + LK * i + (LK if n else CTX)] for i, (e, n) in enumerate(UNITS)]
    turned = [k.ws[:, 4096 + LK * i:4096 + LK * i + (LK if n else CTX)] for i, (e, n) in enumerate(UNITS)]
    neg_max, total, inverse = (k.ws[:, 8000 + 8 * i:8006 + 8 * i] for i in range(3))

    def score_bank(i):
        return k.psum[:, i, :]

    @k.block()
    def _(block):
        def values(pe, c, i):
            e, n = UNITS[i]
            pe.wait_ge(pt_ok, 6 * c + (i + 1))
            out = k.psum[:, i, 448:512]
            col = 64 * e
            if n:
                src = [v3[:, 1, bass.ds(P * c + col, 64)], v3[:, 2, bass.ds(P * c + col, 64)], v_ctx[:, bass.ds(P * c + col, 64)]]
            else:
                src = [v3[:, 0, bass.ds(P * c + col, 64)]]
            for j, v in enumerate(src):
                last = nc.tensor.matmul(out, turned[i][:, P * j:P * j + P], v, start=j == 0, stop=j == len(src) - 1)
            last.then_inc(o_done, 1)

        def turn(act, c, i):
            act.wait_ge(pt_done, 6 * c + (i + 1))
            nc.scalar.copy(turned[i], k.psum[:, 6 + i % 2, 0:LK if UNITS[i][1] else CTX]).then_inc(pt_ok, 1)

        @block.tensor
        def _(pe):
            with pe.Fori(0, H // 2) as c:
                pe.wait_ge(staged, 3 * c + 3)
                for i, (e, n) in enumerate(UNITS):
                    rows = slice(64 * e, 64 * e + 64)
                    pe.wait_ge(o_ok, 6 * c)
                    q = qs[rows, P * n:P * n + P]
                    if n:
                        nc.tensor.matmul(score_bank(i)[:, 0:LAT], q, ks[rows, CTX:T], start=True, stop=True)
                        nc.tensor.matmul(score_bank(i)[:, LAT:LK], q, kcs[rows, :], start=True, stop=True).then_inc(s_done, 1)
                    else:
                        nc.tensor.matmul(score_bank(i)[:, 0:CTX], q, ks[rows, 0:CTX], start=True, stop=True).then_inc(s_done, 1)
                for i, (e, n) in enumerate(UNITS):
                    tiles = 3 if n else 1
                    pe.wait_ge(e_ok, 6 * c + (i + 1))
                    pe.wait_ge(pt_ok, 6 * c + max(i - 1, 0))
                    for j in range(tiles):
                        last = nc.tensor.transpose(k.psum[:, 6 + i % 2, P * j:P * j + P], probs[i][:, P * j:P * j + P], k.ident[:])
                    last.then_inc(pt_done, 1)
                    if i:
                        values(pe, c, i - 1)
                values(pe, c, 5)

        @block.gpsimd
        def _(pool):
            with pool.Fori(0, H // 2) as c:
                pool.wait_ge(s_done, 6 * c)
                for dst, src in ((qs, q3), (ks, k3), (kcs, kc)):
                    nc.gpsimd.tensor_copy(dst, src[:, bass.ds(c, 1), :].squeeze(1)).then_inc(staged, 1)

        @block.scalar
        def _(act):
            with act.Fori(0, H // 2) as c:
                for i, (e, n) in enumerate(UNITS):
                    act.wait_ge(m_ok, 6 * c + (i + 1))
                    src = probs[i] if n else score_bank(i)[:, 0:CTX]
                    if not n:
                        act.wait_ge(pt_done, 6 * c)
                    nc.scalar.activation(probs[i], src, ACT.Exp, bias=neg_max[:, i:i + 1], accum_out=total[:, i:i + 1]).then_inc(e_ok, 1)
                    if i:
                        turn(act, c, i - 1)
                turn(act, c, 5)

        @block.vector
        def _(dve):
            with dve.Fori(0, H // 2) as c:
                for i, (e, n) in enumerate(UNITS):
                    dve.wait_ge(s_done, 6 * c + (i + 1))
                    if n:
                        lo = GRID * (2 - 2 * (n - 1))
                        nc.vector.tensor_tensor(probs[i][:, 0:LAT], score_bank(i)[:, 0:LAT],
                                                bias[:, bass.ds(2 * c + e, 1), lo:lo + LAT].squeeze(1), ALU.add).then_inc(s_ok, 1)
                        nc.vector.tensor_copy(probs[i][:, LAT:LK], score_bank(i)[:, LAT:LK]).then_inc(s_ok, 1)
                        dve.wait_ge(s_ok, 8 * c + (2 * i + 2))
                        src = probs[i]
                    else:
                        src = score_bank(i)[:, 0:CTX]
                    nc.vector.tensor_reduce(neg_max[:, i:i + 1], src, AX.X, ALU.max, negate=True).then_inc(m_ok, 1)
                for i, (e, n) in enumerate(UNITS):
                    dve.wait_ge(e_ok, 6 * c + (i + 1))
                    nc.vector.reciprocal(inverse[:, i:i + 1], total[:, i:i + 1]).then_inc(r_ok, 1)
                for i, (e, n) in enumerate(UNITS):
                    dve.wait_ge(o_done, 6 * c + (i + 1))
                    dve.wait_ge(r_ok, 6 * c + (i + 1))
                    nc.vector.tensor_scalar(o3[:, n, bass.ds(P * c + 64 * e, 64)], k.psum[:, i, 448:512], inverse[:, i:i + 1],
                                            None, ALU.mult).then_inc(o_ok, 1)


def phase_na_out(k):
    nc = k.nc
    first = k.taken
    k.taken += 6
    o_turned, o_read, done, added = (k.sem("na_out_" + n) for n in ("turned", "read", "done", "added"))
    o3, ot, x = k.tok3(S_AF), k.act3(S_Y), k.act3(S_AB)

    @k.block()
    def _(block):
        @block.tensor
        def _(pe):
            for c in range(DC):
                if c >= 4:
                    pe.wait_ge(o_read, 2 * (c - 3))
                for n in range(NT):
                    last = nc.tensor.transpose(k.psum[:, c % 4, P * n:P * n + P], o3[:, n, P * c:P * c + P], k.ident[:])
                last.then_inc(o_turned, 1)
            for m in range(DC):
                if m % 2 == 0:
                    w = piece_cols(take_piece(k, pe, first + m // 2))
                if m >= 4:
                    pe.wait_ge(added, 2 * (m - 3))
                for c in range(DC):
                    pe.wait_ge(o_read, 2 * (c + 1))
                    last = nc.tensor.matmul(k.psum[:, 4 + m % 4, 0:T], w[:, c, P * (m % 2):P * (m % 2) + P], ot[:, c, :],
                                            start=c == 0, stop=c == DC - 1)
                last.then_inc(done, 1)
                k.used[first + m // 2] = (done, m + 1)

        @block.sync
        def _(sp):
            prefetch(k, sp, first, first + 6)

        @block.scalar
        def _(act):
            for c in range(DC):
                act.wait_ge(o_turned, c + 1)
                nc.scalar.copy(ot[:, c, 0:CTX], k.psum[:, c % 4, 0:CTX]).then_inc(o_read, 1)
                nc.scalar.copy(ot[:, c, CTX:T].rearrange("p (r n) -> p r n", n=GRID),
                               k.psum[:, c % 4, CTX:T].rearrange("p (r n) -> p r n", n=GRID)[:, :, ::-1]).then_inc(o_read, 1)

        @block.vector
        def _(dve):
            for m in range(DC):
                dve.wait_ge(done, m + 1)
                residual(k, dve, x, m, k.psum[:, 4 + m % 4, 0:T], 16, added)


def phase_store(k, y_slab, out_slab):
    nc = k.nc
    turned, read_out, stored = (k.sem("store_" + n) for n in ("turned", "read", "stored"))
    y, out = k.act3(y_slab), k.tok3(out_slab)

    @k.block()
    def _(block):
        @block.tensor
        def _(pe):
            for n in range(NT):
                for g in range(2):
                    for c in range(4):
                        last = nc.tensor.transpose(k.psum[:, 2 * n + g, P * c:P * c + P], y[:, 4 * g + c, P * n:P * n + P], k.ident[:])
                    last.then_inc(turned, 1)

        @block.vector
        def _(dve):
            for n in range(NT):
                for g in range(2):
                    dve.wait_ge(turned, 2 * n + g + 1)
                    nc.vector.tensor_copy(out[:, n, 512 * g:512 * g + 512], k.psum[:, 2 * n + g, :]).then_inc(read_out, 1)

        @block.sync
        def _(sp):
            for n in range(NT):
                sp.wait_ge(read_out, 2 * n + 2)
                dst = k.a["y_prompt"][0] if n == 0 else k.a["y_sample"][0, P * (n - 1):P * n, :]
                sp.dma_start(dst, out[:, n, :]).then_inc(stored, 16)
            sp.wait_ge(stored, 48)


INPUTS = ["x_prompt", "x_sample", "c", "state_rwkv", "cache_na_k", "cache_na_v", "c_ctx", "norm_mix", "norm_ffn",
          "ada_w", "ada_b", "rwkv_mu", "rwkv_w_r", "rwkv_w_k", "rwkv_w_v", "rwkv_w_o", "rwkv_w0", "rwkv_w1", "rwkv_w2",
          "rwkv_a0", "rwkv_a1", "rwkv_a2", "rwkv_g1", "rwkv_g2", "rwkv_k_k", "rwkv_k_a", "rwkv_r_k", "rwkv_lnx_g",
          "rwkv_lnx_b", "na_w_qkv", "na_w_o", "na_rpb", "moe_w_grp", "moe_b_grp", "moe_w_exp", "moe_b_exp",
          "moe_w1", "moe_w3", "moe_w2", "final_norm"]
OUTPUTS = [("y_prompt", (1, CTX, D)), ("y_sample", (1, LAT, D)), ("new_state", (1, 1, 2, H, HD, HD)),
           ("new_k", (1, 1, CTX, H, HD)), ("new_v", (1, 1, CTX, H, HD))]


def program(nc, a, ctx, stop=99):
    k = Kernel(nc, a, ctx)
    add_pieces(k)
    steps = [
        lambda: phase_inputs(k),
        lambda: phase_ada(k, 0),
        lambda: phase_norm(k, "mix0", S_Y, S_PF, S_NKK, V_NMIX, 0),
        lambda: phase_rwkv_project(k),
        lambda: phase_rwkv_rates(k),
        lambda: phase_scan(k),
        lambda: phase_rwkv_out(k),
        lambda: phase_norm(k, "ffn0", S_AB, S_Y, S_PF, V_NFFN, 24),
        lambda: phase_router(k, 0, S_Y),
        lambda: phase_moe(k, 0, S_Y, S_PF),
        lambda: phase_moe_out(k, 0, S_PF, S_AB),
        lambda: phase_ada(k, 1),
        lambda: phase_norm(k, "mix1", S_AB, S_Y, S_PF, V_NMIX + 8, 0),
        lambda: phase_qkv(k),
        lambda: phase_attention(k),
        lambda: phase_na_out(k),
        lambda: phase_norm(k, "ffn1", S_AB, S_Y, S_PF, V_NFFN + 8, 24),
        lambda: phase_router(k, 1, S_Y),
        lambda: phase_moe(k, 1, S_Y, S_PF),
        lambda: phase_moe_out(k, 1, S_PF, S_AB),
        lambda: phase_norm(k, "final", S_AB, S_Y, S_PF, V_FIN, None),
        lambda: phase_store(k, S_Y, S_PF),
    ]
    for s in steps[:stop]:
        s()
    return k


def kernel(**inputs):
    import concourse.bacc as bacc
    from concourse.bass_utils import run_bass_kernel_spmd

    nc = bacc.Bacc("TRN2", target_bir_lowering=False, num_devices=1)
    arrays, a = {}, {}
    given = {n: np.ascontiguousarray(inputs[n]) for n in INPUTS}
    for n, x in {**given, **constants()}.items():
        arrays[n] = x
        a[n] = nc.dram_tensor(n, x.shape, F32, kind="ExternalInput").ap()
    for n, shape in OUTPUTS:
        a[n] = nc.dram_tensor(n, shape, F32, kind="ExternalOutput").ap()
    a["scratch"] = nc.dram_tensor("scratch", (H, 15, P), F32, kind="Internal").ap()
    with ExitStack() as ctx:
        program(nc, a, ctx)
    got = run_bass_kernel_spmd(nc, [arrays], core_ids=[0]).results[0]
    return tuple(got[n] for n, _ in OUTPUTS)
```

```python
from contextlib import ExitStack

import numpy as np
import concourse.bass as bass
from concourse import mybir

F32 = mybir.dt.float32
BF16 = mybir.dt.bfloat16
I32 = mybir.dt.int32
ALU = mybir.AluOpType
ACT = mybir.ActivationFunctionType
AX = mybir.AxisListType

P = 128
D = 1024
DC = D // P
CTX, LAT = 128, 256
T = CTX + LAT
NT = T // P
H, HD = 16, 64
NS = 6
PIECE = 2048
NE, DE = 16, 256
OVER = 2 * T // (P + 1)
BLOCKS = NE + OVER
NG, EPG = 4, 4
LEVELS = 6
DECAY = float(np.exp(-0.5))
EPS, GN_EPS = 1e-6, 64e-5
GRID, ROWS = 64, LAT // 64
WIN_C = 16
BIG = 1e30

V_NMIX, V_NFFN, V_FIN, V_C, V_CCTX, V_MU, V_KK, V_KA, V_RK = 0, 16, 32, 40, 48, 56, 104, 112, 120
V_W0, V_A0, V_LG, V_LB, V_ADAB = 128, 144, 160, 168, 176
NV = 272

SLAB = 3096
S_Y, S_PF, S_PB, S_AF, S_AB, S_R, S_K, S_V, S_NKK = range(9)
NSLAB = 9


def constants():
    s = np.arange(P)
    same = (s[:, None] // HD) == (s[None, :] // HD)
    out = {
        "c_ident": np.eye(P),
        "c_mean": np.full((P, P), 1.0 / D),
        "c_block": same * 1.0,
    }
    hs = np.zeros((P, DC, H))
    for c in range(DC):
        for p in range(P):
            hs[p, c, 2 * c + p // HD] = 1.0
    out["c_headsum"] = hs.reshape(P, DC * H)
    out["c_headcast"] = np.ascontiguousarray(hs.transpose(2, 1, 0)).reshape(H, DC * P)
    reset = np.ones((P, NT, P + 1))
    reset[:, :, 0] = 0.0
    out["c_reset"] = reset.reshape(P, NT * (P + 1))
    earlier = s[:, None] < s[None, :]
    causal = np.zeros((P, 2, 2, P))
    causal[:, 0, 0], causal[:, 0, 1] = earlier, earlier | np.eye(P, dtype=bool)
    causal[:, 1, 0], causal[:, 1, 1] = earlier.T, earlier.T | np.eye(P, dtype=bool)
    out["c_causal"] = causal.reshape(P, 4 * P)
    level = np.zeros((P, 2, LEVELS + 1, HD))
    for l in range(LEVELS + 1):
        m = 1 << l
        for d in range(2):
            early = [n for n in range(P) if (n // m) % 2 == d]
            for j, n in enumerate(early):
                for t in range(P):
                    level[t, d, l, j] = float(t // (2 * m) == n // (2 * m) and (t // m) % 2 != d)
    out["c_level"] = level.reshape(P, 2 * (LEVELS + 1) * HD)
    col = np.arange(GRID)
    start = np.clip(col - WIN_C // 2, 0, GRID - WIN_C)[:, None]
    cap = np.where((col[None] >= start) & (col[None] < start + WIN_C), 3e38, -BIG)
    out["c_cap"] = np.concatenate([cap[::-1], cap[::-1]])
    out["c_order"] = np.tile(np.arange(EPG, 0, -1.0), (P, NT)).reshape(P, NT * EPG)
    out["c_count"] = np.concatenate([np.tile(s, (P, 1)), s[:, None] + P * np.arange(NT)], 1)
    return {k: np.ascontiguousarray(v, dtype=np.float32) for k, v in out.items()}


class Kernel:

    def __init__(self, nc, a, ctx):
        self.nc, self.a, self.ctx = nc, a, ctx
        self.taken = 0
        self.arrival = []
        self.used = {}
        self.overflow = [0] * OVER
        self.plan = []
        sb = self.sb
        self.slab = sb("slab", [P, NSLAB, SLAB])
        self.ring = sb("ring", [P, NS, PIECE])
        self.ws = sb("ws", [P, 9984])
        self.ident = sb("ident", [P, P])
        self.mean = sb("mean", [P, P])
        self.vec = sb("vec", [P, NV])
        self.mod = sb("mod", [P, 48, 2])
        self.silu_c = sb("silu_c", [P, DC, 2])
        self.omka = sb("omka", [P, DC])
        self.sgate = sb("sgate", [P, T])
        self.s0t = sb("s0t", [P, 2, DC, HD])
        self.ep0 = sb("ep0", [P, 2, DC, NT])
        self.epe = sb("epe", [P, 2, DC, NT])
        self.headsum = sb("headsum", [P, DC, H])
        self.causal = sb("causal", [P, 2, 2, P], BF16)
        self.level = sb("level", [P, 2, LEVELS + 1, HD], BF16)
        self.ones16 = sb("ones16", [P, P + NT * NE], BF16)
        self.slots = self.slab[:, S_K, DC * T:DC * T + 2 * NT].bitcast(I32)
        self.overflow_expert = self.slab[:, S_K, DC * T + 8:DC * T + 8 + OVER].bitcast(I32)
        self.block_tokens = self.slab[:, S_V, DC * T:DC * T + BLOCKS].bitcast(I32)
        self.psum = ctx.enter_context(nc.psum_tensor("psum", [P, 8, 512], F32))
        self.ring_in = [nc.alloc_semaphore(name=f"ring_in{i}") for i in range(NS)]
        self.phase_sems = []

    def sb(self, name, shape, dt=F32):
        return self.ctx.enter_context(self.nc.sbuf_tensor(name, shape, dt))

    def sem(self, name):
        self.phase_sems.append(self.nc.alloc_semaphore(name=name))
        return self.phase_sems[-1]

    def block(self):
        def run(body):
            with self.nc.Block() as block:
                body(block)
            self.nc.clear_and_free_semaphores(self.phase_sems)
            self.nc.all_engine_barrier()
            self.phase_sems = []
        return run

    def act3(self, s):
        return self.slab[:, s, 0:DC * T].rearrange("p (c t) -> p c t", c=DC)

    def tok3(self, s):
        return self.slab[:, s, 0:NT * D].rearrange("p (n d) -> p n d", n=NT)

    def p4(self, s):
        return self.slab[:, s, :].rearrange("p (c n t) -> p c n t", c=DC, n=NT)


def cols(w, j):
    return w[:, j * 256:(j + 1) * 256].rearrange("(c p) n -> p c n", p=P)


def add_pieces(k):
    a = k.a

    def whole(src, parts=DC):
        return lambda slot: [(k.ring[:, slot, :].rearrange("p (c n) -> p c n", c=parts), src)]

    def lora_in(slot):
        w = k.ring[:, slot, :].rearrange("p (g c n) -> p g c n", g=2, c=DC)
        return ([(w[:, 0, :, 64 * d:64 * d + 64], a["rwkv_w1"][0, d].rearrange("(c p) n -> p c n", p=P))
                 for d in range(2)]
                + [(w[:, 1, :, 64 * d:64 * d + 64], a["rwkv_a1"][0, d].rearrange("(c p) n -> p c n", p=P))
                   for d in range(2)])

    def gate_in(slot):
        w = k.ring[:, slot, 0:D].rearrange("p (c n) -> p c n", c=DC)
        return [(w, a["rwkv_g1"][0].rearrange("(c p) n -> p c n", p=P))]

    def lora_out(slot):
        return [(k.ring[:, slot, 0:D], a["rwkv_w2"][0].rearrange("d r n -> (d r) n")),
                (k.ring[:, slot, D:2 * D], a["rwkv_a2"][0].rearrange("d r n -> (d r) n"))]

    def gate_out(slot):
        return [(k.ring[:, slot, 0:D], a["rwkv_g2"][0])]

    plan = [whole(cols(a["ada_w"][0], j)) for j in range(24)]
    plan += [lora_in, gate_in]
    for n in ("rwkv_w_r", "rwkv_w_k", "rwkv_w_v"):
        plan += [whole(cols(a[n][0], j)) for j in range(4)]
    plan += [lora_out, gate_out] + [whole(cols(a["rwkv_w_o"][0], j)) for j in range(4)] + [None] * 4

    def block_piece(name, layer, b, parts):
        def piece(slot):
            e = b if b < NE else bass.ds(k.overflow[b - NE], 1)
            src = a[name][layer][e] if b < NE else a[name][layer][e].rearrange("e r n -> (e r) n")
            return [(k.ring[:, slot, :].rearrange("p (c n) -> p c n", c=parts), src.rearrange("(c p) n -> p c n", p=P))]
        return piece

    def experts(layer):
        w1, w3, w2 = ([block_piece(n, layer, b, parts) for b in range(BLOCKS)]
                      for n, parts in (("moe_w1", DC), ("moe_w3", DC), ("moe_w2", 2)))
        out = [w1[0], w3[0]]
        for b in range(BLOCKS):
            out += ([w1[b + 1], w3[b + 1]] if b + 1 < BLOCKS else []) + [w2[b]]
        return out + [None] * 3

    plan += experts(0) + [whole(cols(a["ada_w"][1], j)) for j in range(24)]
    plan += [whole(cols(a["na_w_qkv"][0], j)) for j in range(12)]
    plan += [whole(cols(a["na_w_o"][0], j)) for j in range(4)] + [None] * 2 + experts(1)
    k.plan = plan
    raised = [0] * NS
    for n, piece in enumerate(plan):
        raised[n % NS] += 16 * len(piece(n % NS)) if piece else 0
        k.arrival.append(raised[n % NS])


def load_piece(k, eng, n, first=0):
    if n >= len(k.plan) or k.plan[n] is None:
        return
    slot, before = n % NS, n - NS
    if before >= first and k.plan[before] is None:
        before -= NS
    if before >= first and before in k.used:
        sem, value = k.used[before]
        eng.wait_ge(sem, value)
    for dst, src in k.plan[n](slot):
        eng.dma_start(dst, src).then_inc(k.ring_in[slot], 16)


def take_piece(k, eng, n):
    eng.wait_ge(k.ring_in[n % NS], k.arrival[n])
    return k.ring[:, n % NS, :]


def prefetch(k, eng, first, last):
    for n in range(first + NS, last + NS):
        load_piece(k, eng, n, first)


def piece_cols(w):
    return w.rearrange("p (c n) -> p c n", c=DC)
def load_tokens(k, eng, dst, sem):
    eng.dma_start(dst[:, 0, :], k.a["x_prompt"][0]).then_inc(sem, 16)
    eng.dma_start(dst[:, 1:NT, :], k.a["x_sample"][0].rearrange("(n p) d -> p n d", p=P)).then_inc(sem, 16)


def phase_inputs(k):
    nc, a = k.nc, k.a
    consts_in, vec_in, x_in = k.sem("consts_in"), k.sem("vec_in"), k.sem("x_in")
    vec_t, vec_ok, x_t, x_half = k.sem("vec_t"), k.sem("vec_ok"), k.sem("x_t"), k.sem("x_half")
    sig_c, masks_in = k.sem("sig_c"), k.sem("masks_in")
    rows = [k.ws[0:n, 128 * i:128 * i + 128] for i, n in enumerate((128, 48, 96))]
    masks = k.ws[:, 512:512 + 4 * P + 2 * (LEVELS + 1) * HD]
    xt = k.tok3(S_R)
    x3 = k.act3(S_Y)
    vp = k.psum[:, 0, 0:NV]
    pieces = NS

    @k.block()
    def _(block):
        @block.sync
        def _(sp):
            sp.dma_start(k.ident[:], a["c_ident"]).then_inc(consts_in, 16)
            rvecs = [("norm_mix", 0, 16), ("norm_ffn", 16, 16), ("final_norm", 32, 8), ("c", 40, 8), ("c_ctx", 48, 8),
                     ("rwkv_mu", 56, 48), ("rwkv_k_k", 104, 8), ("rwkv_k_a", 112, 8), ("rwkv_r_k", 120, 8)]
            for n, at, m in rvecs:
                sp.dma_start(rows[0][at:at + m, :], flat(a[n])).then_inc(vec_in, 16)
            for n, at, m in (("rwkv_w0", 0, 16), ("rwkv_a0", 16, 16), ("rwkv_lnx_g", 32, 8), ("rwkv_lnx_b", 40, 8)):
                sp.dma_start(rows[1][at:at + m, :], flat(a[n])).then_inc(vec_in, 16)
            sp.dma_start(rows[2], flat(a["ada_b"])).then_inc(vec_in, 16)
            for n in range(pieces):
                load_piece(k, sp, n)

        @block.scalar
        def _(act):
            load_tokens(k, act, xt, x_in)
            act.dma_start(k.mean[:], a["c_mean"]).then_inc(masks_in, 16)
            act.dma_start(k.headsum[:], a["c_headsum"].rearrange("p (c h) -> p c h", c=DC)).then_inc(masks_in, 16)
            act.dma_start(masks[:, 0:4 * P], a["c_causal"]).then_inc(masks_in, 16)
            act.dma_start(masks[:, 4 * P:], a["c_level"]).then_inc(masks_in, 16)
            act.wait_ge(vec_ok, 1)
            c2 = k.vec[:, V_C:V_C + 16].rearrange("p (s c) -> p c s", s=2)
            nc.scalar.activation(k.silu_c[:, :, 0:1], c2[:, :, 1:2], ACT.Silu).then_inc(sig_c, 1)
            nc.scalar.activation(k.silu_c[:, :, 1:2], c2[:, :, 0:1], ACT.Silu).then_inc(sig_c, 1)
            act.wait_ge(x_t, 4)
            nc.scalar.copy(x3[:, 4:8, :], k.psum[:, 4:8, 0:T]).then_inc(x_half, 1)

        @block.gpsimd
        def _(pool):
            pool.wait_ge(masks_in, 64)
            nc.gpsimd.tensor_copy(k.causal[:].rearrange("p d k t -> p (d k t)"), masks[:, 0:4 * P]).then_inc(sig_c, 1)
            nc.gpsimd.tensor_copy(k.level[:].rearrange("p d l t -> p (d l t)"), masks[:, 4 * P:]).then_inc(sig_c, 1)

        @block.tensor
        def _(pe):
            pe.wait_ge(consts_in, 16)
            pe.wait_ge(vec_in, 16 * 14)
            at = 0
            for r in rows:
                n = r.shape[0]
                last = nc.tensor.transpose(vp[:, at:at + n], r, k.ident[0:n, 0:n])
                at += n
            last.then_inc(vec_t, 1)
            pe.wait_ge(x_in, 32)
            for c in range(DC - 1, -1, -1):
                if c == 0:
                    pe.wait_ge(vec_ok, 1)
                for n in range(NT):
                    last = nc.tensor.transpose(k.psum[:, c, n * P:(n + 1) * P], xt[:, n, c * P:(c + 1) * P], k.ident[:])
                last.then_inc(x_t, 1)

        @block.vector
        def _(dve):
            dve.wait_ge(vec_t, 1)
            nc.vector.tensor_copy(k.vec[:], vp).then_inc(vec_ok, 1)
            dve.wait_ge(vec_ok, 1)
            nc.vector.tensor_scalar(k.omka[:], k.vec[:, V_KA:V_KA + 8], -1.0, 1.0, ALU.mult, ALU.add).then_inc(x_half, 1)
            dve.wait_ge(x_t, 8)
            nc.vector.tensor_copy(x3[:, 0:4, :], k.psum[:, 0:4, 0:T]).then_inc(x_half, 1)


def flat(ap):
    names = "abcdef"[:len(ap.shape)]
    s = " ".join(names)
    if len(ap.shape) > 1:
        ap = ap.rearrange(f"{s} -> ({s})")
    return ap.rearrange("(r q) -> r q", q=P)


def phase_ada(k, layer):
    nc = k.nc
    first = k.taken
    k.taken += 24
    multiplied = k.sem(f"ada{layer}_multiplied")
    added = k.sem(f"ada{layer}_added")
    acc = k.psum[:, 0, 0:96]

    @k.block()
    def _(block):
        @block.tensor
        def _(pe):
            base = [k.arrival[first + u] for u in range(NS)]
            with pe.Fori(0, 4) as i:
                for u in range(NS):
                    pe.wait_ge(k.ring_in[u], 16 * i + base[u])
                    w = piece_cols(k.ring[:, u, :])
                    for m in range(2):
                        out = acc[:, bass.ds(4 * NS * i + 4 * u + 2 * m, 2)]
                        for c in range(DC):
                            last = nc.tensor.matmul(out, w[:, c, m * P:(m + 1) * P], k.silu_c[:, c, :],
                                                    start=c == 0, stop=c == DC - 1)
                    last.then_inc(multiplied, 1)
            for u in range(NS):
                k.used[first + 18 + u] = (multiplied, 19 + u)

        @block.sync
        def _(sp):
            with sp.Fori(0, 3) as i:
                for u in range(NS):
                    sp.wait_ge(multiplied, NS * i + u + 1)
                    src = k.a["ada_w"][layer][:, bass.ds(256 * NS * i + 256 * (NS + u), 256)]
                    sp.dma_start(piece_cols(k.ring[:, u, :]), src.rearrange("(c p) n -> p c n", p=P)).then_inc(k.ring_in[u], 16)
            prefetch(k, sp, first + 18, first + 24)

        @block.vector
        def _(dve):
            dve.wait_ge(multiplied, 24)
            bias = k.vec[:, V_ADAB + 48 * layer:V_ADAB + 48 * layer + 48]
            nc.vector.tensor_tensor(k.mod[:], acc.rearrange("p (j s) -> p j s", s=2),
                                    bias.unsqueeze(2).to_broadcast([P, 48, 2]), ALU.add).then_inc(added, 1)


def phase_norm(k, name, x_slab, h_slab, tmp_slab, v_gain, mod_at):
    nc = k.nc
    squared, summed, meaned, rooted, scaled = (k.sem(f"{name}_{s}") for s in ("squared", "summed", "meaned", "rooted", "scaled"))
    step, out_act = k.sem(f"{name}_step"), k.sem(f"{name}_act")
    x, h, tmp = k.act3(x_slab), k.act3(h_slab), k.act3(tmp_slab)
    acc = k.psum[:, 0, 0:T]
    ms, root, rstd = k.ws[:, 0:T], k.ws[:, T:2 * T], k.ws[:, 2 * T:3 * T]
    gs = k.ws[:, 3 * T:3 * T + 16].rearrange("p (c s) -> p c s", s=2)
    gain = k.vec[:, v_gain:v_gain + DC]

    @k.block()
    def _(block):
        @block.scalar
        def _(act):
            for g in range(4):
                nc.scalar.activation(tmp[:, 2 * g:2 * g + 2, :], x[:, 2 * g:2 * g + 2, :], ACT.Square).then_inc(squared, 1)
            act.wait_ge(meaned, 1)
            nc.scalar.activation(root, ms, ACT.Sqrt).then_inc(rooted, 1)
            if mod_at is not None:
                for c in range(4, DC):
                    act.wait_ge(scaled, c - 3)
                    for s, (t0, t1) in enumerate(((0, CTX), (CTX, T))):
                        nc.scalar.activation(h[:, c, t0:t1], tmp[:, c, t0:t1], ACT.Identity,
                                             bias=k.mod[:, mod_at + c, s:s + 1], scale=gs[:, c, s:s + 1]).then_inc(out_act, 1)

        @block.tensor
        def _(pe):
            for c in range(DC):
                pe.wait_ge(squared, c // 2 + 1)
                last = nc.tensor.matmul(acc, k.mean[:], tmp[:, c, :], start=c == 0, stop=c == DC - 1)
            last.then_inc(summed, 1)

        @block.vector
        def _(dve):
            if mod_at is not None:
                nc.vector.scalar_tensor_tensor(gs, k.mod[:, mod_at + DC:mod_at + 2 * DC, :], 1.0,
                                               gain.unsqueeze(2).to_broadcast([P, DC, 2]), ALU.add, ALU.mult).then_inc(step, 1)
            else:
                nc.vector.tensor_copy(gs[:, :, 0], gain).then_inc(step, 1)
            dve.wait_ge(summed, 1)
            nc.vector.tensor_scalar(ms, acc, EPS, None, ALU.add).then_inc(meaned, 1)
            dve.wait_ge(rooted, 1)
            nc.vector.reciprocal(rstd, root).then_inc(step, 1)
            dve.wait_ge(step, 2)
            for c in list(range(4, DC)) + list(range(4)):
                nc.vector.tensor_tensor(tmp[:, c, :], x[:, c, :], rstd, ALU.mult).then_inc(scaled, 1)
            for c in range(4):
                dve.wait_ge(scaled, c + 5)
                if mod_at is None:
                    nc.vector.tensor_scalar(h[:, c, :], tmp[:, c, :], gs[:, c, 0:1], None, ALU.mult).then_inc(step, 1)
                    nc.vector.tensor_scalar(h[:, c + 4, :], tmp[:, c + 4, :], gs[:, c + 4, 0:1], None, ALU.mult).then_inc(step, 1)
                else:
                    for s, (t0, t1) in enumerate(((0, CTX), (CTX, T))):
                        nc.vector.tensor_scalar(h[:, c, t0:t1], tmp[:, c, t0:t1], gs[:, c, s:s + 1],
                                                k.mod[:, mod_at + c, s:s + 1], ALU.mult, ALU.add).then_inc(step, 1)


def phase_rwkv_project(k):
    nc = k.nc
    first = k.taken
    k.taken += 14
    mixed = k.sem("mixed")
    proj, read_out = k.sem("proj"), k.sem("proj_read")
    step = k.sem("shift_step")
    h, dx = k.act3(S_PF), k.act3(S_PB)
    mix = [k.act3(S_AF), k.act3(S_AB)]
    r3, k3, v3 = k.act3(S_R), k.act3(S_K), k.tok3(S_V)
    t1, t2 = k.ws[:, 0:T], k.ws[:, T:2 * T]
    MIX_ORDER = [1, 4, 5, 0, 2, 3]

    def bank(o):
        return k.psum[:, o % 8, :]

    @k.block()
    def _(block):
        @block.vector
        def _(dve):
            n = 0
            for t0, t1_ in ((0, CTX), (CTX, T)):
                nc.vector.tensor_tensor(dx[:, :, t0 + 1:t1_ - 1], h[:, :, t0:t1_ - 2], h[:, :, t0 + 2:t1_], ALU.add).then_inc(step, 1)
                nc.vector.tensor_copy(dx[:, :, t0:t0 + 1], h[:, :, t0 + 1:t0 + 2]).then_inc(step, 1)
                nc.vector.tensor_copy(dx[:, :, t1_ - 1:t1_], h[:, :, t1_ - 2:t1_ - 1]).then_inc(step, 1)
            dve.wait_ge(step, 6)
            for g in range(2):
                nc.vector.scalar_tensor_tensor(dx[:, 4 * g:4 * g + 4, :], dx[:, 4 * g:4 * g + 4, :], 0.5,
                                               h[:, 4 * g:4 * g + 4, :], ALU.mult, ALU.subtract).then_inc(step, 1)
            dve.wait_ge(step, 8)
            for i, mu in enumerate(MIX_ORDER):
                if i >= 2:
                    dve.wait_ge(proj, i - 1 if i < 5 else 11)
                for c in range(DC):
                    nc.vector.scalar_tensor_tensor(mix[i % 2][:, c, :], dx[:, c, :], k.vec[:, V_MU + 8 * mu + c:V_MU + 8 * mu + c + 1],
                                                   h[:, c, :], ALU.mult, ALU.add).then_inc(mixed, 1)

        @block.tensor
        def _(pe):
            for i in range(3):
                if i != 1:
                    piece = take_piece(k, pe, first + i // 2)
                w = piece_cols(piece[:, D * (i % 2):D * (i % 2) + D])
                for c in range(DC):
                    pe.wait_ge(mixed, 8 * i + c + 1)
                    last = nc.tensor.matmul(bank(i)[:, 0:T], w[:, c, :], mix[i % 2][:, c, :], start=c == 0, stop=c == DC - 1)
                last.then_inc(proj, 1)
            k.used[first], k.used[first + 1] = (proj, 2), (proj, 3)
            o = 3
            for i in range(3, 5):
                for j in range(4):
                    n = first + 2 + 4 * (i - 3) + j
                    w = piece_cols(take_piece(k, pe, n))
                    for m in range(2):
                        if o >= 8:
                            pe.wait_ge(read_out, o - 7)
                        for c in range(DC):
                            if j == 0 and m == 0:
                                pe.wait_ge(mixed, 8 * i + c + 1)
                            last = nc.tensor.matmul(bank(o)[:, 0:T], w[:, c, m * P:(m + 1) * P], mix[i % 2][:, c, :],
                                                    start=c == 0, stop=c == DC - 1)
                        last.then_inc(proj, 1)
                        o += 1
                    k.used[n] = (proj, o)
            for j in range(4):
                w = piece_cols(take_piece(k, pe, first + 10 + j))
                for n in range(NT):
                    pe.wait_ge(read_out, o - 7)
                    for c in range(DC):
                        if j == 0 and n == 0:
                            pe.wait_ge(mixed, 40 + c + 1)
                        last = nc.tensor.matmul(bank(o)[:, 0:256], mix[1][:, c, n * P:(n + 1) * P], w[:, c, :],
                                                start=c == 0, stop=c == DC - 1)
                    last.then_inc(proj, 1)
                    o += 1
                k.used[first + 10 + j] = (proj, o)

        @block.sync
        def _(sp):
            prefetch(k, sp, first, first + 14)

        @block.scalar
        def _(act):
            act.wait_ge(proj, 1)
            nc.scalar.activation(t1, bank(0)[:, 0:T], ACT.Tanh).then_inc(read_out, 1)
            act.wait_ge(proj, 2)
            nc.scalar.copy(t2, bank(1)[:, 0:T]).then_inc(read_out, 1)
            act.wait_ge(proj, 3)
            nc.scalar.activation(k.sgate[:], bank(2)[:, 0:T], ACT.Sigmoid).then_inc(read_out, 1)
            o = 3
            for dst in (r3, k3):
                for c in range(DC):
                    act.wait_ge(proj, o + 1)
                    nc.scalar.copy(dst[:, c, :], bank(o)[:, 0:T]).then_inc(read_out, 1)
                    o += 1
            for j in range(4):
                for n in range(NT):
                    act.wait_ge(proj, o + 1)
                    nc.scalar.copy(v3[:, n, 256 * j:256 * j + 256], bank(o)[:, 0:256]).then_inc(read_out, 1)
                    o += 1


def phase_rwkv_rates(k):
    nc = k.nc
    first = k.taken
    k.taken += 1
    names = ("z_done", "z_read", "consts2_in", "scanned", "kk_scaled", "kk_squared", "kk_summed", "kk_copied", "kk_rooted",
             "kk_floored", "kk_inverse", "cast_done", "nkk_ok", "state_in", "state_turned", "state_ok", "edges_ok", "mid_ok",
             "centred", "edge_zero")
    (z_done, z_read, consts2, scanned, kk_scaled, kk_squared, kk_summed, kk_copied, kk_rooted, kk_floored, kk_inverse,
     cast_done, nkk_ok, state_in, state_turned, state_ok, edges_ok, mid_ok, centred, edge_zero) = (k.sem(n) for n in names)
    t1, t2 = k.ws[:, 0:T], k.ws[:, T:2 * T]
    reset = k.ws[:, 768:768 + NT * (P + 1)]
    cast = k.ws[0:H, 1160:1160 + D].rearrange("h (c p) -> h c p", c=DC)
    norm2, norm, inverse = (k.ws[0:H, 2200 + T * i:2200 + T * i + T] for i in range(3))
    mid = [k.ws[:, 3356 + 24 * d:3356 + 24 * d + 24] for d in range(2)]
    state = k.ws[0:HD, 3410:3410 + 2 * D]
    k3, kk, sq = k.act3(S_K), k.act3(S_NKK), k.act3(S_AF)
    rates = k.p4(S_Y)

    def z_bank(d, c):
        return k.psum[:, 3 * d + c % 3, 0:T]

    @k.block()
    def _(block):
        @block.tensor
        def _(pe):
            w = take_piece(k, pe, first)

            def outer(i, src):
                for d in range(2):
                    rows = slice(HD * d, HD * d + HD)
                    for c in range(DC):
                        o = 16 * i + 8 * d + c
                        if c >= 3:
                            pe.wait_ge(z_read, o - 2)
                        elif i:
                            pe.wait_ge(z_read, 8 * (2 * i + d - 1))
                        nc.tensor.matmul(z_bank(d, c), w[rows, D * i + c * P:D * i + c * P + P], src[rows, :],
                                         start=True, stop=True).then_inc(z_done, 1)

            outer(0, t1)
            pe.wait_ge(consts2, 32)
            for c in range(DC):
                pe.wait_ge(kk_squared, c + 1)
                last = nc.tensor.matmul(k.psum[0:H, 6, 0:T], k.headsum[:, c, :], sq[:, c, :], start=c == 0, stop=c == DC - 1)
            last.then_inc(kk_summed, 1)
            outer(1, t2)
            k.used[first] = (z_done, 32)
            pe.wait_ge(z_read, 32)
            pe.wait_ge(state_in, 16)
            for d in range(2):
                for c in range(DC):
                    last = nc.tensor.transpose(k.psum[:, d, HD * c:HD * c + HD], state[:, D * d + c * P:D * d + c * P + P],
                                               k.ident[0:HD, 0:HD])
            last.then_inc(state_turned, 1)
            pe.wait_ge(kk_inverse, 1)
            for c in range(DC):
                if c >= 4:
                    pe.wait_ge(nkk_ok, c - 3)
                nc.tensor.matmul(k.psum[:, 2 + c % 4, 0:T], cast[:, c, :], inverse, start=True, stop=True).then_inc(cast_done, 1)

        @block.sync
        def _(sp):
            sp.dma_start(reset, k.a["c_reset"]).then_inc(consts2, 16)
            sp.dma_start(k.ws[0:H, 1160:1160 + D], k.a["c_headcast"]).then_inc(consts2, 16)
            sp.dma_start(state.rearrange("i (e h j) -> i e h j", e=2, h=H),
                         k.a["state_rwkv"][0, 0].rearrange("e h i j -> i e h j")).then_inc(state_in, 16)
            prefetch(k, sp, first, first + 1)

        @block.scalar
        def _(act):
            act.wait_ge(edge_zero, 1)
            for d in range(2):
                if d == 1:
                    act.wait_ge(scanned, 8)
                for c in range(DC):
                    act.wait_ge(z_done, 8 * d + c + 1)
                    nc.scalar.activation(rates[:, c, :, 1:P + 1], z_bank(d, c).rearrange("p (n t) -> p n t", n=NT),
                                         ACT.Sigmoid, bias=k.vec[:, V_W0 + 8 * d + c:V_W0 + 8 * d + c + 1]).then_inc(z_read, 1)
            for c in range(DC):
                act.wait_ge(kk_scaled, c + 1)
                nc.scalar.activation(sq[:, c, :], kk[:, c, :], ACT.Square).then_inc(kk_squared, 1)
            act.wait_ge(kk_summed, 1)
            for d in range(2):
                dst = k.act3((S_AF, S_AB)[d])
                for c in range(DC):
                    act.wait_ge(z_done, 16 + 8 * d + c + 1)
                    nc.scalar.activation(dst[:, c, :], z_bank(d, c), ACT.Sigmoid,
                                         bias=k.vec[:, V_A0 + 8 * d + c:V_A0 + 8 * d + c + 1]).then_inc(z_read, 1)
            act.wait_ge(kk_copied, 1)
            nc.scalar.activation(norm, norm2, ACT.Sqrt).then_inc(kk_rooted, 1)
            act.wait_ge(centred, 2)
            for d in range(2):
                p = k.p4((S_PF, S_PB)[d])
                nc.scalar.activation(k.ep0[:, d, :, :], p[:, :, :, 0], ACT.Exp, scale=DECAY).then_inc(edges_ok, 1)
                nc.scalar.activation(k.epe[:, d, :, :], p[:, :, :, P], ACT.Exp, scale=-DECAY).then_inc(edges_ok, 1)

        @block.vector
        def _(dve):
            nc.vector.memset(rates[:, :, :, 0:1], 0.0).then_inc(edge_zero, 1)
            for c in range(DC):
                nc.vector.tensor_scalar(kk[:, c, :], k3[:, c, :], k.vec[:, V_KK + c:V_KK + c + 1], None, ALU.mult).then_inc(kk_scaled, 1)
            dve.wait_ge(consts2, 32)
            for d in range(2):
                p = k.slab[:, (S_PF, S_PB)[d], :].rearrange("p (c t) -> p c t", c=DC)
                src = k.slab[:, S_Y, :].rearrange("p (c t) -> p c t", c=DC)
                for c in range(DC):
                    dve.wait_ge(z_read, 8 * d + c + 1)
                    nc.vector.tensor_tensor_scan(p[:, c, :], reset, src[:, c, :], 0.0, ALU.mult, ALU.add).then_inc(scanned, 1)
            for d in range(2):
                p = k.slab[:, (S_PF, S_PB)[d], :].rearrange("p (n t) -> p n t", t=P + 1)
                dve.wait_ge(scanned, 8 * d + 8)
                nc.vector.tensor_copy(mid[d], p[:, :, P // 2]).then_inc(mid_ok, 1)
                dve.wait_ge(mid_ok, d + 1)
                nc.vector.tensor_tensor(p, p, mid[d].unsqueeze(2).to_broadcast([P, DC * NT, P + 1]), ALU.subtract).then_inc(centred, 1)
            dve.wait_ge(kk_summed, 1)
            nc.vector.tensor_copy(norm2, k.psum[0:H, 6, 0:T]).then_inc(kk_copied, 1)
            dve.wait_ge(kk_rooted, 1)
            nc.vector.tensor_scalar(norm2, norm, 1e-12, -1.0, ALU.max, ALU.mult).then_inc(kk_floored, 1)
            dve.wait_ge(kk_floored, 1)
            nc.vector.reciprocal(inverse, norm2).then_inc(kk_inverse, 1)
            dve.wait_ge(state_turned, 1)
            dve.wait_ge(edges_ok, 4)
            for d, (e, n) in enumerate(((k.ep0, 1), (k.epe, 2))):
                nc.vector.tensor_tensor(k.s0t[:, d, :, :], k.psum[:, d, :].rearrange("p (c i) -> p c i", c=DC),
                                        e[:, d, :, n:n + 1].to_broadcast([P, DC, HD]), ALU.mult).then_inc(state_ok, 1)
            for c in range(DC):
                dve.wait_ge(cast_done, c + 1)
                nc.vector.tensor_tensor(kk[:, c, :], kk[:, c, :], k.psum[:, 2 + c % 4, 0:T], ALU.mult).then_inc(nkk_ok, 1)


def phase_scan(k):
    nc = k.nc
    WORDS = 4992

    def pair(name):
        return [k.sem(f"scan_{name}{d}") for d in range(2)]

    exp_ok, staged, rate_ok, ar_ok, tmp_ok, kb_ok = (pair(n) for n in ("exp_ok", "staged", "rate_ok", "ar_ok", "tmp_ok", "kb_ok"))
    a_done, a_ok, t_done, t_ok, x_done, x_ok, xt_done, xt_ok = (
        pair(n) for n in ("a_done", "a_ok", "t_done", "t_ok", "x_done", "x_ok", "xt_done", "xt_ok"))
    x_init, r_done, r_ok, u_done, u_ok, y_done, y_ok = (
        pair(n) for n in ("x_init", "r_done", "r_ok", "u_done", "u_ok", "y_done", "y_ok"))
    khat_ok, kt_done, kt_ok, s_done, s_copied, s_out, s_step, s_ok = (
        pair(n) for n in ("khat_ok", "kt_done", "kt_ok", "s_done", "s_copied", "s_out", "s_step", "s_ok"))
    zero_ok = k.sem("scan_zero_ok")

    NL = LEVELS + 1
    TILE = [(0, 0), (1, 2), (2, 1)]

    def at(step, q, per, local):
        return q * per + (4 * per * step + local)

    class Dir:
        def __init__(self, d):
            w = k.ws[:, WORDS * d:WORDS * (d + 1)]
            self.ar = w[:, 0:512].rearrange("p (c g t) -> p c g t", c=2, g=2)
            self.kb = w[:, 512:1024].rearrange("p (g c t) -> p g c t", g=2, c=2)
            self.ak = w[:, 1024:2048].rearrange("p (e c g t) -> p e c g t", e=2, c=2, g=2)
            self.ab = w[:, 2048:3072].rearrange("p (e c g t) -> p e c g t", e=2, c=2, g=2)
            self.x = w[:, 3072:3584].rearrange("p (u t) -> p u t", u=4)
            self.kt = w[:, 3072:3584].rearrange("p (g c f) -> p g c f", g=2, c=2)
            self.xt = w[:, 3584:4096].rearrange("p (u t) -> p u t", u=4)
            self.tmp = w[:, 3584:3840].rearrange("p (c t) -> p c t", c=2)
            self.rate = w[:, 3840:4096].rearrange("p (c t) -> p c t", c=2)
            self.t1 = w[:, 4096:4352].rearrange("p (u n) -> p u n", u=4)
            self.r = self.t1
            self.s = w[:, 4096:4224].rearrange("p (c n) -> p c n", c=2)
            self.u = w[:, 4352:4608].rearrange("p (u n) -> p u n", u=4)
            self.v = w[:, 4608:4864].rearrange("p (c e n) -> p c e n", c=2, e=2)
            self.s0 = w[:, 4864:4992].rearrange("p (c n) -> p c n", c=2)
            self.p = k.p4((S_PF, S_PB)[d])
            self.a = k.act3((S_AF, S_AB)[d])
            self.bank = 4 * d
            self.w_end = (k.epe, k.ep0)[d][:, d]
            self.w_mid = (k.ep0, k.epe)[d][:, d]
            self.late = slice(64, 128) if d == 0 else slice(0, 64)
            self.early = slice(0, 64) if d == 0 else slice(64, 128)

        def halves(self, x, level):
            return x.rearrange("p u (b h m) -> p u b h m", h=2, m=1 << level)

    D2 = [Dir(0), Dir(1)]

    @k.block()
    def _(block):
        @block.tensor
        def _(pe):
            pe.wait_ge(zero_ok, 4)
            for step in range(3):
                with pe.Fori(0, 4) as q:
                    for d, b in enumerate(D2):
                        pe.wait_ge(kb_ok[d], at(step, q, 2, 2))
                        pe.wait_ge(ar_ok[d], at(step, q, 2, 2))
                        pe.wait_ge(y_ok[d], at(step, q, 2, 0))
                        if step < 2:
                            pe.wait_ge((s_copied, s_ok)[step][d], q)
                        else:
                            pe.wait_ge(s_ok[d], 4)
                        for g in range(2):
                            for e in range(2):
                                rows = slice(64 * e, 64 * e + 64)
                                out = k.psum[:, b.bank + 2 * g + e, :].rearrange("p (c g t) -> p c g t", c=2, g=2)
                                for c in range(2):
                                    nc.tensor.matmul(out[:, c, :, b.late], b.kb[rows, g, c, :], b.ar[rows, c, :, b.late],
                                                     start=True, stop=True)
                                    last = nc.tensor.matmul(out[b.early, c, :, b.early], b.kb[rows, g, c, b.early],
                                                            b.ar[rows, c, :, b.early], start=True, stop=True)
                            last.then_inc(a_done[d], 1)
                    for l in range(NL):
                        for d, b in enumerate(D2):
                            if l == 0:
                                pe.wait_ge(a_ok[d], at(step, q, 4, 4))
                            else:
                                pe.wait_ge(x_ok[d], at(step, q, NL, l))
                            for u in range(4):
                                src = k.ident[:].unsqueeze(1) if l == 0 else b.x[:, u:u + 1, :]
                                last = nc.tensor.matmul(k.psum[:, b.bank, 64 * u:64 * u + 64], b.ab[:, u // 2, u % 2, 0, :],
                                                        b.halves(src, l)[:, 0, :, d, :], start=True, stop=True)
                            last.then_inc(t_done[d], 1)
                        if l:
                            for d, b in enumerate(D2):
                                pe.wait_ge(t_ok[d], at(step, q, NL, l + 1))
                                pe.wait_ge(xt_ok[d], at(step, q, NL, l))
                                for u in range(4):
                                    last = nc.tensor.matmul(k.psum[:, b.bank + 1, 64 * u:64 * u + 64], b.xt[:, u, :], b.t1[:, u, :],
                                                            start=True, stop=True)
                                last.then_inc(x_done[d], 1)
                        for d, b in enumerate(D2):
                            pe.wait_ge(x_ok[d], at(step, q, NL, l + 1))
                            for u in range(4):
                                last = nc.tensor.transpose(k.psum[:, b.bank + 2, P * u:P * u + P], b.x[:, u, :], k.ident[:])
                            last.then_inc(xt_done[d], 1)
                    for d, b in enumerate(D2):
                        pe.wait_ge(staged[d], at(step, q, 2, 2))
                        pe.wait_ge(xt_ok[d], at(step, q, NL, NL))
                        for u in range(4):
                            e, c = u // 2, u % 2
                            rows = slice(64 * e, 64 * e + 64)
                            out = k.psum[:, b.bank + e, 64 * c:64 * c + 64]
                            if step:
                                nc.tensor.matmul(out, b.ar[rows, c, 0, :], b.s0[rows, c, :], start=True, stop=False)
                            last = nc.tensor.matmul(out, b.ak[:, e, c, 0, :], b.v[:, c, e, :], start=step == 0, stop=True)
                        last.then_inc(r_done[d], 1)
                    if step < 2:
                        for d, b in enumerate(D2):
                            pe.wait_ge(khat_ok[d], at(step, q, 2, 2))
                            for g in range(2):
                                for c in range(2):
                                    last = nc.tensor.transpose(k.psum[:, b.bank + 3, P * (2 * g + c):P * (2 * g + c) + P],
                                                               b.kb[:, g, c, :], k.ident[:])
                            last.then_inc(kt_done[d], 1)
                    for d, b in enumerate(D2):
                        pe.wait_ge(r_ok[d], at(step, q, 1, 1))
                        for u in range(4):
                            last = nc.tensor.matmul(k.psum[:, b.bank + 2, 64 * u:64 * u + 64], b.xt[:, u, :], b.r[:, u, :],
                                                    start=True, stop=True)
                        last.then_inc(u_done[d], 1)
                    for d, b in enumerate(D2):
                        pe.wait_ge(u_ok[d], at(step, q, 1, 1))
                        if step < 2:
                            pe.wait_ge(kt_ok[d], at(step, q, 1, 1))
                            for u in range(4):
                                e, c = u // 2, u % 2
                                out = k.psum[64 * e:64 * e + 64, b.bank + 1, 64 * c:64 * c + 64]
                                kj, bj = (b.kt[:, g, c, 64 * e:64 * e + 64] for g in range(2))
                                if step == 0:
                                    nc.tensor.matmul(out, b.v[:, c, e, :], kj, start=True, stop=False)
                                    last = nc.tensor.matmul(out, b.u[:, u, :], bj, start=False, stop=True)
                                else:
                                    nc.tensor.matmul(out, kj, b.v[:, c, e, :], start=True, stop=False)
                                    last = nc.tensor.matmul(out, bj, b.u[:, u, :], start=False, stop=True)
                            last.then_inc(s_done[d], 1)
                    for d, b in enumerate(D2):
                        for u in range(4):
                            e, c = u // 2, u % 2
                            rows = slice(64 * e, 64 * e + 64)
                            out = k.psum[rows, b.bank + 3 * e, P * c:P * c + P]
                            nc.tensor.matmul(out, b.v[:, c, e, :], b.ak[:, e, c, 1, :], start=True, stop=False)
                            if step:
                                nc.tensor.matmul(out, b.s0[rows, c, :], b.ar[rows, c, 1, :], start=False, stop=False)
                            last = nc.tensor.matmul(out, b.u[:, u, :], b.ab[:, e, c, 1, :], start=False, stop=True)
                        last.then_inc(y_done[d], 1)

        @block.scalar
        def _(act):
            for step in range(3):
                with act.Fori(0, 4) as q:
                    for d, b in enumerate(D2):
                        n = TILE[step][d]
                        act.wait_ge(y_done[d], at(step, q, 1, 0))
                        inc, exc = (b.p[:, bass.ds(2 * q, 2), n, lo:lo + P] for lo in (1, 0))
                        ins = (exc, inc, inc) if d == 0 else (inc, exc, exc)
                        for dst, src, sign in zip((b.ar[:, :, 0, :], b.ar[:, :, 1, :], b.kb[:, 0, :, :]), ins, (-1, -1, 1)):
                            nc.scalar.activation(dst, src, ACT.Exp, scale=DECAY * (sign if d == 0 else -sign)).then_inc(exp_ok[d], 1)
                    for l in range(NL):
                        for d, b in enumerate(D2):
                            act.wait_ge(xt_done[d], at(step, q, NL, l + 1))
                            if l == 0:
                                nc.scalar.copy(b.xt, k.psum[:, b.bank + 2, :].rearrange("p (u t) -> p u t", u=4)).then_inc(xt_ok[d], 1)
                            else:
                                nc.scalar.copy(b.halves(b.xt, l)[:, :, :, 1 - d, :],
                                               b.halves(k.psum[:, b.bank + 2, :].rearrange("p (u t) -> p u t", u=4), l)[:, :, :, 1 - d, :]).then_inc(xt_ok[d], 1)
                    for d, b in enumerate(D2):
                        act.wait_ge(r_done[d], at(step, q, 1, 1))
                        nc.scalar.copy(b.r.rearrange("p (e c) n -> p e (c n)", e=2), k.psum[:, b.bank:b.bank + 2, 0:P]).then_inc(r_ok[d], 1)
                    if step < 2:
                        for d, b in enumerate(D2):
                            act.wait_ge(kt_done[d], at(step, q, 1, 1))
                            nc.scalar.copy(b.kt.rearrange("p g c f -> p (g c f)"), k.psum[:, b.bank + 3, :]).then_inc(kt_ok[d], 1)
                    for d, b in enumerate(D2):
                        act.wait_ge(u_done[d], at(step, q, 1, 1))
                        nc.scalar.copy(b.u.rearrange("p u n -> p (u n)"), k.psum[:, b.bank + 2, 0:256]).then_inc(u_ok[d], 1)
                    if step == 0:
                        for d, b in enumerate(D2):
                            act.wait_ge(s_done[d], at(step, q, 1, 1))
                            nc.scalar.copy(b.s.rearrange("p c n -> p (c n)"), k.psum[:, b.bank + 1, 0:P]).then_inc(s_copied[d], 1)

        @block.vector
        def _(dve):
            for b in D2:
                nc.vector.memset(b.ak[b.late, :, :, :, b.early], 0.0).then_inc(zero_ok, 1)
                nc.vector.memset(b.ab[b.late, :, :, :, b.early], 0.0).then_inc(zero_ok, 1)
            for step in range(3):
                with dve.Fori(0, 4) as q:
                    for d, b in enumerate(D2):
                        n = TILE[step][d]
                        toks = slice(P * n, P * n + P)
                        dve.wait_ge(y_done[d], at(step, q, 1, 0))
                        for c in range(2):
                            nc.vector.tensor_scalar(b.tmp[:, c, :], b.a[:, bass.ds(2 * q + c, 1), toks].squeeze(1),
                                                    k.vec[:, bass.ds(2 * q + (V_KA + c), 1)], k.omka[:, bass.ds(2 * q + c, 1)],
                                                    ALU.mult, ALU.add).then_inc(tmp_ok[d], 1)
                    for d, b in enumerate(D2):
                        n = TILE[step][d]
                        toks = slice(P * n, P * n + P)
                        dve.wait_ge(exp_ok[d], at(step, q, 3, 3))
                        nkk, r = (k.act3(i)[:, bass.ds(2 * q, 2), toks] for i in (S_NKK, S_R))
                        nc.vector.tensor_tensor(b.ar[:, :, 0, :], b.ar[:, :, 0, :], nkk, ALU.mult).then_inc(ar_ok[d], 1)
                        nc.vector.tensor_tensor(b.ar[:, :, 1, :], b.ar[:, :, 1, :], r, ALU.mult).then_inc(ar_ok[d], 1)
                        dve.wait_ge(rate_ok[d], at(step, q, 1, 1))
                        nc.vector.scalar_tensor_tensor(b.kb[:, 1, :, :], b.rate, -1.0, b.kb[:, 0, :, :], ALU.mult, ALU.mult).then_inc(kb_ok[d], 1)
                        dve.wait_ge(tmp_ok[d], at(step, q, 3, 2))
                        nc.vector.tensor_tensor(b.tmp, b.tmp, k.act3(S_K)[:, bass.ds(2 * q, 2), toks], ALU.mult).then_inc(tmp_ok[d], 1)
                        dve.wait_ge(tmp_ok[d], at(step, q, 3, 3))
                        dve.wait_ge(kb_ok[d], at(step, q, 2, 1))
                        nc.vector.tensor_tensor(b.kb[:, 0, :, :], b.kb[:, 0, :, :], b.tmp, ALU.mult).then_inc(kb_ok[d], 1)
                    for d, b in enumerate(D2):
                        for g, dst in enumerate((b.ak, b.ab)):
                            dve.wait_ge(a_done[d], at(step, q, 2, g + 1))
                            src = k.psum[:, b.bank + 2 * g:b.bank + 2 * g + 2, :].rearrange("p e (c g t) -> p (e c) g t", c=2, g=2)
                            dst = dst.rearrange("p e c g t -> p (e c) g t")
                            for part, cols in ((slice(0, P), b.late), (b.early, b.early)):
                                mask = k.causal[part, d, :, cols].unsqueeze(1).to_broadcast([part.stop - part.start, 4, 2, 64])
                                nc.vector.tensor_tensor(dst[part, :, :, cols], src[part, :, :, cols], mask, ALU.mult).then_inc(a_ok[d], 1)
                    for l in range(NL):
                        for d, b in enumerate(D2):
                            dve.wait_ge(t_done[d], at(step, q, NL, l + 1))
                            if l == 0 and step < 2:
                                dve.wait_ge(s_out[d], 32 * q if step == 0 else 128)
                            mask = k.level[:, d, l, :].unsqueeze(1).to_broadcast([P, 4, 64])
                            nc.vector.tensor_tensor(b.t1, k.psum[:, b.bank, 0:256].rearrange("p (u n) -> p u n", u=4), mask,
                                                    ALU.mult).then_inc(t_ok[d], 1)
                        for d, b in enumerate(D2):
                            early = b.halves(b.x, l)[:, :, :, d, :]
                            if l == 0:
                                dve.wait_ge(x_init[d], at(step, q, 1, 1))
                                dve.wait_ge(t_ok[d], at(step, q, NL, 1))
                                src = b.t1.rearrange("p u (b m) -> p u b m", m=1)
                            else:
                                dve.wait_ge(x_done[d], at(step, q, NL - 1, l))
                                dve.wait_ge(x_ok[d], at(step, q, NL, l))
                                src = k.psum[:, b.bank + 1, 0:256].rearrange("p (u b m) -> p u b m", u=4, m=1 << l)
                            nc.vector.tensor_tensor(early, early, src, ALU.add).then_inc(x_ok[d], 1)
                    if step == 1:
                        for d, b in enumerate(D2):
                            n, nxt = TILE[1][d], TILE[2][d]
                            w_end, w_mid = (w[:, bass.ds(2 * q, 2), i:i + 1].to_broadcast([P, 2, 64])
                                            for w, i in ((b.w_end, n), (b.w_mid, nxt)))
                            dve.wait_ge(s_done[d], at(1, q, 1, 1))
                            nc.vector.tensor_tensor(b.s, b.s0, w_end, ALU.mult).then_inc(s_step[d], 1)
                            dve.wait_ge(s_step[d], 2 * q + 1)
                            nc.vector.tensor_tensor(b.s, b.s, k.psum[:, b.bank + 1, 0:P].rearrange("p (c n) -> p c n", c=2),
                                                    ALU.add).then_inc(s_step[d], 1)
                            dve.wait_ge(s_step[d], 2 * q + 2)
                            nc.vector.tensor_tensor(k.s0t[:, d, bass.ds(2 * q, 2), :], b.s, w_mid, ALU.mult).then_inc(s_ok[d], 1)
                    for d, b in enumerate(D2):
                        n = TILE[step][d]
                        dve.wait_ge(y_done[d], at(step, q, 1, 1))
                        if step == 0 and d == 1:
                            dve.wait_ge(y_ok[0], at(step, q, 2, 2))
                        for e in range(2):
                            rows = slice(64 * e, 64 * e + 64)
                            y = k.act3(S_Y)[rows, bass.ds(2 * q, 2), P * n:P * n + P]
                            src = k.psum[rows, b.bank + 3 * e, 0:256].rearrange("p (c t) -> p c t", c=2)
                            if step == 1 or (step, d) == (0, 0):
                                nc.vector.tensor_copy(y, src).then_inc(y_ok[d], 1)
                            else:
                                nc.vector.tensor_tensor(y, y, src, ALU.add).then_inc(y_ok[d], 1)

        @block.gpsimd
        def _(pool):
            for step in range(3):
                with pool.Fori(0, 4) as q:
                    for d, b in enumerate(D2):
                        n = TILE[step][d]
                        toks = slice(P * n, P * n + P)
                        pool.wait_ge(y_done[d], at(step, q, 1, 0))
                        nkk = k.act3(S_NKK)[:, bass.ds(2 * q, 2), toks]
                        nc.gpsimd.tensor_tensor(b.rate, nkk, b.a[:, bass.ds(2 * q, 2), toks], ALU.mult).then_inc(rate_ok[d], 1)
                        nc.gpsimd.tensor_copy(b.x, k.ident[:].unsqueeze(1).to_broadcast([P, 4, P])).then_inc(x_init[d], 1)
                    for d, b in enumerate(D2):
                        n = TILE[step][d]
                        nc.gpsimd.tensor_copy(b.v.rearrange("p c e n -> p (c e n)"),
                                              k.tok3(S_V)[:, n, bass.ds(256 * q, 256)]).then_inc(staged[d], 1)
                        if step:
                            pool.wait_ge(s_ok[d], q if step == 1 else 4)
                        nc.gpsimd.tensor_copy(b.s0, k.s0t[:, d, bass.ds(2 * q, 2), :]).then_inc(staged[d], 1)
                    if step < 2:
                        for d, b in enumerate(D2):
                            n = TILE[step][d]
                            pool.wait_ge(a_done[d], at(step, q, 2, 2))
                            w_end = b.w_end[:, bass.ds(2 * q, 2), n:n + 1].to_broadcast([P, 2, P])
                            for g in range(2):
                                nc.gpsimd.tensor_tensor(b.kb[:, g, :, :], b.kb[:, g, :, :], w_end, ALU.mult).then_inc(khat_ok[d], 1)

        @block.sync
        def _(sp):
            new = k.a["new_state"][0, 0]
            with sp.Fori(0, 4) as q:
                for d, b in enumerate(D2):
                    sp.wait_ge(s_copied[d], q + 1)
                    dst = new[d][bass.ds(4 * q, 4)]
                    for e in range(2):
                        sp.dma_start(dst.rearrange("(c e) i j -> e i c j", e=2)[e], b.s[64 * e:64 * e + 64]).then_inc(s_out[d], 16)


def residual(k, dve, x, c, acc, gate_at, sem):
    for s, (t0, t1) in enumerate(((0, CTX), (CTX, T))):
        k.nc.vector.scalar_tensor_tensor(x[:, c, t0:t1], acc[:, t0:t1], k.mod[:, gate_at + c, s:s + 1], x[:, c, t0:t1],
                                         ALU.mult, ALU.add).then_inc(sem, 1)


def phase_rwkv_out(k):
    nc = k.nc
    first = k.taken
    k.taken += 9
    names = ("block_in", "cast_in", "x_in2", "rates_sum", "bonus_a", "bonus_b", "bonus_t", "mean_done", "less_mean", "y_squared",
             "var_done", "var_eps", "var_root", "rstd_ok", "bonus_done", "bonus_read", "vt_done", "bonus_ok", "rs_done", "y_scaled",
             "y_affine", "y_bonus", "g_done", "y_gated", "x_turned", "x_read", "o_done", "o_read", "omka2_ok")
    (block_in, cast_in, x_in, rates_sum, bonus_a, bonus_b, bonus_t, mean_done, less_mean, y_squared, var_done, var_eps, var_root,
     rstd_ok, bonus_done, bonus_read, vt_done, bonus_ok, rs_done, y_scaled, y_affine, y_bonus, g_done, y_gated, x_turned, x_read,
     o_done, o_read, omka2_ok) = (k.sem("post_" + n) for n in names)
    ones = k.ws[:, 0:P]
    cast = k.ws[0:H, 1160:1160 + D].rearrange("h (c p) -> h c p", c=DC)
    var, root, rstd = (k.ws[0:H, 2200 + T * i:2200 + T * i + T] for i in range(3))
    omka2 = k.ws[:, 130:138]
    y, sq, tb = k.act3(S_Y), k.act3(S_PF), k.act3(S_PB)
    af, ab, r3, k3, v3, xt, x = (k.act3(S_AF), k.act3(S_AB), k.act3(S_R), k.act3(S_K), k.tok3(S_V), k.tok3(S_NKK), k.act3(S_AB))

    @k.block()
    def _(block):
        @block.tensor
        def _(pe):
            pe.wait_ge(block_in, 16)
            for c in range(DC):
                if c >= 2:
                    pe.wait_ge(less_mean, c - 1)
                nc.tensor.matmul(k.psum[:, c % 2, 0:T], ones, y[:, c, :], start=True, stop=True).then_inc(mean_done, 1)
            for c in range(DC):
                pe.wait_ge(bonus_t, c + 1)
                if c >= 2:
                    pe.wait_ge(bonus_read, c - 1)
                nc.tensor.matmul(k.psum[:, 3 + c % 2, 0:T], ones, tb[:, c, :], start=True, stop=True).then_inc(bonus_done, 1)
            for c in range(DC):
                if c >= 2:
                    pe.wait_ge(bonus_ok, c - 1)
                for n in range(NT):
                    last = nc.tensor.transpose(k.psum[:, 5 + c % 2, P * n:P * n + P], v3[:, n, P * c:P * c + P], k.ident[:])
                last.then_inc(vt_done, 1)
            for c in range(DC):
                pe.wait_ge(y_squared, c + 1)
                last = nc.tensor.matmul(k.psum[0:H, 2, 0:T], k.headsum[:, c, :], sq[:, c, :], start=c == 0, stop=c == DC - 1)
            last.then_inc(var_done, 1)
            pe.wait_ge(x_in, 32)
            for c in range(DC):
                if c >= 2:
                    pe.wait_ge(x_read, c - 1)
                else:
                    pe.wait_ge(bonus_read, 8)
                for n in range(NT):
                    last = nc.tensor.transpose(k.psum[:, 3 + c % 2, P * n:P * n + P], xt[:, n, P * c:P * c + P], k.ident[:])
                last.then_inc(x_turned, 1)
            pe.wait_ge(rstd_ok, 1)
            pe.wait_ge(cast_in, 16)
            g2 = take_piece(k, pe, first)
            for c in range(DC):
                if c >= 2:
                    pe.wait_ge(y_scaled, c - 1)
                else:
                    pe.wait_ge(less_mean, 8)
                nc.tensor.matmul(k.psum[:, c % 2, 0:T], cast[:, c, :], rstd, start=True, stop=True).then_inc(rs_done, 1)
                if c >= 2:
                    pe.wait_ge(y_gated, c - 1)
                nc.tensor.matmul(k.psum[:, (7, 2)[c % 2], 0:T], g2[:, P * c:P * c + P], k.sgate[:], start=True, stop=True).then_inc(g_done, 1)
            k.used[first] = (g_done, 8)
            for o in range(DC):
                if o % 2 == 0:
                    w = piece_cols(take_piece(k, pe, first + 1 + o // 2))
                if o < 2:
                    pe.wait_ge(bonus_ok, 8)
                else:
                    pe.wait_ge(o_read, 2 * (o - 1))
                for c in range(DC):
                    pe.wait_ge(y_gated, c + 1)
                    last = nc.tensor.matmul(k.psum[:, 5 + o % 2, 0:T], w[:, c, P * (o % 2):P * (o % 2) + P], y[:, c, :],
                                            start=c == 0, stop=c == DC - 1)
                last.then_inc(o_done, 1)
                k.used[first + 1 + o // 2] = (o_done, o + 1)

        @block.sync
        def _(sp):
            load_tokens(k, sp, xt, x_in)
            sp.dma_start(ones, k.a["c_block"]).then_inc(block_in, 16)
            sp.dma_start(k.ws[0:H, 1160:1160 + D], k.a["c_headcast"]).then_inc(cast_in, 16)
            prefetch(k, sp, first, first + 9)

        @block.gpsimd
        def _(pool):
            for g in range(4):
                nc.gpsimd.tensor_tensor(tb[:, 2 * g:2 * g + 2, :], af[:, 2 * g:2 * g + 2, :], ab[:, 2 * g:2 * g + 2, :], ALU.add).then_inc(rates_sum, 1)

        @block.scalar
        def _(act):
            for c in range(DC):
                act.wait_ge(less_mean, c + 1)
                nc.scalar.activation(sq[:, c, :], y[:, c, :], ACT.Square).then_inc(y_squared, 1)
                act.wait_ge(bonus_done, c + 1)
                act.wait_ge(rates_sum, 4)
                nc.scalar.copy(af[:, c, :], k.psum[:, 3 + c % 2, 0:T]).then_inc(bonus_read, 1)
            act.wait_ge(var_eps, 1)
            nc.scalar.activation(root, var, ACT.Sqrt).then_inc(var_root, 1)
            for c in range(DC):
                act.wait_ge(x_turned, c + 1)
                nc.scalar.copy(x[:, c, :], k.psum[:, 3 + c % 2, 0:T]).then_inc(x_read, 1)
            for c in range(DC):
                act.wait_ge(y_scaled, c + 1)
                nc.scalar.activation(y[:, c, :], y[:, c, :], ACT.Identity, bias=k.vec[:, V_LB + c:V_LB + c + 1],
                                     scale=k.vec[:, V_LG + c:V_LG + c + 1]).then_inc(y_affine, 1)

        @block.vector
        def _(dve):
            nc.vector.tensor_scalar(omka2, k.omka[:], 2.0, None, ALU.mult).then_inc(omka2_ok, 1)
            dve.wait_ge(omka2_ok, 1)
            for c in range(DC):
                dve.wait_ge(mean_done, c + 1)
                nc.vector.scalar_tensor_tensor(y[:, c, :], k.psum[:, c % 2, 0:T], -1.0 / HD, y[:, c, :], ALU.mult, ALU.add).then_inc(less_mean, 1)
                dve.wait_ge(rates_sum, c // 2 + 1)
                nc.vector.tensor_scalar(tb[:, c, :], tb[:, c, :], k.vec[:, V_KA + c:V_KA + c + 1], omka2[:, c:c + 1],
                                        ALU.mult, ALU.add).then_inc(bonus_a, 1)
                dve.wait_ge(bonus_a, c + 1)
                nc.vector.tensor_tensor(tb[:, c, :], tb[:, c, :], k3[:, c, :], ALU.mult).then_inc(bonus_b, 1)
                dve.wait_ge(bonus_b, c + 1)
                nc.vector.scalar_tensor_tensor(tb[:, c, :], r3[:, c, :], k.vec[:, V_RK + c:V_RK + c + 1], tb[:, c, :],
                                               ALU.mult, ALU.mult).then_inc(bonus_t, 1)
            for c in range(DC):
                dve.wait_ge(vt_done, c + 1)
                dve.wait_ge(bonus_read, c + 1)
                nc.vector.tensor_tensor(af[:, c, :], af[:, c, :], k.psum[:, 5 + c % 2, 0:T], ALU.mult).then_inc(bonus_ok, 1)
            dve.wait_ge(var_done, 1)
            nc.vector.tensor_scalar(var, k.psum[0:H, 2, 0:T], 1.0 / HD, GN_EPS, ALU.mult, ALU.add).then_inc(var_eps, 1)
            dve.wait_ge(var_root, 1)
            nc.vector.reciprocal(rstd, root).then_inc(rstd_ok, 1)
            for c in range(DC + 1):
                if c < DC:
                    dve.wait_ge(rs_done, c + 1)
                    nc.vector.tensor_tensor(y[:, c, :], y[:, c, :], k.psum[:, c % 2, 0:T], ALU.mult).then_inc(y_scaled, 1)
                if c:
                    b = c - 1
                    dve.wait_ge(y_affine, b + 1)
                    nc.vector.tensor_tensor(y[:, b, :], y[:, b, :], af[:, b, :], ALU.add).then_inc(y_bonus, 1)
                    dve.wait_ge(g_done, b + 1)
                    dve.wait_ge(y_bonus, b + 1)
                    nc.vector.tensor_tensor(y[:, b, :], y[:, b, :], k.psum[:, (7, 2)[b % 2], 0:T], ALU.mult).then_inc(y_gated, 1)
            dve.wait_ge(x_read, 8)
            for o in range(DC):
                dve.wait_ge(o_done, o + 1)
                residual(k, dve, x, o, k.psum[:, 5 + o % 2, 0:T], 16, o_read)


def phase_router(k, layer, h_slab):
    nc, a = k.nc, k.a
    names = ("w_in", "b_in", "logit_done", "step", "exps", "rows_turned", "rows_read", "rows_out", "chosen", "ranked",
             "placed", "listed")
    w_in, b_in, logit_done, step, exps, rows_turned, rows_read, rows_out, chosen, ranked, placed, listed = (
        k.sem(f"router{layer}_{n}") for n in names)
    h, rows = k.act3(h_slab), k.tok3(S_R)
    w = k.ws[:, 0:DC * 20].rearrange("p (c n) -> p c n", c=DC)
    bias, order = k.ws[:, 160:180], k.ws[:, 180:192].rearrange("p (n j) -> p n j", n=NT)
    count = k.ws[:, 1024:1024 + P]
    token = k.ws[:, 1024 + P:1024 + P + NT]
    at = [192]

    def buf(*shape):
        n = int(np.prod(shape))
        v = k.ws[:, at[0]:at[0] + n]
        at[0] += n
        names = "abc"[:len(shape)]
        return v if len(shape) == 1 else v.rearrange(f"p ({' '.join(names)}) -> p {' '.join(names)}",
                                                     **dict(zip(names, shape)))

    lg, gmax, rel, gexp, gsum, one_g, top = buf(NT, 20), buf(NT), buf(NT, 4), buf(NT, 4), buf(NT), buf(NT, 4), buf(NT)
    sel, le, m1, d1, one1, d2, m2, one2, e2 = (buf(NT, 4, 4), buf(NT, 4), buf(NT), buf(NT, 4), buf(NT, 4), buf(NT, 4),
                                               buf(NT), buf(NT, 4), buf(NT))
    den, t4 = buf(NT), buf(NT, 4)
    at[0] = 1200
    pick = buf(2, NT, NE)
    rank, high, blk, pos, part = (buf(NT, NE) for _ in range(5))
    over, over_sum, over_at, flags = buf(NE), buf(NE), buf(NE), buf(OVER, NE)
    found, slot_f, blk_f, pos_f = buf(OVER), buf(2, NT), buf(2, NT), buf(2, NT)
    in_pos, in_blk = buf(2 * NT, P), buf(2 * NT, BLOCKS)
    both, ones = k.ones16[:, P:P + NT * NE], k.ones16[:, 0:P]
    weight = k.ws[:, WEIGHT_AT:WEIGHT_AT + 2 * NT].rearrange("p (k n) -> p k n", k=2)

    def wide(v, n=4):
        return v.unsqueeze(2).to_broadcast([P, NT, n])

    @k.block()
    def _(block):
        @block.sync
        def _(sp):
            for n, lo, hi in (("grp", 0, 4), ("exp", 4, 20)):
                sp.dma_start(w[:, :, lo:hi], a["moe_w_" + n][layer].rearrange("(c p) n -> p c n", p=P)).then_inc(w_in, 16)
                sp.dma_start(bias[:, lo:hi], a["moe_b_" + n][layer].partition_broadcast(P)).then_inc(b_in, 16)
            sp.dma_start(k.ws[:, 180:192], a["c_order"]).then_inc(b_in, 16)
            sp.dma_start(k.ws[:, 1024:1024 + P + NT], a["c_count"]).then_inc(b_in, 16)
            for n in range(NT):
                sp.wait_ge(rows_read, 2 * n + 2)
                sp.dma_start(a["h_rows"][P * n:P * n + P, :], rows[:, n, :]).then_inc(rows_out, 16)
            sp.wait_ge(rows_out, 16 * NT)

        @block.tensor
        def _(pe):
            pe.wait_ge(w_in, 32)
            for n in range(NT):
                for c in range(DC):
                    last = nc.tensor.matmul(k.psum[:, n, 0:20], h[:, c, P * n:P * n + P], w[:, c, :], start=c == 0, stop=c == DC - 1)
            last.then_inc(logit_done, 1)
            for n in range(NT):
                for g in range(2):
                    i = 2 * n + g
                    if i >= 4:
                        pe.wait_ge(rows_read, i - 3)
                    for c in range(4):
                        last = nc.tensor.transpose(k.psum[:, 3 + i % 4, P * c:P * c + P], h[:, 4 * g + c, P * n:P * n + P], k.ident[:])
                    last.then_inc(rows_turned, 1)
            pe.wait_ge(chosen, 2)
            for n in range(NT):
                for m in range(n + 1):
                    nc.tensor.matmul(k.psum[:, 7, NE * n:NE * n + NE], k.causal[:, 0, 0, :] if m == n else ones,
                                     both[:, NE * m:NE * m + NE], start=m == 0, stop=m == n)
            for m in range(NT):
                last = nc.tensor.matmul(k.psum[:, 7, 3 * NE:4 * NE], ones, both[:, NE * m:NE * m + NE], start=m == 0, stop=m == NT - 1)
            last.then_inc(ranked, 1)
            pe.wait_ge(placed, 2)
            for i in range(2 * NT):
                last = nc.tensor.matmul(k.psum[:, 0, 0:BLOCKS], in_pos[:, i, :], in_blk[:, i, :], start=i == 0, stop=i == 2 * NT - 1)
            last.then_inc(listed, 1)

        @block.scalar
        def _(act):
            for i in range(2 * NT):
                act.wait_ge(rows_turned, i + 1)
                nc.scalar.copy(rows[:, i // 2, 512 * (i % 2):512 * (i % 2) + 512], k.psum[:, 3 + i % 4, :]).then_inc(rows_read, 1)
            act.wait_ge(step, 3)
            nc.scalar.activation(gexp, rel, ACT.Exp).then_inc(exps, 1)
            act.wait_ge(step, SECOND)
            nc.scalar.activation(e2, m2, ACT.Exp).then_inc(exps, 1)

        @block.gpsimd
        def _(pool):
            nc.gpsimd.memset(ones, 1.0).then_inc(chosen, 1)

        @block.vector
        def _(dve):
            n = [0]

            def then(ins):
                n[0] += 1
                ins.then_inc(step, 1)
                dve.wait_ge(step, n[0])

            def first_of(dst, flags):
                then(nc.vector.tensor_tensor(t4, flags, order, ALU.mult))
                then(nc.vector.tensor_reduce(top, t4, AX.X, ALU.max))
                then(nc.vector.tensor_tensor(dst, t4, wide(top), ALU.is_equal))

            dve.wait_ge(logit_done, 1)
            dve.wait_ge(b_in, 64)
            then(nc.vector.tensor_tensor(lg, k.psum[:, 0:NT, 0:20], bias.unsqueeze(1).to_broadcast([P, NT, 20]), ALU.add))
            then(nc.vector.tensor_reduce(gmax, lg[:, :, 0:4], AX.X, ALU.max))
            then(nc.vector.tensor_tensor(rel, lg[:, :, 0:4], wide(gmax), ALU.subtract))
            then(nc.vector.tensor_scalar(d1, rel, 0.0, None, ALU.is_ge))
            first_of(one_g, d1)
            then(nc.vector.tensor_tensor(sel, lg[:, :, 4:20].rearrange("p n (g j) -> p n g j", g=4),
                                         one_g.unsqueeze(3).to_broadcast([P, NT, 4, 4]), ALU.mult))
            then(nc.vector.tensor_reduce(le, sel.rearrange("p n g j -> p n j g"), AX.X, ALU.add))
            then(nc.vector.tensor_reduce(m1, le, AX.X, ALU.max))
            then(nc.vector.tensor_tensor(d1, le, wide(m1), ALU.subtract))
            then(nc.vector.tensor_scalar(d2, d1, 0.0, None, ALU.is_ge))
            first_of(one1, d2)
            then(nc.vector.scalar_tensor_tensor(d2, one1, -BIG, d1, ALU.mult, ALU.add))
            then(nc.vector.tensor_reduce(m2, d2, AX.X, ALU.max))
            assert n[0] == SECOND
            then(nc.vector.tensor_tensor(d1, d2, wide(m2), ALU.is_ge))
            first_of(one2, d1)
            for i, one in enumerate((one1, one2)):
                then(nc.vector.tensor_tensor(pick[:, i].rearrange("p n (g j) -> p n g j", g=NG),
                                             one_g.unsqueeze(3).to_broadcast([P, NT, 4, 4]),
                                             one.unsqueeze(2).to_broadcast([P, NT, 4, 4]), ALU.mult))
            nc.vector.tensor_tensor(both.rearrange("p (n e) -> p n e", n=NT), pick[:, 0], pick[:, 1], ALU.add).then_inc(chosen, 1)
            dve.wait_ge(exps, 2)
            then(nc.vector.tensor_reduce(gsum, gexp, AX.X, ALU.add))
            then(nc.vector.scalar_tensor_tensor(den, e2, 1.0, gsum, ALU.add, ALU.mult))
            then(nc.vector.reciprocal(weight[:, 0], den))
            then(nc.vector.tensor_tensor(weight[:, 1], weight[:, 0], e2, ALU.mult))
            dve.wait_ge(ranked, 1)
            total = k.psum[:, 7, 3 * NE:4 * NE]
            then(nc.vector.tensor_scalar(over, total, float(P) + 0.5, None, ALU.is_ge))
            then(nc.vector.tensor_scalar(over_at, total, 2.0 * P + 0.5, None, ALU.is_ge))
            then(nc.vector.tensor_tensor(over, over, over_at, ALU.add))
            then(nc.vector.tensor_tensor_scan(over_sum, over, over, 0.0, ALU.add, ALU.max))
            then(nc.vector.tensor_tensor(over_at, over_sum, over, ALU.subtract))
            then(nc.vector.tensor_tensor(flags, count[:, 0:OVER].unsqueeze(2).to_broadcast([P, OVER, NE]),
                                         over_at.unsqueeze(1).to_broadcast([P, OVER, NE]), ALU.is_ge))
            then(nc.vector.tensor_reduce(found, flags, AX.X, ALU.add))
            then(nc.vector.tensor_scalar(k.overflow_expert[:], found, -1.0, None, ALU.add))
            then(nc.vector.tensor_copy(rank, k.psum[:, 7, 0:NT * NE].rearrange("p (n e) -> p n e", n=NT)))
            then(nc.vector.tensor_scalar(part, rank, float(P), None, ALU.is_ge))
            then(nc.vector.tensor_scalar(high, rank, 2.0 * P, None, ALU.is_ge))
            then(nc.vector.tensor_tensor(high, high, part, ALU.add))
            then(nc.vector.scalar_tensor_tensor(pos, high, -float(P), rank, ALU.mult, ALU.add))
            then(nc.vector.tensor_scalar(over_sum, over_at, NE - 1.0, None, ALU.add))
            then(nc.vector.tensor_tensor(over_sum, over_sum, count[:, 0:NE], ALU.subtract))
            then(nc.vector.tensor_tensor(blk, high, over_sum.unsqueeze(1).to_broadcast([P, NT, NE]), ALU.add))
            then(nc.vector.tensor_tensor(blk, blk, part, ALU.mult))
            then(nc.vector.tensor_tensor(blk, blk, count[:, 0:NE].unsqueeze(1).to_broadcast([P, NT, NE]), ALU.add))
            for src, dst in ((pos, pos_f), (blk, blk_f)):
                for i in range(2):
                    then(nc.vector.tensor_tensor(part, pick[:, i], src, ALU.mult))
                    then(nc.vector.tensor_reduce(dst[:, i], part, AX.X, ALU.add))
            pf, bf = pos_f.rearrange("p k n -> p (k n)"), blk_f.rearrange("p k n -> p (k n)")
            then(nc.vector.tensor_tensor(in_blk, count[:, 0:BLOCKS].unsqueeze(1).to_broadcast([P, 2 * NT, BLOCKS]),
                                         bf.unsqueeze(2).to_broadcast([P, 2 * NT, BLOCKS]), ALU.is_equal))
            for i in range(2):
                both_n = in_blk[:, NT * i:NT * i + NT, :]
                ins = nc.vector.tensor_tensor(both_n, both_n, token.unsqueeze(2).to_broadcast([P, NT, BLOCKS]), ALU.mult)
                if i:
                    ins.then_inc(placed, 1)
                else:
                    then(ins)
            nc.vector.tensor_tensor(in_pos, count.unsqueeze(1).to_broadcast([P, 2 * NT, P]),
                                    pf.unsqueeze(2).to_broadcast([P, 2 * NT, P]), ALU.is_equal).then_inc(placed, 1)
            then(nc.vector.scalar_tensor_tensor(slot_f.rearrange("p k n -> p (k n)"), bf, float(P), pf, ALU.mult, ALU.add))
            then(nc.vector.tensor_copy(k.slots[:], slot_f.rearrange("p k n -> p (k n)")))
            dve.wait_ge(listed, 1)
            then(nc.vector.tensor_copy(k.block_tokens[:], k.psum[:, 0, 0:BLOCKS]))


SECOND = 17
WEIGHT_AT = 1184


def phase_moe(k, layer):
    nc, a = k.nc, k.a
    first = k.taken
    k.taken += 66
    names = ("gathered0", "gathered1", "y_out0", "y_out1", "turned", "turn_read", "h_done", "silu_ok", "hid_ok", "y_done", "y_half0", "y_half1")
    gathered0, gathered1, y_out0, y_out1, turned, turn_read, h_done, silu_ok, hid_ok, y_done, y_half0, y_half1 = (
        k.sem(f"moe{layer}_{n}") for n in names)
    gathered, y_out = (gathered0, gathered1), (y_out0, y_out1)
    rows = [k.slab[:, S_R, D * i:D * i + D] for i in range(2)]
    cols_ = [k.slab[:, S_PF, D * i:D * i + D].rearrange("p (c s) -> p c s", c=DC) for i in range(2)]
    ys = [k.slab[:, S_PB, D * i:D * i + D] for i in range(2)]
    silu = [k.ws[:, 2048 + 256 * i:2304 + 256 * i].rearrange("p (f s) -> p f s", f=2) for i in range(2)]
    hid = [k.ws[:, 3072 + 256 * i:3328 + 256 * i].rearrange("p (f s) -> p f s", f=2) for i in range(2)]

    def w1_at(b):
        return 3 * b - 1 if b else 0

    def w3_at(b):
        return 3 * b if b else 1

    def w2_at(b):
        return 3 * b + 4 if b < BLOCKS - 1 else 3 * BLOCKS - 1

    LOOPS = (BLOCKS - 3) // 2

    @k.block()
    def _(block):
        @block.tensor
        def _(pe):
            def arrived(i, place):
                pe.wait_ge(k.ring_in[place % NS], i * 16 + k.arrival[first + place])
                return k.ring[:, place % NS, :]

            def turn(i, b):
                pe.wait_ge(gathered[b % 2], 16 * i + 16 * (b // 2 + 1))
                if b:
                    pe.wait_ge(turn_read, 4 * i + 2 * b)
                for c in range(DC):
                    last = nc.tensor.transpose(k.psum[:, c // 4, P * (c % 4):P * (c % 4) + P],
                                               rows[b % 2][:, P * c:P * c + P], k.ident[:])
                last.then_inc(turned, 1)

            def inner(i, b):
                w1, w3 = piece_cols(arrived(i, w1_at(b))), piece_cols(arrived(i, w3_at(b)))
                pe.wait_ge(turn_read, 4 * i + (2 * b + 2))
                if b >= 2:
                    pe.wait_ge(hid_ok, 2 * i + (b - 1))
                for j, w in enumerate((w1, w3)):
                    for f in range(2):
                        for c in range(DC):
                            last = nc.tensor.matmul(k.psum[:, 2 + b % 2, P * (2 * j + f):P * (2 * j + f) + P],
                                                    w[:, c, P * f:P * f + P], cols_[b % 2][:, c, :], start=c == 0, stop=c == DC - 1)
                last.then_inc(h_done, 1)

            def outer(i, b):
                w2 = arrived(i, w2_at(b)).rearrange("p (f n) -> p f n", f=2)
                pe.wait_ge(hid_ok, 2 * i + (b + 1))
                if b >= 2:
                    pe.wait_ge(y_half0, 2 * i + (b - 1))
                    pe.wait_ge(y_half1, 2 * i + (b - 1))
                for half in range(2):
                    for f in range(2):
                        last = nc.tensor.matmul(k.psum[:, 4 + 2 * (b % 2) + half, :], hid[b % 2][:, f, :],
                                                w2[:, f, 512 * half:512 * half + 512], start=f == 0, stop=f == 1)
                last.then_inc(y_done, 1)

            turn(0, 0)
            inner(0, 0)
            turn(0, 1)
            inner(0, 1)
            turn(0, 2)
            outer(0, 0)
            with pe.Fori(0, LOOPS) as i:
                inner(i, 2)
                turn(i, 3)
                outer(i, 1)
                inner(i, 3)
                turn(i, 4)
                outer(i, 2)
            inner(0, BLOCKS - 1)
            outer(0, BLOCKS - 2)
            outer(0, BLOCKS - 1)
            for b in range(BLOCKS):
                k.used[first + w1_at(b)] = k.used[first + w3_at(b)] = (h_done, b + 1)
                k.used[first + w2_at(b)] = (y_done, b + 1)

        @block.sync
        def _(sp):
            k.overflow = [sp.value_load(k.overflow_expert[0:1, j:j + 1], min_val=0, max_val=NE - 1) for j in range(OVER)]
            body = [(6, "moe_w3", 2, [(h_done, 1)]), (7, "moe_w2", 1, [(h_done, 1), (y_done, 0)]),
                    (8, "moe_w1", 3, [(h_done, 2)]), (9, "moe_w3", 3, [(h_done, 2)]),
                    (10, "moe_w2", 2, [(y_done, 1)]), (11, "moe_w1", 4, [(h_done, 3)])]
            with sp.Fori(0, 6) as i:
                for place, name, e, waits in body:
                    sp.wait_ge(h_done, 1)
                    for sem, value in waits:
                        sp.wait_ge(sem, i * 2 + value)
                    src = a[name][layer][bass.ds(2 * i + e, 1)].rearrange("e r n -> (e r) n").rearrange("(c p) n -> p c n", p=P)
                    dst = k.ring[:, place % NS, :].rearrange("p (c n) -> p c n", c=2 if name == "moe_w2" else DC)
                    sp.dma_start(dst, src).then_inc(k.ring_in[place % NS], 16)
            prefetch(k, sp, first + 36, first + 66)

        @block.gpsimd
        def _(pool):
            def put(b):
                pool.wait_ge(y_half0, b + 1)
                pool.wait_ge(y_half1, b + 1)
                pool.dma_start(a["y_rows"][P * b:P * b + P, :], ys[b % 2]).then_inc(y_out[b % 2], 16)

            for b in range(BLOCKS):
                if b >= 2:
                    pool.wait_ge(turned, b - 1)
                nc.gpsimd.indirect_dma_start(rows[b % 2], None, a["h_rows"],
                                             bass.IndirectOffsetOnAxis(ap=k.block_tokens[:, b:b + 1], axis=0)).then_inc(gathered[b % 2], 16)
                if b >= 2:
                    put(b - 2)
            put(BLOCKS - 2)
            put(BLOCKS - 1)
            pool.wait_ge(y_out0, 16 * ((BLOCKS + 1) // 2))
            pool.wait_ge(y_out1, 16 * (BLOCKS // 2))

        @block.scalar
        def _(act):
            def turn_out(i, b):
                act.wait_ge(turned, 2 * i + (b + 1))
                if b >= 2:
                    act.wait_ge(h_done, 2 * i + (b - 1))
                for g in range(2):
                    nc.scalar.copy(cols_[b % 2][:, 4 * g:4 * g + 4, :], k.psum[:, g, :].rearrange("p (c s) -> p c s", c=4)).then_inc(turn_read, 1)

            def gate(i, b):
                act.wait_ge(h_done, 2 * i + (b + 1))
                if b >= 2:
                    act.wait_ge(hid_ok, 2 * i + (b - 1))
                nc.scalar.activation(silu[b % 2], k.psum[:, 2 + b % 2, 0:2 * P].rearrange("p (f s) -> p f s", f=2),
                                     ACT.Silu).then_inc(silu_ok, 1)

            def store(i, b):
                act.wait_ge(y_done, 2 * i + (b + 1))
                if b >= 2:
                    act.wait_ge(y_out[b % 2], 16 * i + 16 * (b // 2))
                nc.scalar.copy(ys[b % 2][:, 0:512], k.psum[:, 4 + 2 * (b % 2), :]).then_inc(y_half0, 1)

            turn_out(0, 0)
            gate(0, 0)
            turn_out(0, 1)
            gate(0, 1)
            turn_out(0, 2)
            store(0, 0)
            with act.Fori(0, LOOPS) as i:
                gate(i, 2)
                turn_out(i, 3)
                store(i, 1)
                gate(i, 3)
                turn_out(i, 4)
                store(i, 2)
            gate(0, BLOCKS - 1)
            store(0, BLOCKS - 2)
            store(0, BLOCKS - 1)

        @block.vector
        def _(dve):
            def hidden(i, b):
                dve.wait_ge(silu_ok, 2 * i + (b + 1))
                if b >= 2:
                    dve.wait_ge(y_done, 2 * i + (b - 1))
                nc.vector.tensor_tensor(hid[b % 2], silu[b % 2], k.psum[:, 2 + b % 2, 2 * P:4 * P].rearrange("p (f s) -> p f s", f=2),
                                        ALU.mult).then_inc(hid_ok, 1)

            def store(i, b):
                dve.wait_ge(y_done, 2 * i + (b + 1))
                if b >= 2:
                    dve.wait_ge(y_out[b % 2], 16 * i + 16 * (b // 2))
                nc.vector.tensor_copy(ys[b % 2][:, 512:D], k.psum[:, 5 + 2 * (b % 2), :]).then_inc(y_half1, 1)

            hidden(0, 0)
            hidden(0, 1)
            store(0, 0)
            with dve.Fori(0, LOOPS) as i:
                hidden(i, 2)
                store(i, 1)
                hidden(i, 3)
                store(i, 2)
            hidden(0, BLOCKS - 1)
            store(0, BLOCKS - 2)
            store(0, BLOCKS - 1)


def phase_moe_out(k, layer, x_slab):
    nc, a = k.nc, k.a
    fetched = [k.sem(f"moe{layer}_fetched{n}") for n in range(NT)]
    weighed, summed, y_turned, x_added = (k.sem(f"moe{layer}_{n}") for n in ("weighed", "summed", "y_turned", "x_added"))
    got = [k.tok3(S_R), k.tok3(S_PF)]
    x = k.act3(x_slab)
    weight = k.ws[:, WEIGHT_AT:WEIGHT_AT + 2 * NT].rearrange("p (k n) -> p k n", k=2)

    @k.block()
    def _(block):
        @block.gpsimd
        def _(pool):
            for n in range(NT):
                for i in range(2):
                    nc.gpsimd.indirect_dma_start(got[i][:, n, :], None, a["y_rows"],
                                                 bass.IndirectOffsetOnAxis(ap=k.slots[:, NT * i + n:NT * i + n + 1], axis=0)).then_inc(fetched[n], 16)

        @block.tensor
        def _(pe):
            for n in range(NT):
                pe.wait_ge(summed, n + 1)
                for c in range(DC):
                    last = nc.tensor.transpose(k.psum[:, c, P * n:P * n + P], got[1][:, n, P * c:P * c + P], k.ident[:])
                    if n == NT - 1:
                        last.then_inc(y_turned, 1)

        @block.vector
        def _(dve):
            for n in range(NT):
                dve.wait_ge(fetched[n], 32)
                nc.vector.tensor_scalar(got[0][:, n, :], got[0][:, n, :], weight[:, 0, n:n + 1], None, ALU.mult).then_inc(weighed, 1)
                dve.wait_ge(weighed, n + 1)
                nc.vector.scalar_tensor_tensor(got[1][:, n, :], got[1][:, n, :], weight[:, 1, n:n + 1], got[0][:, n, :],
                                               ALU.mult, ALU.add).then_inc(summed, 1)
            for c in range(DC):
                dve.wait_ge(y_turned, c + 1)
                residual(k, dve, x, c, k.psum[:, c, 0:T], 40, x_added)


def phase_qkv(k):
    nc, a = k.nc, k.a
    first = k.taken
    k.taken += 12
    proj, read_out, kt_done, kt_ok, stored = (k.sem("qkv_" + n) for n in ("done", "read", "kt_done", "kt_ok", "stored"))
    padded, rpb_in, pad_out, cap_in, bias_in, capped = (
        k.sem("bias_" + n) for n in ("padded", "rpb_in", "pad_out", "cap_in", "in", "capped"))
    q_lat = k.sem("q_lat_ok")
    ctx_in, kc_done, kc_ok = (k.sem("ctx_" + n) for n in ("in", "kc_done", "kc_ok"))
    h, q3, k3, v3 = k.act3(S_Y), k.act3(S_PF), k.act3(S_PB), k.tok3(S_V)
    new_k = k.ws[:, 0:D]
    pad = k.ws[0:H, 1024:1024 + 15 * P].rearrange("h (r n) -> h r n", r=15)
    cap = k.ws[:, 3000:3064]
    MID = GRID - WIN_C
    slabs = k.slab[:, S_R:S_K + 1, :].rearrange("p s n -> p (s n)")
    bias = slabs[:, 0:H * 6 * GRID].rearrange("p (h e n) -> p h e n", h=H, e=6)
    k_tok, v_tok = k.slab[:, S_NKK, 0:D], k.slab[:, S_NKK, D:2 * D]
    kc = k.slab[:, S_NKK, 2 * D:3 * D].rearrange("p (c t) -> p c t", c=DC)

    def bank(o):
        return k.psum[:, o % 6, :]

    @k.block()
    def _(block):
        @block.tensor
        def _(pe):
            o = 0
            for j in range(12):
                w = piece_cols(take_piece(k, pe, first + j))
                for m in range(2 if j < 8 else NT):
                    if o >= 6:
                        pe.wait_ge(read_out, o - 5)
                    for c in range(DC):
                        if j < 8:
                            last = nc.tensor.matmul(bank(o)[:, 0:T], w[:, c, P * m:P * m + P], h[:, c, :], start=c == 0, stop=c == DC - 1)
                        else:
                            last = nc.tensor.matmul(bank(o)[:, 0:256], h[:, c, P * m:P * m + P], w[:, c, :], start=c == 0, stop=c == DC - 1)
                    last.then_inc(proj, 1)
                    o += 1
                k.used[first + j] = (proj, o)
                if j == 8:
                    pe.wait_ge(read_out, 16)
                    for c in range(DC):
                        last = nc.tensor.transpose(k.psum[:, 6 + c // 4, P * (c % 4):P * (c % 4) + P], k3[:, c, 0:CTX], k.ident[:])
                    last.then_inc(kt_done, 1)
            pe.wait_ge(kt_ok, 1)
            pe.wait_ge(ctx_in, 32)
            for c in range(DC):
                last = nc.tensor.transpose(k.psum[:, 6 + c // 4, P * (c % 4):P * (c % 4) + P], k_tok[:, P * c:P * c + P], k.ident[:])
            last.then_inc(kc_done, 1)

        @block.sync
        def _(sp):
            sp.dma_start(k_tok, a["cache_na_k"][0, 0].rearrange("t h d -> t (h d)")).then_inc(ctx_in, 16)
            sp.dma_start(v_tok, a["cache_na_v"][0, 0].rearrange("t h d -> t (h d)")).then_inc(ctx_in, 16)
            prefetch(k, sp, first, first + 12)
            sp.wait_ge(kt_ok, 1)
            sp.dma_start(a["new_k"][0, 0].rearrange("t h d -> t (h d)"), new_k).then_inc(stored, 16)
            sp.wait_ge(read_out, 28)
            sp.dma_start(a["new_v"][0, 0].rearrange("t h d -> t (h d)"), v3[:, 0, :]).then_inc(stored, 16)
            sp.wait_ge(stored, 32)

        @block.scalar
        def _(act):
            act.wait_ge(padded, 1)
            act.dma_start(pad[:, :, MID:MID + 31], a["na_rpb"][0]).then_inc(rpb_in, 16)
            act.wait_ge(rpb_in, 16)
            act.dma_start(a["scratch"], pad).then_inc(pad_out, 16)
            act.dma_start(cap, a["c_cap"]).then_inc(cap_in, 16)
            act.wait_ge(pad_out, 16)
            for half in range(2):
                for e in range(6):
                    row = e + 5 - half
                    src = bass.AP(tensor=a["scratch"].tensor, offset=row * P, ap=[[1, GRID], [15 * P, H], [1, GRID]])
                    act.dma_start(bias[64 * half:64 * half + 64, :, e, :], src).then_inc(bias_in, 16)
            for o in range(28):
                act.wait_ge(proj, o + 1)
                if o < 8:
                    nc.scalar.mul(q3[:, o, CTX:T].rearrange("p (r n) -> p r n", n=GRID),
                                  bank(o)[:, CTX:T].rearrange("p (r n) -> p r n", n=GRID)[:, :, ::-1], HD ** -0.5).then_inc(q_lat, 1)
                    nc.scalar.mul(q3[:, o, 0:CTX], bank(o)[:, 0:CTX], HD ** -0.5).then_inc(read_out, 1)
                elif o < 16:
                    nc.scalar.copy(k3[:, o - 8, :], bank(o)[:, 0:T]).then_inc(read_out, 1)
                else:
                    j, n = divmod(o - 16, NT)
                    nc.scalar.copy(v3[:, n, 256 * j:256 * j + 256], bank(o)[:, 0:256]).then_inc(read_out, 1)

        @block.vector
        def _(dve):
            nc.vector.memset(k.ws[0:H, 1024:1024 + 15 * P], 0.0).then_inc(padded, 1)
            dve.wait_ge(kt_done, 1)
            nc.vector.tensor_copy(new_k.rearrange("p (b n) -> p b n", b=2), k.psum[:, 6:8, :]).then_inc(kt_ok, 1)
            dve.wait_ge(bias_in, 192)
            dve.wait_ge(cap_in, 16)
            for g in range(4):
                part = bias[:, 4 * g:4 * g + 4].rearrange("p h e n -> p (h e) n")
                nc.vector.tensor_tensor(part, part, cap.unsqueeze(1).to_broadcast([P, 24, GRID]), ALU.min).then_inc(capped, 1)
            dve.wait_ge(kc_done, 1)
            nc.vector.tensor_copy(kc.rearrange("p c t -> p (c t)").rearrange("p (b n) -> p b n", b=2), k.psum[:, 6:8, :]).then_inc(kc_ok, 1)


def phase_attention(k):
    nc = k.nc
    staged, s_done, s_ok, m_ok, e_ok, pt_done, pt_ok, o_done, r_ok, o_ok = (
        k.sem("att_" + n) for n in ("staged", "s_done", "s_ok", "m_ok", "e_ok", "pt_done", "pt_ok", "o_done", "r_ok", "o_ok"))
    q3, k3, v3, o3 = k.act3(S_PF), k.act3(S_PB), k.tok3(S_V), k.tok3(S_AF)
    slabs = k.slab[:, S_R:S_K + 1, :].rearrange("p s n -> p (s n)")
    bias = slabs[:, 0:H * 6 * GRID].rearrange("p (h n) -> p h n", h=H)
    v_ctx = k.slab[:, S_NKK, D:2 * D]
    kc = k.slab[:, S_NKK, 2 * D:3 * D].rearrange("p (c t) -> p c t", c=DC)
    qs, ks, kcs = k.ws[:, 0:T], k.ws[:, T:2 * T], k.ws[:, 2 * T:2 * T + P]
    LK = LAT + CTX
    UNITS = [(e, n) for n in (1, 2, 0) for e in range(2)]
    probs = [k.ws[:, 1024 + LK * i:1024 + LK * i + (LK if n else CTX)] for i, (e, n) in enumerate(UNITS)]
    turned = [k.ws[:, 4096 + LK * i:4096 + LK * i + (LK if n else CTX)] for i, (e, n) in enumerate(UNITS)]
    neg_max, total, inverse = (k.ws[:, 8000 + 8 * i:8006 + 8 * i] for i in range(3))

    def score_bank(i):
        return k.psum[:, i, :]

    @k.block()
    def _(block):
        def values(pe, c, i):
            e, n = UNITS[i]
            pe.wait_ge(pt_ok, 6 * c + (i + 1))
            out = k.psum[:, i, 448:512]
            col = 64 * e
            if n:
                src = [v3[:, 1, bass.ds(P * c + col, 64)], v3[:, 2, bass.ds(P * c + col, 64)], v_ctx[:, bass.ds(P * c + col, 64)]]
            else:
                src = [v3[:, 0, bass.ds(P * c + col, 64)]]
            for j, v in enumerate(src):
                last = nc.tensor.matmul(out, turned[i][:, P * j:P * j + P], v, start=j == 0, stop=j == len(src) - 1)
            last.then_inc(o_done, 1)

        def turn(act, c, i):
            act.wait_ge(pt_done, 6 * c + (i + 1))
            nc.scalar.copy(turned[i], k.psum[:, 6 + i % 2, 0:LK if UNITS[i][1] else CTX]).then_inc(pt_ok, 1)

        @block.tensor
        def _(pe):
            with pe.Fori(0, H // 2) as c:
                pe.wait_ge(staged, 3 * c + 3)
                for i, (e, n) in enumerate(UNITS):
                    rows = slice(64 * e, 64 * e + 64)
                    pe.wait_ge(o_ok, 6 * c)
                    q = qs[rows, P * n:P * n + P]
                    if n:
                        nc.tensor.matmul(score_bank(i)[:, 0:LAT], q, ks[rows, CTX:T], start=True, stop=True)
                        nc.tensor.matmul(score_bank(i)[:, LAT:LK], q, kcs[rows, :], start=True, stop=True).then_inc(s_done, 1)
                    else:
                        nc.tensor.matmul(score_bank(i)[:, 0:CTX], q, ks[rows, 0:CTX], start=True, stop=True).then_inc(s_done, 1)
                for i, (e, n) in enumerate(UNITS):
                    tiles = 3 if n else 1
                    pe.wait_ge(e_ok, 6 * c + (i + 1))
                    pe.wait_ge(pt_ok, 6 * c + max(i - 1, 0))
                    for j in range(tiles):
                        last = nc.tensor.transpose(k.psum[:, 6 + i % 2, P * j:P * j + P], probs[i][:, P * j:P * j + P], k.ident[:])
                    last.then_inc(pt_done, 1)
                    if i:
                        values(pe, c, i - 1)
                values(pe, c, 5)

        @block.gpsimd
        def _(pool):
            with pool.Fori(0, H // 2) as c:
                pool.wait_ge(s_done, 6 * c)
                for dst, src in ((qs, q3), (ks, k3), (kcs, kc)):
                    nc.gpsimd.tensor_copy(dst, src[:, bass.ds(c, 1), :].squeeze(1)).then_inc(staged, 1)

        @block.scalar
        def _(act):
            with act.Fori(0, H // 2) as c:
                for i, (e, n) in enumerate(UNITS):
                    act.wait_ge(m_ok, 6 * c + (i + 1))
                    src = probs[i] if n else score_bank(i)[:, 0:CTX]
                    if not n:
                        act.wait_ge(pt_done, 6 * c)
                    nc.scalar.activation(probs[i], src, ACT.Exp, bias=neg_max[:, i:i + 1], accum_out=total[:, i:i + 1]).then_inc(e_ok, 1)
                    if i:
                        turn(act, c, i - 1)
                turn(act, c, 5)

        @block.vector
        def _(dve):
            with dve.Fori(0, H // 2) as c:
                for i, (e, n) in enumerate(UNITS):
                    dve.wait_ge(s_done, 6 * c + (i + 1))
                    if n:
                        lo = GRID * (2 - 2 * (n - 1))
                        nc.vector.tensor_tensor(probs[i][:, 0:LAT], score_bank(i)[:, 0:LAT],
                                                bias[:, bass.ds(2 * c + e, 1), lo:lo + LAT].squeeze(1), ALU.add).then_inc(s_ok, 1)
                        nc.vector.tensor_copy(probs[i][:, LAT:LK], score_bank(i)[:, LAT:LK]).then_inc(s_ok, 1)
                        dve.wait_ge(s_ok, 8 * c + (2 * i + 2))
                        src = probs[i]
                    else:
                        src = score_bank(i)[:, 0:CTX]
                    nc.vector.tensor_reduce(neg_max[:, i:i + 1], src, AX.X, ALU.max, negate=True).then_inc(m_ok, 1)
                for i, (e, n) in enumerate(UNITS):
                    dve.wait_ge(e_ok, 6 * c + (i + 1))
                    nc.vector.reciprocal(inverse[:, i:i + 1], total[:, i:i + 1]).then_inc(r_ok, 1)
                for i, (e, n) in enumerate(UNITS):
                    dve.wait_ge(o_done, 6 * c + (i + 1))
                    dve.wait_ge(r_ok, 6 * c + (i + 1))
                    nc.vector.tensor_scalar(o3[:, n, bass.ds(P * c + 64 * e, 64)], k.psum[:, i, 448:512], inverse[:, i:i + 1],
                                            None, ALU.mult).then_inc(o_ok, 1)


def phase_na_out(k):
    nc = k.nc
    first = k.taken
    k.taken += 6
    o_turned, o_read, done, added = (k.sem("na_out_" + n) for n in ("turned", "read", "done", "added"))
    o3, ot, x = k.tok3(S_AF), k.act3(S_Y), k.act3(S_AB)

    @k.block()
    def _(block):
        @block.tensor
        def _(pe):
            for c in range(DC):
                if c >= 4:
                    pe.wait_ge(o_read, 2 * (c - 3))
                for n in range(NT):
                    last = nc.tensor.transpose(k.psum[:, c % 4, P * n:P * n + P], o3[:, n, P * c:P * c + P], k.ident[:])
                last.then_inc(o_turned, 1)
            for m in range(DC):
                if m % 2 == 0:
                    w = piece_cols(take_piece(k, pe, first + m // 2))
                if m >= 4:
                    pe.wait_ge(added, 2 * (m - 3))
                for c in range(DC):
                    pe.wait_ge(o_read, 2 * (c + 1))
                    last = nc.tensor.matmul(k.psum[:, 4 + m % 4, 0:T], w[:, c, P * (m % 2):P * (m % 2) + P], ot[:, c, :],
                                            start=c == 0, stop=c == DC - 1)
                last.then_inc(done, 1)
                k.used[first + m // 2] = (done, m + 1)

        @block.sync
        def _(sp):
            prefetch(k, sp, first, first + 6)

        @block.scalar
        def _(act):
            for c in range(DC):
                act.wait_ge(o_turned, c + 1)
                nc.scalar.copy(ot[:, c, 0:CTX], k.psum[:, c % 4, 0:CTX]).then_inc(o_read, 1)
                nc.scalar.copy(ot[:, c, CTX:T].rearrange("p (r n) -> p r n", n=GRID),
                               k.psum[:, c % 4, CTX:T].rearrange("p (r n) -> p r n", n=GRID)[:, :, ::-1]).then_inc(o_read, 1)

        @block.vector
        def _(dve):
            for m in range(DC):
                dve.wait_ge(done, m + 1)
                residual(k, dve, x, m, k.psum[:, 4 + m % 4, 0:T], 16, added)


def phase_store(k, y_slab, out_slab):
    nc = k.nc
    turned, read_out, stored = (k.sem("store_" + n) for n in ("turned", "read", "stored"))
    y, out = k.act3(y_slab), k.tok3(out_slab)

    @k.block()
    def _(block):
        @block.tensor
        def _(pe):
            for n in range(NT):
                for g in range(2):
                    for c in range(4):
                        last = nc.tensor.transpose(k.psum[:, 2 * n + g, P * c:P * c + P], y[:, 4 * g + c, P * n:P * n + P], k.ident[:])
                    last.then_inc(turned, 1)

        @block.vector
        def _(dve):
            for n in range(NT):
                for g in range(2):
                    dve.wait_ge(turned, 2 * n + g + 1)
                    nc.vector.tensor_copy(out[:, n, 512 * g:512 * g + 512], k.psum[:, 2 * n + g, :]).then_inc(read_out, 1)

        @block.sync
        def _(sp):
            for n in range(NT):
                sp.wait_ge(read_out, 2 * n + 2)
                dst = k.a["y_prompt"][0] if n == 0 else k.a["y_sample"][0, P * (n - 1):P * n, :]
                sp.dma_start(dst, out[:, n, :]).then_inc(stored, 16)
            sp.wait_ge(stored, 48)


INPUTS = ["x_prompt", "x_sample", "c", "state_rwkv", "cache_na_k", "cache_na_v", "c_ctx", "norm_mix", "norm_ffn",
          "ada_w", "ada_b", "rwkv_mu", "rwkv_w_r", "rwkv_w_k", "rwkv_w_v", "rwkv_w_o", "rwkv_w0", "rwkv_w1", "rwkv_w2",
          "rwkv_a0", "rwkv_a1", "rwkv_a2", "rwkv_g1", "rwkv_g2", "rwkv_k_k", "rwkv_k_a", "rwkv_r_k", "rwkv_lnx_g",
          "rwkv_lnx_b", "na_w_qkv", "na_w_o", "na_rpb", "moe_w_grp", "moe_b_grp", "moe_w_exp", "moe_b_exp",
          "moe_w1", "moe_w3", "moe_w2", "final_norm"]
OUTPUTS = [("y_prompt", (1, CTX, D)), ("y_sample", (1, LAT, D)), ("new_state", (1, 1, 2, H, HD, HD)),
           ("new_k", (1, 1, CTX, H, HD)), ("new_v", (1, 1, CTX, H, HD))]


def program(nc, a, ctx, stop=99):
    k = Kernel(nc, a, ctx)
    add_pieces(k)
    steps = [
        lambda: phase_inputs(k),
        lambda: phase_ada(k, 0),
        lambda: phase_norm(k, "mix0", S_Y, S_PF, S_NKK, V_NMIX, 0),
        lambda: phase_rwkv_project(k),
        lambda: phase_rwkv_rates(k),
        lambda: phase_scan(k),
        lambda: phase_rwkv_out(k),
        lambda: phase_norm(k, "ffn0", S_AB, S_Y, S_PF, V_NFFN, 24),
        lambda: phase_router(k, 0, S_Y),
        lambda: phase_moe(k, 0),
        lambda: phase_moe_out(k, 0, S_AB),
        lambda: phase_ada(k, 1),
        lambda: phase_norm(k, "mix1", S_AB, S_Y, S_PF, V_NMIX + 8, 0),
        lambda: phase_qkv(k),
        lambda: phase_attention(k),
        lambda: phase_na_out(k),
        lambda: phase_norm(k, "ffn1", S_AB, S_Y, S_PF, V_NFFN + 8, 24),
        lambda: phase_router(k, 1, S_Y),
        lambda: phase_moe(k, 1),
        lambda: phase_moe_out(k, 1, S_AB),
        lambda: phase_norm(k, "final", S_AB, S_Y, S_PF, V_FIN, None),
        lambda: phase_store(k, S_Y, S_PF),
    ]
    for s in steps[:stop]:
        s()
    return k


def kernel(**inputs):
    import concourse.bacc as bacc
    from concourse.bass_utils import run_bass_kernel_spmd

    nc = bacc.Bacc("TRN2", target_bir_lowering=False, num_devices=1)
    arrays, a = {}, {}
    given = {n: np.ascontiguousarray(inputs[n]) for n in INPUTS}
    for n, x in {**given, **constants()}.items():
        arrays[n] = x
        a[n] = nc.dram_tensor(n, x.shape, F32, kind="ExternalInput").ap()
    for n, shape in OUTPUTS:
        a[n] = nc.dram_tensor(n, shape, F32, kind="ExternalOutput").ap()
    a["h_rows"] = nc.dram_tensor("h_rows", (T, D), F32, kind="Internal").ap()
    a["y_rows"] = nc.dram_tensor("y_rows", (BLOCKS * P, D), F32, kind="Internal").ap()
    a["scratch"] = nc.dram_tensor("scratch", (H, 15, P), F32, kind="Internal").ap()
    with ExitStack() as ctx:
        program(nc, a, ctx)
    got = run_bass_kernel_spmd(nc, [arrays], core_ids=[0]).results[0]
    return tuple(got[n] for n, _ in OUTPUTS)
```

```python
from contextlib import ExitStack

import numpy as np
import concourse.bass as bass
from concourse import mybir

F32 = mybir.dt.float32
BF16 = mybir.dt.bfloat16
I32 = mybir.dt.int32
ALU = mybir.AluOpType
ACT = mybir.ActivationFunctionType
AX = mybir.AxisListType

P = 128
D = 1024
DC = D // P
CTX, LAT = 128, 256
T = CTX + LAT
NT = T // P
H, HD = 16, 64
NS = 6
PIECE = 2048
NE, DE = 16, 256
OVER = 2 * T // (P + 1)
BLOCKS = NE + OVER
NG, EPG = 4, 4
LEVELS = 6
DECAY = float(np.exp(-0.5))
EPS, GN_EPS = 1e-6, 64e-5
GRID, ROWS = 64, LAT // 64
WIN_C = 16
BIG = 1e30

V_NMIX, V_NFFN, V_FIN, V_C, V_CCTX, V_MU, V_KK, V_KA, V_RK = 0, 16, 32, 40, 48, 56, 104, 112, 120
V_W0, V_A0, V_LG, V_LB, V_ADAB = 128, 144, 160, 168, 176
NV = 272

SLAB = 3096
S_Y, S_PF, S_PB, S_AF, S_AB, S_R, S_K, S_V, S_NKK = range(9)
NSLAB = 9


def constants():
    s = np.arange(P)
    same = (s[:, None] // HD) == (s[None, :] // HD)
    out = {
        "c_ident": np.eye(P),
        "c_mean": np.full((P, P), 1.0 / D),
        "c_block": same * 1.0,
    }
    hs = np.zeros((P, DC, H))
    for c in range(DC):
        for p in range(P):
            hs[p, c, 2 * c + p // HD] = 1.0
    out["c_headsum"] = hs.reshape(P, DC * H)
    out["c_headcast"] = np.ascontiguousarray(hs.transpose(2, 1, 0)).reshape(H, DC * P)
    reset = np.ones((P, NT, P + 1))
    reset[:, :, 0] = 0.0
    out["c_reset"] = reset.reshape(P, NT * (P + 1))
    earlier = s[:, None] < s[None, :]
    causal = np.zeros((P, 2, 2, P))
    causal[:, 0, 0], causal[:, 0, 1] = earlier, earlier | np.eye(P, dtype=bool)
    causal[:, 1, 0], causal[:, 1, 1] = earlier.T, earlier.T | np.eye(P, dtype=bool)
    out["c_causal"] = causal.reshape(P, 4 * P)
    level = np.zeros((P, 2, LEVELS + 1, HD))
    for l in range(LEVELS + 1):
        m = 1 << l
        for d in range(2):
            early = [n for n in range(P) if (n // m) % 2 == d]
            for j, n in enumerate(early):
                for t in range(P):
                    level[t, d, l, j] = float(t // (2 * m) == n // (2 * m) and (t // m) % 2 != d)
    out["c_level"] = level.reshape(P, 2 * (LEVELS + 1) * HD)
    col = np.arange(GRID)
    start = np.clip(col - WIN_C // 2, 0, GRID - WIN_C)[:, None]
    cap = np.where((col[None] >= start) & (col[None] < start + WIN_C), 3e38, -BIG)
    out["c_cap"] = np.concatenate([cap[::-1], cap[::-1]])
    out["c_order"] = np.tile(np.arange(EPG, 0, -1.0), (P, NT)).reshape(P, NT * EPG)
    out["c_count"] = np.concatenate([np.tile(s, (P, 1)), s[:, None] + P * np.arange(NT)], 1)
    return {k: np.ascontiguousarray(v, dtype=np.float32) for k, v in out.items()}


class Kernel:

    def __init__(self, nc, a, ctx):
        self.nc, self.a, self.ctx = nc, a, ctx
        self.taken = 0
        self.arrival = []
        self.used = {}
        self.overflow = [0] * OVER
        self.plan = []
        sb = self.sb
        self.slab = sb("slab", [P, NSLAB, SLAB])
        self.ring = sb("ring", [P, NS, PIECE])
        self.ws = sb("ws", [P, 9984])
        self.ident = sb("ident", [P, P])
        self.mean = sb("mean", [P, P])
        self.vec = sb("vec", [P, NV])
        self.mod = sb("mod", [P, 48, 2])
        self.silu_c = sb("silu_c", [P, DC, 2])
        self.omka = sb("omka", [P, DC])
        self.sgate = sb("sgate", [P, T])
        self.s0t = sb("s0t", [P, 2, DC, HD])
        self.ep0 = sb("ep0", [P, 2, DC, NT])
        self.epe = sb("epe", [P, 2, DC, NT])
        self.headsum = sb("headsum", [P, DC, H])
        self.causal = sb("causal", [P, 2, 2, P], BF16)
        self.level = sb("level", [P, 2, LEVELS + 1, HD], BF16)
        self.ones16 = sb("ones16", [P, P + NT * NE], BF16)
        self.slots = self.slab[:, S_K, DC * T:DC * T + 2 * NT].bitcast(I32)
        self.overflow_expert = self.slab[:, S_K, DC * T + 8:DC * T + 8 + OVER].bitcast(I32)
        self.block_tokens = self.slab[:, S_V, DC * T:DC * T + BLOCKS].bitcast(I32)
        self.psum = ctx.enter_context(nc.psum_tensor("psum", [P, 8, 512], F32))
        self.ring_in = [nc.alloc_semaphore(name=f"ring_in{i}") for i in range(NS)]
        self.phase_sems = []

    def sb(self, name, shape, dt=F32):
        return self.ctx.enter_context(self.nc.sbuf_tensor(name, shape, dt))

    def sem(self, name):
        self.phase_sems.append(self.nc.alloc_semaphore(name=name))
        return self.phase_sems[-1]

    def block(self):
        def run(body):
            with self.nc.Block() as block:
                body(block)
            self.nc.clear_and_free_semaphores(self.phase_sems)
            self.nc.all_engine_barrier()
            self.phase_sems = []
        return run

    def act3(self, s):
        return self.slab[:, s, 0:DC * T].rearrange("p (c t) -> p c t", c=DC)

    def tok3(self, s):
        return self.slab[:, s, 0:NT * D].rearrange("p (n d) -> p n d", n=NT)

    def p4(self, s):
        return self.slab[:, s, :].rearrange("p (c n t) -> p c n t", c=DC, n=NT)


def cols(w, j):
    return w[:, j * 256:(j + 1) * 256].rearrange("(c p) n -> p c n", p=P)


def add_pieces(k):
    a = k.a

    def whole(src, parts=DC):
        return lambda slot: [(k.ring[:, slot, :].rearrange("p (c n) -> p c n", c=parts), src)]

    def lora_in(slot):
        w = k.ring[:, slot, :].rearrange("p (g c n) -> p g c n", g=2, c=DC)
        return ([(w[:, 0, :, 64 * d:64 * d + 64], a["rwkv_w1"][0, d].rearrange("(c p) n -> p c n", p=P))
                 for d in range(2)]
                + [(w[:, 1, :, 64 * d:64 * d + 64], a["rwkv_a1"][0, d].rearrange("(c p) n -> p c n", p=P))
                   for d in range(2)])

    def gate_in(slot):
        w = k.ring[:, slot, 0:D].rearrange("p (c n) -> p c n", c=DC)
        return [(w, a["rwkv_g1"][0].rearrange("(c p) n -> p c n", p=P))]

    def lora_out(slot):
        return [(k.ring[:, slot, 0:D], a["rwkv_w2"][0].rearrange("d r n -> (d r) n")),
                (k.ring[:, slot, D:2 * D], a["rwkv_a2"][0].rearrange("d r n -> (d r) n"))]

    def gate_out(slot):
        return [(k.ring[:, slot, 0:D], a["rwkv_g2"][0])]

    plan = [whole(cols(a["ada_w"][0], j)) for j in range(24)]
    plan += [lora_in, gate_in]
    for n in ("rwkv_w_r", "rwkv_w_k", "rwkv_w_v"):
        plan += [whole(cols(a[n][0], j)) for j in range(4)]
    plan += [lora_out] + [None] * NS + [gate_out] + [whole(cols(a["rwkv_w_o"][0], j)) for j in range(4)] + [None] * 4

    def block_piece(name, layer, b, parts):
        def piece(slot):
            e = b if b < NE else bass.ds(k.overflow[b - NE], 1)
            src = a[name][layer][e] if b < NE else a[name][layer][e].rearrange("e r n -> (e r) n")
            return [(k.ring[:, slot, :].rearrange("p (c n) -> p c n", c=parts), src.rearrange("(c p) n -> p c n", p=P))]
        return piece

    def experts(layer):
        w1, w3, w2 = ([block_piece(n, layer, b, parts) for b in range(BLOCKS)]
                      for n, parts in (("moe_w1", DC), ("moe_w3", DC), ("moe_w2", 2)))
        out = [w1[0], w3[0]]
        for b in range(BLOCKS):
            out += ([w1[b + 1], w3[b + 1]] if b + 1 < BLOCKS else []) + [w2[b]]
        return out + [None] * 3

    plan += experts(0) + [whole(cols(a["ada_w"][1], j)) for j in range(24)]
    plan += [whole(cols(a["na_w_qkv"][0], j)) for j in range(12)]
    plan += [whole(cols(a["na_w_o"][0], j)) for j in range(4)] + [None] * 2 + experts(1)
    k.plan = plan
    raised = [0] * NS
    for n, piece in enumerate(plan):
        raised[n % NS] += 16 * len(piece(n % NS)) if piece else 0
        k.arrival.append(raised[n % NS])


def load_piece(k, eng, n, first=0):
    if n >= len(k.plan) or k.plan[n] is None:
        return
    slot, before = n % NS, n - NS
    if before >= first and k.plan[before] is None:
        before -= NS
    if before >= first and before in k.used:
        sem, value = k.used[before]
        eng.wait_ge(sem, value)
    for dst, src in k.plan[n](slot):
        eng.dma_start(dst, src).then_inc(k.ring_in[slot], 16)


def take_piece(k, eng, n):
    eng.wait_ge(k.ring_in[n % NS], k.arrival[n])
    return k.ring[:, n % NS, :]


def prefetch(k, eng, first, last):
    for n in range(first + NS, last + NS):
        load_piece(k, eng, n, first)


def piece_cols(w):
    return w.rearrange("p (c n) -> p c n", c=DC)
def load_tokens(k, eng, dst, sem):
    eng.dma_start(dst[:, 0, :], k.a["x_prompt"][0]).then_inc(sem, 16)
    eng.dma_start(dst[:, 1:NT, :], k.a["x_sample"][0].rearrange("(n p) d -> p n d", p=P)).then_inc(sem, 16)


def phase_inputs(k):
    nc, a = k.nc, k.a
    consts_in, vec_in, x_in = k.sem("consts_in"), k.sem("vec_in"), k.sem("x_in")
    vec_t, vec_ok, x_t, x_half = k.sem("vec_t"), k.sem("vec_ok"), k.sem("x_t"), k.sem("x_half")
    sig_c, masks_in = k.sem("sig_c"), k.sem("masks_in")
    rows = [k.ws[0:n, 128 * i:128 * i + 128] for i, n in enumerate((128, 48, 96))]
    masks = k.ws[:, 512:512 + 4 * P + 2 * (LEVELS + 1) * HD]
    xt = k.tok3(S_R)
    x3 = k.act3(S_Y)
    vp = k.psum[:, 0, 0:NV]
    pieces = NS

    @k.block()
    def _(block):
        @block.sync
        def _(sp):
            sp.dma_start(k.ident[:], a["c_ident"]).then_inc(consts_in, 16)
            rvecs = [("norm_mix", 0, 16), ("norm_ffn", 16, 16), ("final_norm", 32, 8), ("c", 40, 8), ("c_ctx", 48, 8),
                     ("rwkv_mu", 56, 48), ("rwkv_k_k", 104, 8), ("rwkv_k_a", 112, 8), ("rwkv_r_k", 120, 8)]
            for n, at, m in rvecs:
                sp.dma_start(rows[0][at:at + m, :], flat(a[n])).then_inc(vec_in, 16)
            for n, at, m in (("rwkv_w0", 0, 16), ("rwkv_a0", 16, 16), ("rwkv_lnx_g", 32, 8), ("rwkv_lnx_b", 40, 8)):
                sp.dma_start(rows[1][at:at + m, :], flat(a[n])).then_inc(vec_in, 16)
            sp.dma_start(rows[2], flat(a["ada_b"])).then_inc(vec_in, 16)
            for n in range(pieces):
                load_piece(k, sp, n)

        @block.scalar
        def _(act):
            load_tokens(k, act, xt, x_in)
            act.dma_start(k.mean[:], a["c_mean"]).then_inc(masks_in, 16)
            act.dma_start(k.headsum[:], a["c_headsum"].rearrange("p (c h) -> p c h", c=DC)).then_inc(masks_in, 16)
            act.dma_start(masks[:, 0:4 * P], a["c_causal"]).then_inc(masks_in, 16)
            act.dma_start(masks[:, 4 * P:], a["c_level"]).then_inc(masks_in, 16)
            act.wait_ge(vec_ok, 1)
            c2 = k.vec[:, V_C:V_C + 16].rearrange("p (s c) -> p c s", s=2)
            nc.scalar.activation(k.silu_c[:, :, 0:1], c2[:, :, 1:2], ACT.Silu).then_inc(sig_c, 1)
            nc.scalar.activation(k.silu_c[:, :, 1:2], c2[:, :, 0:1], ACT.Silu).then_inc(sig_c, 1)
            act.wait_ge(x_t, 4)
            nc.scalar.copy(x3[:, 4:8, :], k.psum[:, 4:8, 0:T]).then_inc(x_half, 1)

        @block.gpsimd
        def _(pool):
            pool.wait_ge(masks_in, 64)
            nc.gpsimd.tensor_copy(k.causal[:].rearrange("p d k t -> p (d k t)"), masks[:, 0:4 * P]).then_inc(sig_c, 1)
            nc.gpsimd.tensor_copy(k.level[:].rearrange("p d l t -> p (d l t)"), masks[:, 4 * P:]).then_inc(sig_c, 1)

        @block.tensor
        def _(pe):
            pe.wait_ge(consts_in, 16)
            pe.wait_ge(vec_in, 16 * 14)
            at = 0
            for r in rows:
                n = r.shape[0]
                last = nc.tensor.transpose(vp[:, at:at + n], r, k.ident[0:n, 0:n])
                at += n
            last.then_inc(vec_t, 1)
            pe.wait_ge(x_in, 32)
            for c in range(DC - 1, -1, -1):
                if c == 0:
                    pe.wait_ge(vec_ok, 1)
                for n in range(NT):
                    last = nc.tensor.transpose(k.psum[:, c, n * P:(n + 1) * P], xt[:, n, c * P:(c + 1) * P], k.ident[:])
                last.then_inc(x_t, 1)

        @block.vector
        def _(dve):
            dve.wait_ge(vec_t, 1)
            nc.vector.tensor_copy(k.vec[:], vp).then_inc(vec_ok, 1)
            dve.wait_ge(vec_ok, 1)
            nc.vector.tensor_scalar(k.omka[:], k.vec[:, V_KA:V_KA + 8], -1.0, 1.0, ALU.mult, ALU.add).then_inc(x_half, 1)
            dve.wait_ge(x_t, 8)
            nc.vector.tensor_copy(x3[:, 0:4, :], k.psum[:, 0:4, 0:T]).then_inc(x_half, 1)


def flat(ap):
    names = "abcdef"[:len(ap.shape)]
    s = " ".join(names)
    if len(ap.shape) > 1:
        ap = ap.rearrange(f"{s} -> ({s})")
    return ap.rearrange("(r q) -> r q", q=P)


def phase_ada(k, layer):
    nc = k.nc
    first = k.taken
    k.taken += 24
    multiplied, copied, turned, added = (k.sem(f"ada{layer}_{n}") for n in ("multiplied", "copied", "turned", "added"))
    rows = k.ws[0:2, 0:48 * P]
    acc = k.psum[:, NS, 0:96]

    @k.block()
    def _(block):
        @block.tensor
        def _(pe):
            base = [k.arrival[first + u] for u in range(NS)]
            with pe.Fori(0, 4) as i:
                for u in range(NS):
                    pe.wait_ge(k.ring_in[u], 16 * i + base[u])
                    pe.wait_ge(copied, NS * i + (u + 1))
                    w = piece_cols(k.ring[:, u, :])
                    for c in range(DC):
                        last = nc.tensor.matmul(k.psum[0:2, u, 0:256], k.silu_c[:, c, :], w[:, c, :], start=c == 0, stop=c == DC - 1)
                    last.then_inc(multiplied, 1)
            for u in range(NS):
                k.used[first + 18 + u] = (multiplied, 19 + u)
            pe.wait_ge(copied, NS + 24)
            for j in range(48):
                last = nc.tensor.transpose(acc[:, 2 * j:2 * j + 2], rows[:, P * j:P * j + P], k.ident[0:2, 0:2])
            last.then_inc(turned, 1)

        @block.sync
        def _(sp):
            with sp.Fori(0, 3) as i:
                for u in range(NS):
                    sp.wait_ge(multiplied, NS * i + u + 1)
                    src = k.a["ada_w"][layer][:, bass.ds(256 * NS * i + 256 * (NS + u), 256)]
                    sp.dma_start(piece_cols(k.ring[:, u, :]), src.rearrange("(c p) n -> p c n", p=P)).then_inc(k.ring_in[u], 16)
            prefetch(k, sp, first + 18, first + 24)

        @block.scalar
        def _(act):
            nc.scalar.copy(k.ws[0:2, 48 * P:48 * P + 1], k.silu_c[0:2, 0, 0:1]).then_inc(copied, NS)
            with act.Fori(0, 4) as i:
                for u in range(NS):
                    act.wait_ge(multiplied, NS * i + u + 1)
                    nc.scalar.copy(rows[:, bass.ds(256 * NS * i + 256 * u, 256)], k.psum[0:2, u, 0:256]).then_inc(copied, 1)

        @block.vector
        def _(dve):
            dve.wait_ge(turned, 1)
            bias = k.vec[:, V_ADAB + 48 * layer:V_ADAB + 48 * layer + 48]
            nc.vector.tensor_tensor(k.mod[:], acc.rearrange("p (j s) -> p j s", s=2),
                                    bias.unsqueeze(2).to_broadcast([P, 48, 2]), ALU.add).then_inc(added, 1)


def phase_norm(k, name, x_slab, h_slab, tmp_slab, v_gain, mod_at, router=None):
    nc = k.nc
    squared, summed, meaned, rooted, scaled = (k.sem(f"{name}_{s}") for s in ("squared", "summed", "meaned", "rooted", "scaled"))
    step, out_act = k.sem(f"{name}_step"), k.sem(f"{name}_act")
    x, h, tmp = k.act3(x_slab), k.act3(h_slab), k.act3(tmp_slab)
    acc = k.psum[:, 0, 0:T]
    ms, root, rstd = (k.ws[:, 4096 + T * i:4096 + T * i + T] for i in range(3))
    gs = k.ws[:, 4096 + 3 * T:4096 + 3 * T + 16].rearrange("p (c s) -> p c s", s=2)
    router_in = k.sem(f"{name}_router_in")
    gain = k.vec[:, v_gain:v_gain + DC]

    @k.block()
    def _(block):
        @block.sync
        def _(sp):
            if router is not None:
                load_router(k, router, sp, router_in)
                sp.wait_ge(router_in, 96)

        @block.scalar
        def _(act):
            for g in range(4):
                nc.scalar.activation(tmp[:, 2 * g:2 * g + 2, :], x[:, 2 * g:2 * g + 2, :], ACT.Square).then_inc(squared, 1)
            act.wait_ge(meaned, 1)
            nc.scalar.activation(root, ms, ACT.Sqrt).then_inc(rooted, 1)
            if mod_at is not None:
                for c in range(4, DC):
                    act.wait_ge(scaled, c - 3)
                    for s, (t0, t1) in enumerate(((0, CTX), (CTX, T))):
                        nc.scalar.activation(h[:, c, t0:t1], tmp[:, c, t0:t1], ACT.Identity,
                                             bias=k.mod[:, mod_at + c, s:s + 1], scale=gs[:, c, s:s + 1]).then_inc(out_act, 1)

        @block.tensor
        def _(pe):
            for c in range(DC):
                pe.wait_ge(squared, c // 2 + 1)
                last = nc.tensor.matmul(acc, k.mean[:], tmp[:, c, :], start=c == 0, stop=c == DC - 1)
            last.then_inc(summed, 1)

        @block.vector
        def _(dve):
            if mod_at is not None:
                nc.vector.scalar_tensor_tensor(gs, k.mod[:, mod_at + DC:mod_at + 2 * DC, :], 1.0,
                                               gain.unsqueeze(2).to_broadcast([P, DC, 2]), ALU.add, ALU.mult).then_inc(step, 1)
            else:
                nc.vector.tensor_copy(gs[:, :, 0], gain).then_inc(step, 1)
            dve.wait_ge(summed, 1)
            nc.vector.tensor_scalar(ms, acc, EPS, None, ALU.add).then_inc(meaned, 1)
            dve.wait_ge(rooted, 1)
            nc.vector.reciprocal(rstd, root).then_inc(step, 1)
            dve.wait_ge(step, 2)
            for c in list(range(4, DC)) + list(range(4)):
                nc.vector.tensor_tensor(tmp[:, c, :], x[:, c, :], rstd, ALU.mult).then_inc(scaled, 1)
            for c in range(4):
                dve.wait_ge(scaled, c + 5)
                if mod_at is None:
                    nc.vector.tensor_scalar(h[:, c, :], tmp[:, c, :], gs[:, c, 0:1], None, ALU.mult).then_inc(step, 1)
                    nc.vector.tensor_scalar(h[:, c + 4, :], tmp[:, c + 4, :], gs[:, c + 4, 0:1], None, ALU.mult).then_inc(step, 1)
                else:
                    for s, (t0, t1) in enumerate(((0, CTX), (CTX, T))):
                        nc.vector.tensor_scalar(h[:, c, t0:t1], tmp[:, c, t0:t1], gs[:, c, s:s + 1],
                                                k.mod[:, mod_at + c, s:s + 1], ALU.mult, ALU.add).then_inc(step, 1)


def phase_rwkv_project(k):
    nc = k.nc
    first = k.taken
    k.taken += 14
    mixed = k.sem("mixed")
    proj, read_out = k.sem("proj"), k.sem("proj_read")
    step = k.sem("shift_step")
    h, dx = k.act3(S_PF), k.act3(S_PB)
    mix = [k.act3(S_AF), k.act3(S_AB)]
    r3, k3, v3 = k.act3(S_R), k.act3(S_K), k.tok3(S_V)
    t1, t2 = k.ws[:, 0:T], k.ws[:, T:2 * T]
    MIX_ORDER = [1, 4, 5, 0, 2, 3]

    def bank(o):
        return k.psum[:, o % 8, :]

    @k.block()
    def _(block):
        @block.vector
        def _(dve):
            n = 0
            for t0, t1_ in ((0, CTX), (CTX, T)):
                nc.vector.tensor_tensor(dx[:, :, t0 + 1:t1_ - 1], h[:, :, t0:t1_ - 2], h[:, :, t0 + 2:t1_], ALU.add).then_inc(step, 1)
                nc.vector.tensor_copy(dx[:, :, t0:t0 + 1], h[:, :, t0 + 1:t0 + 2]).then_inc(step, 1)
                nc.vector.tensor_copy(dx[:, :, t1_ - 1:t1_], h[:, :, t1_ - 2:t1_ - 1]).then_inc(step, 1)
            dve.wait_ge(step, 6)
            for g in range(2):
                nc.vector.scalar_tensor_tensor(dx[:, 4 * g:4 * g + 4, :], dx[:, 4 * g:4 * g + 4, :], 0.5,
                                               h[:, 4 * g:4 * g + 4, :], ALU.mult, ALU.subtract).then_inc(step, 1)
            dve.wait_ge(step, 8)
            for i, mu in enumerate(MIX_ORDER):
                if i >= 2:
                    dve.wait_ge(proj, i - 1 if i < 5 else 11)
                for c in range(DC):
                    nc.vector.scalar_tensor_tensor(mix[i % 2][:, c, :], dx[:, c, :], k.vec[:, V_MU + 8 * mu + c:V_MU + 8 * mu + c + 1],
                                                   h[:, c, :], ALU.mult, ALU.add).then_inc(mixed, 1)

        @block.tensor
        def _(pe):
            for i in range(3):
                if i != 1:
                    piece = take_piece(k, pe, first + i // 2)
                w = piece_cols(piece[:, D * (i % 2):D * (i % 2) + D])
                for c in range(DC):
                    pe.wait_ge(mixed, 8 * i + c + 1)
                    last = nc.tensor.matmul(bank(i)[:, 0:T], w[:, c, :], mix[i % 2][:, c, :], start=c == 0, stop=c == DC - 1)
                last.then_inc(proj, 1)
            k.used[first], k.used[first + 1] = (proj, 2), (proj, 3)
            o = 3
            for i in range(3, 5):
                for j in range(4):
                    n = first + 2 + 4 * (i - 3) + j
                    w = piece_cols(take_piece(k, pe, n))
                    for m in range(2):
                        if o >= 8:
                            pe.wait_ge(read_out, o - 7)
                        for c in range(DC):
                            if j == 0 and m == 0:
                                pe.wait_ge(mixed, 8 * i + c + 1)
                            last = nc.tensor.matmul(bank(o)[:, 0:T], w[:, c, m * P:(m + 1) * P], mix[i % 2][:, c, :],
                                                    start=c == 0, stop=c == DC - 1)
                        last.then_inc(proj, 1)
                        o += 1
                    k.used[n] = (proj, o)
            for j in range(4):
                w = piece_cols(take_piece(k, pe, first + 10 + j))
                for n in range(NT):
                    pe.wait_ge(read_out, o - 7)
                    for c in range(DC):
                        if j == 0 and n == 0:
                            pe.wait_ge(mixed, 40 + c + 1)
                        last = nc.tensor.matmul(bank(o)[:, 0:256], mix[1][:, c, n * P:(n + 1) * P], w[:, c, :],
                                                start=c == 0, stop=c == DC - 1)
                    last.then_inc(proj, 1)
                    o += 1
                k.used[first + 10 + j] = (proj, o)

        @block.sync
        def _(sp):
            prefetch(k, sp, first, first + 14)

        @block.scalar
        def _(act):
            act.wait_ge(proj, 1)
            nc.scalar.activation(t1, bank(0)[:, 0:T], ACT.Tanh).then_inc(read_out, 1)
            act.wait_ge(proj, 2)
            nc.scalar.copy(t2, bank(1)[:, 0:T]).then_inc(read_out, 1)
            act.wait_ge(proj, 3)
            nc.scalar.activation(k.sgate[:], bank(2)[:, 0:T], ACT.Sigmoid).then_inc(read_out, 1)
            o = 3
            for dst in (r3, k3):
                for c in range(DC):
                    act.wait_ge(proj, o + 1)
                    nc.scalar.copy(dst[:, c, :], bank(o)[:, 0:T]).then_inc(read_out, 1)
                    o += 1
            for j in range(4):
                for n in range(NT):
                    act.wait_ge(proj, o + 1)
                    nc.scalar.copy(v3[:, n, 256 * j:256 * j + 256], bank(o)[:, 0:256]).then_inc(read_out, 1)
                    o += 1


def phase_rwkv_rates(k):
    nc = k.nc
    first = k.taken
    k.taken += 1
    names = ("z_done", "z_read", "consts2_in", "scanned", "kk_scaled", "kk_squared", "kk_summed", "kk_copied", "kk_rooted",
             "kk_floored", "kk_inverse", "cast_done", "nkk_ok", "state_in", "state_turned", "state_ok", "edges_ok", "mid_ok",
             "centred", "edge_zero")
    (z_done, z_read, consts2, scanned, kk_scaled, kk_squared, kk_summed, kk_copied, kk_rooted, kk_floored, kk_inverse,
     cast_done, nkk_ok, state_in, state_turned, state_ok, edges_ok, mid_ok, centred, edge_zero) = (k.sem(n) for n in names)
    t1, t2 = k.ws[:, 0:T], k.ws[:, T:2 * T]
    reset = k.ws[:, 768:768 + NT * (P + 1)]
    cast = k.ws[0:H, 1160:1160 + D].rearrange("h (c p) -> h c p", c=DC)
    norm2, norm, inverse = (k.ws[0:H, 2200 + T * i:2200 + T * i + T] for i in range(3))
    mid = [k.ws[:, 3356 + 24 * d:3356 + 24 * d + 24] for d in range(2)]
    state = k.ws[0:HD, 3410:3410 + 2 * D]
    k3, kk, sq = k.act3(S_K), k.act3(S_NKK), k.act3(S_AF)
    rates = k.p4(S_Y)

    def z_bank(d, c):
        return k.psum[:, 3 * d + c % 3, 0:T]

    @k.block()
    def _(block):
        @block.tensor
        def _(pe):
            w = take_piece(k, pe, first)

            def outer(i, src):
                for d in range(2):
                    rows = slice(HD * d, HD * d + HD)
                    for c in range(DC):
                        o = 16 * i + 8 * d + c
                        if c >= 3:
                            pe.wait_ge(z_read, o - 2)
                        elif i:
                            pe.wait_ge(z_read, 8 * (2 * i + d - 1))
                        nc.tensor.matmul(z_bank(d, c), w[rows, D * i + c * P:D * i + c * P + P], src[rows, :],
                                         start=True, stop=True).then_inc(z_done, 1)

            outer(0, t1)
            pe.wait_ge(consts2, 32)
            for c in range(DC):
                pe.wait_ge(kk_squared, c + 1)
                last = nc.tensor.matmul(k.psum[0:H, 6, 0:T], k.headsum[:, c, :], sq[:, c, :], start=c == 0, stop=c == DC - 1)
            last.then_inc(kk_summed, 1)
            outer(1, t2)
            k.used[first] = (z_done, 32)
            pe.wait_ge(z_read, 32)
            pe.wait_ge(state_in, 16)
            for d in range(2):
                for c in range(DC):
                    last = nc.tensor.transpose(k.psum[:, d, HD * c:HD * c + HD], state[:, D * d + c * P:D * d + c * P + P],
                                               k.ident[0:HD, 0:HD])
            last.then_inc(state_turned, 1)
            pe.wait_ge(kk_inverse, 1)
            for c in range(DC):
                if c >= 4:
                    pe.wait_ge(nkk_ok, c - 3)
                nc.tensor.matmul(k.psum[:, 2 + c % 4, 0:T], cast[:, c, :], inverse, start=True, stop=True).then_inc(cast_done, 1)

        @block.sync
        def _(sp):
            sp.dma_start(reset, k.a["c_reset"]).then_inc(consts2, 16)
            sp.dma_start(k.ws[0:H, 1160:1160 + D], k.a["c_headcast"]).then_inc(consts2, 16)
            sp.dma_start(state.rearrange("i (e h j) -> i e h j", e=2, h=H),
                         k.a["state_rwkv"][0, 0].rearrange("e h i j -> i e h j")).then_inc(state_in, 16)
            prefetch(k, sp, first, first + 1)

        @block.scalar
        def _(act):
            act.wait_ge(edge_zero, 1)
            for d in range(2):
                if d == 1:
                    act.wait_ge(scanned, 8)
                for c in range(DC):
                    act.wait_ge(z_done, 8 * d + c + 1)
                    nc.scalar.activation(rates[:, c, :, 1:P + 1], z_bank(d, c).rearrange("p (n t) -> p n t", n=NT),
                                         ACT.Sigmoid, bias=k.vec[:, V_W0 + 8 * d + c:V_W0 + 8 * d + c + 1]).then_inc(z_read, 1)
            for c in range(DC):
                act.wait_ge(kk_scaled, c + 1)
                nc.scalar.activation(sq[:, c, :], kk[:, c, :], ACT.Square).then_inc(kk_squared, 1)
            act.wait_ge(kk_summed, 1)
            for d in range(2):
                dst = k.act3((S_AF, S_AB)[d])
                for c in range(DC):
                    act.wait_ge(z_done, 16 + 8 * d + c + 1)
                    nc.scalar.activation(dst[:, c, :], z_bank(d, c), ACT.Sigmoid,
                                         bias=k.vec[:, V_A0 + 8 * d + c:V_A0 + 8 * d + c + 1]).then_inc(z_read, 1)
            act.wait_ge(kk_copied, 1)
            nc.scalar.activation(norm, norm2, ACT.Sqrt).then_inc(kk_rooted, 1)
            act.wait_ge(centred, 2)
            for d in range(2):
                p = k.p4((S_PF, S_PB)[d])
                nc.scalar.activation(k.ep0[:, d, :, :], p[:, :, :, 0], ACT.Exp, scale=DECAY).then_inc(edges_ok, 1)
                nc.scalar.activation(k.epe[:, d, :, :], p[:, :, :, P], ACT.Exp, scale=-DECAY).then_inc(edges_ok, 1)

        @block.vector
        def _(dve):
            nc.vector.memset(rates[:, :, :, 0:1], 0.0).then_inc(edge_zero, 1)
            for c in range(DC):
                nc.vector.tensor_scalar(kk[:, c, :], k3[:, c, :], k.vec[:, V_KK + c:V_KK + c + 1], None, ALU.mult).then_inc(kk_scaled, 1)
            dve.wait_ge(consts2, 32)
            for d in range(2):
                p = k.slab[:, (S_PF, S_PB)[d], :].rearrange("p (c t) -> p c t", c=DC)
                src = k.slab[:, S_Y, :].rearrange("p (c t) -> p c t", c=DC)
                for c in range(DC):
                    dve.wait_ge(z_read, 8 * d + c + 1)
                    nc.vector.tensor_tensor_scan(p[:, c, :], reset, src[:, c, :], 0.0, ALU.mult, ALU.add).then_inc(scanned, 1)
            for d in range(2):
                p = k.slab[:, (S_PF, S_PB)[d], :].rearrange("p (n t) -> p n t", t=P + 1)
                dve.wait_ge(scanned, 8 * d + 8)
                nc.vector.tensor_copy(mid[d], p[:, :, P // 2]).then_inc(mid_ok, 1)
                dve.wait_ge(mid_ok, d + 1)
                nc.vector.tensor_tensor(p, p, mid[d].unsqueeze(2).to_broadcast([P, DC * NT, P + 1]), ALU.subtract).then_inc(centred, 1)
            dve.wait_ge(kk_summed, 1)
            nc.vector.tensor_copy(norm2, k.psum[0:H, 6, 0:T]).then_inc(kk_copied, 1)
            dve.wait_ge(kk_rooted, 1)
            nc.vector.tensor_scalar(norm2, norm, 1e-12, -1.0, ALU.max, ALU.mult).then_inc(kk_floored, 1)
            dve.wait_ge(kk_floored, 1)
            nc.vector.reciprocal(inverse, norm2).then_inc(kk_inverse, 1)
            dve.wait_ge(state_turned, 1)
            dve.wait_ge(edges_ok, 4)
            for d, (e, n) in enumerate(((k.ep0, 1), (k.epe, 2))):
                nc.vector.tensor_tensor(k.s0t[:, d, :, :], k.psum[:, d, :].rearrange("p (c i) -> p c i", c=DC),
                                        e[:, d, :, n:n + 1].to_broadcast([P, DC, HD]), ALU.mult).then_inc(state_ok, 1)
            for c in range(DC):
                dve.wait_ge(cast_done, c + 1)
                nc.vector.tensor_tensor(kk[:, c, :], kk[:, c, :], k.psum[:, 2 + c % 4, 0:T], ALU.mult).then_inc(nkk_ok, 1)


def phase_scan(k):
    nc = k.nc
    WORDS, LENT = 4992, NS * PIECE // 2
    k.taken += NS

    def pair(name):
        return [k.sem(f"scan_{name}{d}") for d in range(2)]

    exp_ok, staged, rate_ok, ar_ok, tmp_ok, kb_ok = (pair(n) for n in ("exp_ok", "staged", "rate_ok", "ar_ok", "tmp_ok", "kb_ok"))
    a_done, a_ok, t_done, t_ok, x_done, x_ok, xt_done, xt_ok = (
        pair(n) for n in ("a_done", "a_ok", "t_done", "t_ok", "x_done", "x_ok", "xt_done", "xt_ok"))
    x_init, r_done, r_ok, u_done, u_ok, y_done, y_ok = (
        pair(n) for n in ("x_init", "r_done", "r_ok", "u_done", "u_ok", "y_done", "y_ok"))
    khat_ok, kt_done, kt_ok, s_done, s_copied, s_out, s_step, s_ok = (
        pair(n) for n in ("khat_ok", "kt_done", "kt_ok", "s_done", "s_copied", "s_out", "s_step", "s_ok"))
    NL = LEVELS + 1
    TILE = [(0, 0), (1, 2), (2, 1)]

    def at(step, q, per, local):
        return q * per + (4 * per * step + local)

    def following(step, half, odd, d):
        n, after = TILE[step][d], TILE[min(step + 1, 2)][d]
        if not odd:
            return 2 * half + 1, n
        return half * -2 + 2, half * (after - n) + n if after != n else n

    class Dir:
        def __init__(self, d):
            w = k.ws[:, WORDS * d:WORDS * (d + 1)]
            lent = k.ring[:].rearrange("p s n -> p (s n)")[:, LENT * d:LENT * (d + 1)]
            self.ars, self.kbs = [], []
            for x in (w, lent):
                self.ars.append(x[:, 0:512].rearrange("p (c g t) -> p c g t", c=2, g=2))
                self.kbs.append(x[:, 512:1024].rearrange("p (g c t) -> p g c t", g=2, c=2))
            self.tmp = lent[:, 1024:1280].rearrange("p (c t) -> p c t", c=2)
            self.rate = lent[:, 1280:1536].rearrange("p (c t) -> p c t", c=2)
            self.s_ctx = lent[:, 1536:2048].rearrange("p (c n) -> p c n", c=DC)
            self.s = lent[:, 2048:2176].rearrange("p (c n) -> p c n", c=2)
            self.ak = w[:, 1024:2048].rearrange("p (e c g t) -> p e c g t", e=2, c=2, g=2)
            self.ab = w[:, 2048:3072].rearrange("p (e c g t) -> p e c g t", e=2, c=2, g=2)
            self.x = w[:, 3072:3584].rearrange("p (u t) -> p u t", u=4)
            self.kt = w[:, 3072:3584].rearrange("p (g c f) -> p g c f", g=2, c=2)
            self.xt = w[:, 3584:4096].rearrange("p (u t) -> p u t", u=4)
            self.t1 = w[:, 4096:4352].rearrange("p (u n) -> p u n", u=4)
            self.r = self.t1
            self.u = w[:, 4352:4608].rearrange("p (u n) -> p u n", u=4)
            self.v = w[:, 4608:4864].rearrange("p (c e n) -> p c e n", c=2, e=2)
            self.s0 = w[:, 4864:4992].rearrange("p (c n) -> p c n", c=2)
            self.p = k.p4((S_PF, S_PB)[d])
            self.a = k.act3((S_AF, S_AB)[d])
            self.bank = 4 * d
            self.w_end = (k.epe, k.ep0)[d][:, d]
            self.w_mid = (k.ep0, k.epe)[d][:, d]
            self.late = slice(64, 128) if d == 0 else slice(0, 64)
            self.early = slice(0, 64) if d == 0 else slice(64, 128)

        def halves(self, x, level):
            return x.rearrange("p u (b h m) -> p u b h m", h=2, m=1 << level)

    D2 = [Dir(0), Dir(1)]

    @k.block()
    def _(block):
        @block.tensor
        def _(pe):
            def turn_x(step, q, l):
                for d, b in enumerate(D2):
                    if l == 0:
                        pe.wait_ge(a_ok[d], at(step, q, 4, 4))
                    pe.wait_ge(x_ok[d], at(step, q, NL, l + 1))
                    for u in range(4):
                        last = nc.tensor.transpose(k.psum[:, b.bank + 2, P * u:P * u + P], b.x[:, u, :], k.ident[:])
                    last.then_inc(xt_done[d], 1)

            for step in range(3):
                with pe.Fori(0, 2) as half:
                    for odd in range(2):
                        q = 2 * half + odd
                        for d, b in enumerate(D2):
                            pe.wait_ge(kb_ok[d], at(step, q, 2, 2))
                            pe.wait_ge(ar_ok[d], at(step, q, 2, 2))
                            pe.wait_ge(y_ok[d], at(step, q, 2, 2))
                            for g in (1, 0):
                                for e in range(2):
                                    rows = slice(64 * e, 64 * e + 64)
                                    out = k.psum[:, b.bank + 2 * (1 - g) + e, :].rearrange("p (c g t) -> p c g t", c=2, g=2)
                                    for c in range(2):
                                        nc.tensor.matmul(out[:, c, :, b.late], b.kbs[odd][rows, g, c, :], b.ars[odd][rows, c, :, b.late],
                                                         start=True, stop=True)
                                        last = nc.tensor.matmul(out[b.early, c, :, b.early], b.kbs[odd][rows, g, c, b.early],
                                                                b.ars[odd][rows, c, :, b.early], start=True, stop=True)
                                last.then_inc(a_done[d], 1)
                        for l in range(NL):
                            for d, b in enumerate(D2):
                                if l == 0:
                                    pe.wait_ge(a_ok[d], at(step, q, 4, 2))
                                else:
                                    pe.wait_ge(x_ok[d], at(step, q, NL, l))
                                for u in range(4):
                                    if l == 0:
                                        last = nc.tensor.transpose(k.psum[:, b.bank, P * u:P * u + P], b.ab[:, u // 2, u % 2, 0, :], k.ident[:])
                                    elif l == 1:
                                        last = nc.tensor.matmul(k.psum[:, b.bank, P * u:P * u + P], b.ab[:, u // 2, u % 2, 0, :],
                                                                b.x[:, u, :], start=True, stop=True)
                                    else:
                                        last = nc.tensor.matmul(k.psum[:, b.bank, 64 * u:64 * u + 64], b.ab[:, u // 2, u % 2, 0, :],
                                                                b.halves(b.x[:, u:u + 1, :], l)[:, 0, :, d, :], start=True, stop=True)
                                last.then_inc(t_done[d], 1)
                            if l == 1:
                                turn_x(step, q, 0)
                            if l:
                                for d, b in enumerate(D2):
                                    pe.wait_ge(t_ok[d], at(step, q, NL, l + 1))
                                    pe.wait_ge(xt_ok[d], at(step, q, NL, l))
                                    for u in range(4):
                                        last = nc.tensor.matmul(k.psum[:, b.bank + 1, 64 * u:64 * u + 64], b.xt[:, u, :], b.t1[:, u, :],
                                                                start=True, stop=True)
                                    last.then_inc(x_done[d], 1)
                                turn_x(step, q, l)
                        for d, b in enumerate(D2):
                            pe.wait_ge(staged[d], at(step, q, 2, 2))
                            pe.wait_ge(xt_ok[d], at(step, q, NL, NL))
                            for u in range(4):
                                e, c = u // 2, u % 2
                                rows = slice(64 * e, 64 * e + 64)
                                out = k.psum[:, b.bank + e, 64 * c:64 * c + 64]
                                if step:
                                    nc.tensor.matmul(out, b.ars[odd][rows, c, 0, :], b.s0[rows, c, :], start=True, stop=False)
                                last = nc.tensor.matmul(out, b.ak[:, e, c, 0, :], b.v[:, c, e, :], start=step == 0, stop=True)
                            last.then_inc(r_done[d], 1)
                        if step < 2:
                            for d, b in enumerate(D2):
                                pe.wait_ge(khat_ok[d], at(step, q, 2, 2))
                                for g in range(2):
                                    for c in range(2):
                                        last = nc.tensor.transpose(k.psum[:, b.bank + 3, P * (2 * g + c):P * (2 * g + c) + P],
                                                                   b.kbs[odd][:, g, c, :], k.ident[:])
                                last.then_inc(kt_done[d], 1)
                        for d, b in enumerate(D2):
                            pe.wait_ge(r_ok[d], at(step, q, 1, 1))
                            for u in range(4):
                                last = nc.tensor.matmul(k.psum[:, b.bank + 2, 64 * u:64 * u + 64], b.xt[:, u, :], b.r[:, u, :],
                                                        start=True, stop=True)
                            last.then_inc(u_done[d], 1)
                        for d, b in enumerate(D2):
                            pe.wait_ge(u_ok[d], at(step, q, 1, 1))
                            if step < 2:
                                pe.wait_ge(kt_ok[d], at(step, q, 1, 1))
                                for u in range(4):
                                    e, c = u // 2, u % 2
                                    out = k.psum[64 * e:64 * e + 64, b.bank + 1, 64 * c:64 * c + 64]
                                    kj, bj = (b.kt[:, g, c, 64 * e:64 * e + 64] for g in range(2))
                                    if step == 0:
                                        nc.tensor.matmul(out, b.v[:, c, e, :], kj, start=True, stop=False)
                                        last = nc.tensor.matmul(out, b.u[:, u, :], bj, start=False, stop=True)
                                    else:
                                        nc.tensor.matmul(out, kj, b.v[:, c, e, :], start=True, stop=False)
                                        last = nc.tensor.matmul(out, bj, b.u[:, u, :], start=False, stop=True)
                                last.then_inc(s_done[d], 1)
                        for d, b in enumerate(D2):
                            if step < 2:
                                pe.wait_ge((s_copied, s_step)[step][d], (step + 1) * q + (step + 1))
                            for u in range(4):
                                e, c = u // 2, u % 2
                                rows = slice(64 * e, 64 * e + 64)
                                out = k.psum[rows, b.bank + 3 * e, P * c:P * c + P]
                                nc.tensor.matmul(out, b.v[:, c, e, :], b.ak[:, e, c, 1, :], start=True, stop=False)
                                if step:
                                    nc.tensor.matmul(out, b.s0[rows, c, :], b.ars[odd][rows, c, 1, :], start=False, stop=False)
                                last = nc.tensor.matmul(out, b.u[:, u, :], b.ab[:, e, c, 1, :], start=False, stop=True)
                            last.then_inc(y_done[d], 1)

        @block.scalar
        def _(act):
            def exps(d, q, n, odd):
                b = D2[d]
                inc, exc = (b.p[:, bass.ds(2 * q, 2), bass.ds(n, 1), lo:lo + P].squeeze(2) for lo in (1, 0))
                ar, kb = b.ars[odd], b.kbs[odd]
                ins = (exc, inc, inc) if d == 0 else (inc, exc, exc)
                for dst, src, sign in zip((ar[:, :, 0, :], ar[:, :, 1, :], kb[:, 0, :, :]), ins, (-1, -1, 1)):
                    nc.scalar.activation(dst, src, ACT.Exp, scale=DECAY * (sign if d == 0 else -sign)).then_inc(exp_ok[d], 1)

            for d in range(2):
                exps(d, 0, TILE[0][d], 0)
            for step in range(3):
                with act.Fori(0, 2) as half:
                    for odd in range(2):
                        q = 2 * half + odd
                        for d in range(2):
                            act.wait_ge(y_ok[d], at(step, q, 2, 2))
                            exps(d, *following(step, half, odd, d), 1 - odd)
                        for l in range(NL):
                            for d, b in enumerate(D2):
                                act.wait_ge(xt_done[d], at(step, q, NL, l + 1))
                                if l == 0:
                                    nc.scalar.copy(b.xt, k.psum[:, b.bank + 2, :].rearrange("p (u t) -> p u t", u=4)).then_inc(xt_ok[d], 1)
                                else:
                                    nc.scalar.copy(b.halves(b.xt, l)[:, :, :, 1 - d, :],
                                                   b.halves(k.psum[:, b.bank + 2, :].rearrange("p (u t) -> p u t", u=4), l)[:, :, :, 1 - d, :]).then_inc(xt_ok[d], 1)
                        for d, b in enumerate(D2):
                            act.wait_ge(r_done[d], at(step, q, 1, 1))
                            nc.scalar.copy(b.r.rearrange("p (e c) n -> p e (c n)", e=2), k.psum[:, b.bank:b.bank + 2, 0:P]).then_inc(r_ok[d], 1)
                        if step < 2:
                            for d, b in enumerate(D2):
                                act.wait_ge(kt_done[d], at(step, q, 1, 1))
                                nc.scalar.copy(b.kt.rearrange("p g c f -> p (g c f)"), k.psum[:, b.bank + 3, :]).then_inc(kt_ok[d], 1)
                        for d, b in enumerate(D2):
                            act.wait_ge(u_done[d], at(step, q, 1, 1))
                            nc.scalar.copy(b.u.rearrange("p u n -> p (u n)"), k.psum[:, b.bank + 2, 0:256]).then_inc(u_ok[d], 1)
                        if step == 0:
                            for d, b in enumerate(D2):
                                act.wait_ge(s_done[d], at(step, q, 1, 1))
                                nc.scalar.copy(b.s_ctx[:, bass.ds(2 * q, 2), :].rearrange("p c n -> p (c n)"), k.psum[:, b.bank + 1, 0:P]).then_inc(s_copied[d], 1)

        @block.vector
        def _(dve):
            def scaled(d, q, n, odd, ahead, part):
                b = D2[d]
                ar, kb = b.ars[odd], b.kbs[odd]
                toks = bass.ds(P * n, P)
                nkk, r, key = (k.act3(i)[:, bass.ds(2 * q, 2), toks] for i in (S_NKK, S_R, S_K))
                if part == 0:
                    dve.wait_ge(exp_ok[d], 3 * ahead + 3)
                    nc.vector.tensor_tensor(ar[:, :, 0, :], ar[:, :, 0, :], nkk, ALU.mult).then_inc(ar_ok[d], 1)
                    nc.vector.tensor_tensor(ar[:, :, 1, :], ar[:, :, 1, :], r, ALU.mult).then_inc(ar_ok[d], 1)
                elif part == 1:
                    for c in range(2):
                        nc.vector.tensor_scalar(b.tmp[:, c, :], b.a[:, bass.ds(2 * q + c, 1), toks].squeeze(1),
                                                k.vec[:, bass.ds(2 * q + (V_KA + c), 1)], k.omka[:, bass.ds(2 * q + c, 1)],
                                                ALU.mult, ALU.add).then_inc(tmp_ok[d], 1)
                    dve.wait_ge(tmp_ok[d], 3 * ahead + 2)
                    nc.vector.tensor_tensor(b.tmp, b.tmp, key, ALU.mult).then_inc(tmp_ok[d], 1)
                else:
                    dve.wait_ge(rate_ok[d], ahead + 1)
                    nc.vector.scalar_tensor_tensor(kb[:, 1, :, :], b.rate, -1.0, kb[:, 0, :, :], ALU.mult, ALU.mult).then_inc(kb_ok[d], 1)
                    dve.wait_ge(tmp_ok[d], 3 * ahead + 3)
                    dve.wait_ge(kb_ok[d], 2 * ahead + 1)
                    nc.vector.tensor_tensor(kb[:, 0, :, :], kb[:, 0, :, :], b.tmp, ALU.mult).then_inc(kb_ok[d], 1)

            def masked(step, q, d, i):
                b = D2[d]
                dve.wait_ge(a_done[d], at(step, q, 2, i + 1))
                src = k.psum[:, b.bank + 2 * i:b.bank + 2 * i + 2, :].rearrange("p e (c g t) -> p (e c) g t", c=2, g=2)
                dst = (b.ab, b.ak)[i].rearrange("p e c g t -> p (e c) g t")
                for part, cols in ((slice(0, P), b.late), (b.early, b.early)):
                    mask = k.causal[part, d, :, cols].unsqueeze(1).to_broadcast([part.stop - part.start, 4, 2, 64])
                    nc.vector.tensor_tensor(dst[part, :, :, cols], src[part, :, :, cols], mask, ALU.mult).then_inc(a_ok[d], 1)

            for d, b in enumerate(D2):
                nc.vector.memset(b.ak[b.late, :, :, :, b.early], 0.0).then_inc(y_ok[d], 1)
                nc.vector.memset(b.ab[b.late, :, :, :, b.early], 0.0).then_inc(y_ok[d], 1)
            for part in range(3):
                for d in range(2):
                    scaled(d, 0, TILE[0][d], 0, 0, part)
            for step in range(3):
                with dve.Fori(0, 2) as half:
                    for odd in range(2):
                        q = 2 * half + odd
                        for d in range(2):
                            masked(step, q, d, 0)
                        for l in range(NL):
                            for d, b in enumerate(D2):
                                dve.wait_ge(t_done[d], at(step, q, NL, l + 1))
                                if l < 2:
                                    src = b.halves(k.psum[:, b.bank, :].rearrange("p (u t) -> p u t", u=4), l)[:, :, :, d, :]
                                else:
                                    src = k.psum[:, b.bank, 0:256].rearrange("p (u b m) -> p u b m", u=4, m=1 << l)
                                mask = k.level[:, d, l, :].rearrange("p (b m) -> p b m", m=1 << l)
                                nc.vector.tensor_tensor(b.t1.rearrange("p u (b m) -> p u b m", m=1 << l), src,
                                                        mask.unsqueeze(1).to_broadcast([P, 4, 64 >> l, 1 << l]), ALU.mult).then_inc(t_ok[d], 1)
                            for d, b in enumerate(D2):
                                early = b.halves(b.x, l)[:, :, :, d, :]
                                if l == 0:
                                    dve.wait_ge(x_init[d], at(step, q, 1, 1))
                                    dve.wait_ge(t_ok[d], at(step, q, NL, 1))
                                    src = b.t1.rearrange("p u (b m) -> p u b m", m=1)
                                else:
                                    dve.wait_ge(x_done[d], at(step, q, NL - 1, l))
                                    dve.wait_ge(x_ok[d], at(step, q, NL, l))
                                    src = k.psum[:, b.bank + 1, 0:256].rearrange("p (u b m) -> p u b m", u=4, m=1 << l)
                                nc.vector.tensor_tensor(early, early, src, ALU.add).then_inc(x_ok[d], 1)
                            if l == 0:
                                for d in range(2):
                                    masked(step, q, d, 1)
                            else:
                                d = (l - 1) // 3
                                scaled(d, *following(step, half, odd, d), 1 - odd, at(step, q, 1, 1), (l - 1) % 3)
                        if step == 1:
                            for d, b in enumerate(D2):
                                n, nxt = TILE[1][d], TILE[2][d]
                                w_end, w_mid = (w[:, bass.ds(2 * q, 2), i:i + 1].to_broadcast([P, 2, 64])
                                                for w, i in ((b.w_end, n), (b.w_mid, nxt)))
                                dve.wait_ge(s_done[d], at(1, q, 1, 1))
                                nc.vector.tensor_tensor(b.s, b.s0, w_end, ALU.mult).then_inc(s_step[d], 1)
                                dve.wait_ge(s_step[d], 2 * q + 1)
                                nc.vector.tensor_tensor(b.s, b.s, k.psum[:, b.bank + 1, 0:P].rearrange("p (c n) -> p c n", c=2),
                                                        ALU.add).then_inc(s_step[d], 1)
                                dve.wait_ge(s_step[d], 2 * q + 2)
                                nc.vector.tensor_tensor(k.s0t[:, d, bass.ds(2 * q, 2), :], b.s, w_mid, ALU.mult).then_inc(s_ok[d], 1)
                        for d, b in enumerate(D2):
                            n = TILE[step][d]
                            dve.wait_ge(y_done[d], at(step, q, 1, 1))
                            if step == 0 and d == 1:
                                dve.wait_ge(y_ok[0], at(step, q, 2, 4))
                            for e in range(2):
                                rows = slice(64 * e, 64 * e + 64)
                                y = k.act3(S_Y)[rows, bass.ds(2 * q, 2), P * n:P * n + P]
                                src = k.psum[rows, b.bank + 3 * e, 0:256].rearrange("p (c t) -> p c t", c=2)
                                if step == 1 or (step, d) == (0, 0):
                                    nc.vector.tensor_copy(y, src).then_inc(y_ok[d], 1)
                                else:
                                    nc.vector.tensor_tensor(y, y, src, ALU.add).then_inc(y_ok[d], 1)

        @block.gpsimd
        def _(pool):
            def rates(d, q, n):
                b = D2[d]
                toks = bass.ds(P * n, P)
                nc.gpsimd.tensor_tensor(b.rate, k.act3(S_NKK)[:, bass.ds(2 * q, 2), toks], b.a[:, bass.ds(2 * q, 2), toks],
                                        ALU.mult).then_inc(rate_ok[d], 1)

            for d in range(2):
                rates(d, 0, TILE[0][d])
            for step in range(3):
                with pool.Fori(0, 2) as half:
                    for odd in range(2):
                        q = 2 * half + odd
                        for d, b in enumerate(D2):
                            pool.wait_ge(y_ok[d], at(step, q, 2, 2))
                            eye = k.ident[:].unsqueeze(1).to_broadcast([P, 4, P])
                            nc.gpsimd.tensor_tensor(b.x, eye, eye, ALU.mult).then_inc(x_init[d], 1)
                        for d, b in enumerate(D2):
                            n = TILE[step][d]
                            nc.gpsimd.tensor_copy(b.v.rearrange("p c e n -> p (c e n)"),
                                                  k.tok3(S_V)[:, n, bass.ds(256 * q, 256)]).then_inc(staged[d], 1)
                            if step == 2:
                                pool.wait_ge(s_ok[d], 4)
                            nc.gpsimd.tensor_copy(b.s0, k.s0t[:, d, bass.ds(2 * q, 2), :]).then_inc(staged[d], 1)
                        if step < 2:
                            for d, b in enumerate(D2):
                                n = TILE[step][d]
                                pool.wait_ge(a_done[d], at(step, q, 2, 2))
                                w_end = b.w_end[:, bass.ds(2 * q, 2), n:n + 1].to_broadcast([P, 2, P])
                                for g in range(2):
                                    nc.gpsimd.tensor_tensor(b.kbs[odd][:, g, :, :], b.kbs[odd][:, g, :, :], w_end, ALU.mult).then_inc(khat_ok[d], 1)
                        for d, b in enumerate(D2):
                            pool.wait_ge(kb_ok[d], at(step, q, 2, 2))
                            rates(d, *following(step, half, odd, d))

        @block.sync
        def _(sp):
            new = k.a["new_state"][0, 0]
            with sp.Fori(0, 4) as q:
                for d, b in enumerate(D2):
                    sp.wait_ge(s_copied[d], q + 1)
                    dst = new[d][bass.ds(4 * q, 4)]
                    for e in range(2):
                        sp.dma_start(dst.rearrange("(c e) i j -> e i c j", e=2)[e],
                                     b.s_ctx[64 * e:64 * e + 64, bass.ds(2 * q, 2), :]).then_inc(s_out[d], 16)
            for d in range(2):
                sp.wait_ge(s_out[d], 128)


def residual(k, dve, x, c, acc, gate_at, sem):
    for s, (t0, t1) in enumerate(((0, CTX), (CTX, T))):
        k.nc.vector.scalar_tensor_tensor(x[:, c, t0:t1], acc[:, t0:t1], k.mod[:, gate_at + c, s:s + 1], x[:, c, t0:t1],
                                         ALU.mult, ALU.add).then_inc(sem, 1)


def phase_rwkv_out(k):
    nc = k.nc
    first = k.taken
    k.taken += 9
    names = ("block_in", "cast_in", "x_in2", "rates_sum", "bonus_a", "bonus_b", "bonus_t", "mean_done", "less_mean", "y_squared",
             "var_done", "var_eps", "var_root", "rstd_ok", "bonus_done", "bonus_read", "vt_done", "bonus_ok", "rs_done", "y_scaled",
             "y_affine", "y_bonus", "g_done", "y_gated", "x_turned", "x_read", "o_done", "o_read", "omka2_ok")
    (block_in, cast_in, x_in, rates_sum, bonus_a, bonus_b, bonus_t, mean_done, less_mean, y_squared, var_done, var_eps, var_root,
     rstd_ok, bonus_done, bonus_read, vt_done, bonus_ok, rs_done, y_scaled, y_affine, y_bonus, g_done, y_gated, x_turned, x_read,
     o_done, o_read, omka2_ok) = (k.sem("post_" + n) for n in names)
    ones = k.ws[:, 0:P]
    cast = k.ws[0:H, 1160:1160 + D].rearrange("h (c p) -> h c p", c=DC)
    var, root, rstd = (k.ws[0:H, 2200 + T * i:2200 + T * i + T] for i in range(3))
    omka2 = k.ws[:, 130:138]
    y, sq, tb = k.act3(S_Y), k.act3(S_PF), k.act3(S_PB)
    af, ab, r3, k3, v3, xt, x = (k.act3(S_AF), k.act3(S_AB), k.act3(S_R), k.act3(S_K), k.tok3(S_V), k.tok3(S_NKK), k.act3(S_AB))

    @k.block()
    def _(block):
        @block.tensor
        def _(pe):
            pe.wait_ge(block_in, 16)
            for c in range(DC):
                if c >= 2:
                    pe.wait_ge(less_mean, c - 1)
                nc.tensor.matmul(k.psum[:, c % 2, 0:T], ones, y[:, c, :], start=True, stop=True).then_inc(mean_done, 1)
            for c in range(DC):
                pe.wait_ge(bonus_t, c + 1)
                if c >= 2:
                    pe.wait_ge(bonus_read, c - 1)
                nc.tensor.matmul(k.psum[:, 3 + c % 2, 0:T], ones, tb[:, c, :], start=True, stop=True).then_inc(bonus_done, 1)
            for c in range(DC):
                if c >= 2:
                    pe.wait_ge(bonus_ok, c - 1)
                for n in range(NT):
                    last = nc.tensor.transpose(k.psum[:, 5 + c % 2, P * n:P * n + P], v3[:, n, P * c:P * c + P], k.ident[:])
                last.then_inc(vt_done, 1)
            for c in range(DC):
                pe.wait_ge(y_squared, c + 1)
                last = nc.tensor.matmul(k.psum[0:H, 2, 0:T], k.headsum[:, c, :], sq[:, c, :], start=c == 0, stop=c == DC - 1)
            last.then_inc(var_done, 1)
            pe.wait_ge(x_in, 32)
            for c in range(DC):
                if c >= 2:
                    pe.wait_ge(x_read, c - 1)
                else:
                    pe.wait_ge(bonus_read, 8)
                for n in range(NT):
                    last = nc.tensor.transpose(k.psum[:, 3 + c % 2, P * n:P * n + P], xt[:, n, P * c:P * c + P], k.ident[:])
                last.then_inc(x_turned, 1)
            pe.wait_ge(rstd_ok, 1)
            pe.wait_ge(cast_in, 16)
            g2 = take_piece(k, pe, first)
            for c in range(DC):
                if c >= 2:
                    pe.wait_ge(y_scaled, c - 1)
                else:
                    pe.wait_ge(less_mean, 8)
                nc.tensor.matmul(k.psum[:, c % 2, 0:T], cast[:, c, :], rstd, start=True, stop=True).then_inc(rs_done, 1)
                if c >= 2:
                    pe.wait_ge(y_gated, c - 1)
                nc.tensor.matmul(k.psum[:, (7, 2)[c % 2], 0:T], g2[:, P * c:P * c + P], k.sgate[:], start=True, stop=True).then_inc(g_done, 1)
            k.used[first] = (g_done, 8)
            for o in range(DC):
                if o % 2 == 0:
                    w = piece_cols(take_piece(k, pe, first + 1 + o // 2))
                if o < 2:
                    pe.wait_ge(bonus_ok, 8)
                else:
                    pe.wait_ge(o_read, 2 * (o - 1))
                for c in range(DC):
                    pe.wait_ge(y_gated, c + 1)
                    last = nc.tensor.matmul(k.psum[:, 5 + o % 2, 0:T], w[:, c, P * (o % 2):P * (o % 2) + P], y[:, c, :],
                                            start=c == 0, stop=c == DC - 1)
                last.then_inc(o_done, 1)
                k.used[first + 1 + o // 2] = (o_done, o + 1)

        @block.sync
        def _(sp):
            sp.dma_start(ones, k.a["c_block"]).then_inc(block_in, 16)
            sp.dma_start(k.ws[0:H, 1160:1160 + D], k.a["c_headcast"]).then_inc(cast_in, 16)
            load_tokens(k, sp, xt, x_in)
            prefetch(k, sp, first - NS, first)
            prefetch(k, sp, first, first + 9)

        @block.gpsimd
        def _(pool):
            for g in range(4):
                nc.gpsimd.tensor_tensor(tb[:, 2 * g:2 * g + 2, :], af[:, 2 * g:2 * g + 2, :], ab[:, 2 * g:2 * g + 2, :], ALU.add).then_inc(rates_sum, 1)

        @block.scalar
        def _(act):
            for c in range(DC):
                act.wait_ge(less_mean, c + 1)
                nc.scalar.activation(sq[:, c, :], y[:, c, :], ACT.Square).then_inc(y_squared, 1)
                act.wait_ge(bonus_done, c + 1)
                act.wait_ge(rates_sum, 4)
                nc.scalar.copy(af[:, c, :], k.psum[:, 3 + c % 2, 0:T]).then_inc(bonus_read, 1)
            act.wait_ge(var_eps, 1)
            nc.scalar.activation(root, var, ACT.Sqrt).then_inc(var_root, 1)
            for c in range(DC):
                act.wait_ge(x_turned, c + 1)
                nc.scalar.copy(x[:, c, :], k.psum[:, 3 + c % 2, 0:T]).then_inc(x_read, 1)
            for c in range(DC):
                act.wait_ge(y_scaled, c + 1)
                nc.scalar.activation(y[:, c, :], y[:, c, :], ACT.Identity, bias=k.vec[:, V_LB + c:V_LB + c + 1],
                                     scale=k.vec[:, V_LG + c:V_LG + c + 1]).then_inc(y_affine, 1)

        @block.vector
        def _(dve):
            nc.vector.tensor_scalar(omka2, k.omka[:], 2.0, None, ALU.mult).then_inc(omka2_ok, 1)
            dve.wait_ge(omka2_ok, 1)
            for c in range(DC):
                dve.wait_ge(mean_done, c + 1)
                nc.vector.scalar_tensor_tensor(y[:, c, :], k.psum[:, c % 2, 0:T], -1.0 / HD, y[:, c, :], ALU.mult, ALU.add).then_inc(less_mean, 1)
                dve.wait_ge(rates_sum, c // 2 + 1)
                nc.vector.tensor_scalar(tb[:, c, :], tb[:, c, :], k.vec[:, V_KA + c:V_KA + c + 1], omka2[:, c:c + 1],
                                        ALU.mult, ALU.add).then_inc(bonus_a, 1)
                dve.wait_ge(bonus_a, c + 1)
                nc.vector.tensor_tensor(tb[:, c, :], tb[:, c, :], k3[:, c, :], ALU.mult).then_inc(bonus_b, 1)
                dve.wait_ge(bonus_b, c + 1)
                nc.vector.scalar_tensor_tensor(tb[:, c, :], r3[:, c, :], k.vec[:, V_RK + c:V_RK + c + 1], tb[:, c, :],
                                               ALU.mult, ALU.mult).then_inc(bonus_t, 1)
            for c in range(DC):
                dve.wait_ge(vt_done, c + 1)
                dve.wait_ge(bonus_read, c + 1)
                nc.vector.tensor_tensor(af[:, c, :], af[:, c, :], k.psum[:, 5 + c % 2, 0:T], ALU.mult).then_inc(bonus_ok, 1)
            dve.wait_ge(var_done, 1)
            nc.vector.tensor_scalar(var, k.psum[0:H, 2, 0:T], 1.0 / HD, GN_EPS, ALU.mult, ALU.add).then_inc(var_eps, 1)
            dve.wait_ge(var_root, 1)
            nc.vector.reciprocal(rstd, root).then_inc(rstd_ok, 1)
            for c in range(DC + 1):
                if c < DC:
                    dve.wait_ge(rs_done, c + 1)
                    nc.vector.tensor_tensor(y[:, c, :], y[:, c, :], k.psum[:, c % 2, 0:T], ALU.mult).then_inc(y_scaled, 1)
                if c:
                    b = c - 1
                    dve.wait_ge(y_affine, b + 1)
                    nc.vector.tensor_tensor(y[:, b, :], y[:, b, :], af[:, b, :], ALU.add).then_inc(y_bonus, 1)
                    dve.wait_ge(g_done, b + 1)
                    dve.wait_ge(y_bonus, b + 1)
                    nc.vector.tensor_tensor(y[:, b, :], y[:, b, :], k.psum[:, (7, 2)[b % 2], 0:T], ALU.mult).then_inc(y_gated, 1)
            dve.wait_ge(x_read, 8)
            for o in range(DC):
                dve.wait_ge(o_done, o + 1)
                residual(k, dve, x, o, k.psum[:, 5 + o % 2, 0:T], 16, o_read)


def load_router(k, layer, eng, sem):
    a = k.a
    w, bias = k.ws[:, 0:DC * 20].rearrange("p (c n) -> p c n", c=DC), k.ws[:, 160:180]
    for n, lo, hi in (("grp", 0, 4), ("exp", 4, 20)):
        eng.dma_start(w[:, :, lo:hi], a["moe_w_" + n][layer].rearrange("(c p) n -> p c n", p=P)).then_inc(sem, 16)
        eng.dma_start(bias[:, lo:hi], a["moe_b_" + n][layer].partition_broadcast(P)).then_inc(sem, 16)
    eng.dma_start(k.ws[:, 180:192], a["c_order"]).then_inc(sem, 16)
    eng.dma_start(k.ws[:, 1024:1024 + P + NT], a["c_count"]).then_inc(sem, 16)


def phase_router(k, layer, h_slab):
    nc, a = k.nc, k.a
    names = ("logit_done", "step", "exps", "rows_turned", "rows_read", "rows_out", "chosen", "ranked",
             "placed", "listed")
    logit_done, step, exps, rows_turned, rows_read, rows_out, chosen, ranked, placed, listed = (
        k.sem(f"router{layer}_{n}") for n in names)
    h, rows = k.act3(h_slab), k.tok3(S_R)
    w = k.ws[:, 0:DC * 20].rearrange("p (c n) -> p c n", c=DC)
    bias, order = k.ws[:, 160:180], k.ws[:, 180:192].rearrange("p (n j) -> p n j", n=NT)
    count = k.ws[:, 1024:1024 + P]
    token = k.ws[:, 1024 + P:1024 + P + NT]
    at = [192]

    def buf(*shape):
        n = int(np.prod(shape))
        v = k.ws[:, at[0]:at[0] + n]
        at[0] += n
        names = "abc"[:len(shape)]
        return v if len(shape) == 1 else v.rearrange(f"p ({' '.join(names)}) -> p {' '.join(names)}",
                                                     **dict(zip(names, shape)))

    lg, gmax, rel, gexp, gsum, one_g, top = buf(NT, 20), buf(NT), buf(NT, 4), buf(NT, 4), buf(NT), buf(NT, 4), buf(NT)
    sel, le, m1, d1, one1, d2, m2, one2, e2 = (buf(NT, 4, 4), buf(NT, 4), buf(NT), buf(NT, 4), buf(NT, 4), buf(NT, 4),
                                               buf(NT), buf(NT, 4), buf(NT))
    den, t4 = buf(NT), buf(NT, 4)
    at[0] = 1200
    pick = buf(2, NT, NE)
    rank, high, blk, pos, part = (buf(NT, NE) for _ in range(5))
    over, over_sum, over_at, flags = buf(NE), buf(NE), buf(NE), buf(OVER, NE)
    found, slot_f, blk_f, pos_f = buf(OVER), buf(2, NT), buf(2, NT), buf(2, NT)
    in_pos, in_blk = buf(2 * NT, P), buf(2 * NT, BLOCKS)
    both, ones = k.ones16[:, P:P + NT * NE], k.ones16[:, 0:P]
    weight = k.ws[:, WEIGHT_AT:WEIGHT_AT + 2 * NT].rearrange("p (k n) -> p k n", k=2)

    def wide(v, n=4):
        return v.unsqueeze(2).to_broadcast([P, NT, n])

    @k.block()
    def _(block):
        @block.sync
        def _(sp):
            for n in range(NT):
                sp.wait_ge(rows_read, 2 * n + 2)
                sp.dma_start(a["h_rows"][P * n:P * n + P, :], rows[:, n, :]).then_inc(rows_out, 16)
            sp.wait_ge(rows_out, 16 * NT)

        @block.tensor
        def _(pe):
            for n in range(NT):
                for c in range(DC):
                    last = nc.tensor.matmul(k.psum[:, n, 0:20], h[:, c, P * n:P * n + P], w[:, c, :], start=c == 0, stop=c == DC - 1)
            last.then_inc(logit_done, 1)
            for n in range(NT):
                for g in range(2):
                    i = 2 * n + g
                    if i >= 4:
                        pe.wait_ge(rows_read, i - 3)
                    for c in range(4):
                        last = nc.tensor.transpose(k.psum[:, 3 + i % 4, P * c:P * c + P], h[:, 4 * g + c, P * n:P * n + P], k.ident[:])
                    last.then_inc(rows_turned, 1)
            pe.wait_ge(chosen, 2)
            for n in range(NT):
                for m in range(n + 1):
                    nc.tensor.matmul(k.psum[:, 7, NE * n:NE * n + NE], k.causal[:, 0, 0, :] if m == n else ones,
                                     both[:, NE * m:NE * m + NE], start=m == 0, stop=m == n)
            for m in range(NT):
                last = nc.tensor.matmul(k.psum[:, 7, 3 * NE:4 * NE], ones, both[:, NE * m:NE * m + NE], start=m == 0, stop=m == NT - 1)
            last.then_inc(ranked, 1)
            pe.wait_ge(placed, 2)
            for i in range(2 * NT):
                last = nc.tensor.matmul(k.psum[:, 0, 0:BLOCKS], in_pos[:, i, :], in_blk[:, i, :], start=i == 0, stop=i == 2 * NT - 1)
            last.then_inc(listed, 1)

        @block.scalar
        def _(act):
            for i in range(2 * NT):
                act.wait_ge(rows_turned, i + 1)
                nc.scalar.copy(rows[:, i // 2, 512 * (i % 2):512 * (i % 2) + 512], k.psum[:, 3 + i % 4, :]).then_inc(rows_read, 1)
            act.wait_ge(step, 3)
            nc.scalar.activation(gexp, rel, ACT.Exp).then_inc(exps, 1)
            act.wait_ge(step, SECOND)
            nc.scalar.activation(e2, m2, ACT.Exp).then_inc(exps, 1)

        @block.gpsimd
        def _(pool):
            nc.gpsimd.memset(ones, 1.0).then_inc(chosen, 1)

        @block.vector
        def _(dve):
            n = [0]

            def then(ins):
                n[0] += 1
                ins.then_inc(step, 1)
                dve.wait_ge(step, n[0])

            def first_of(dst, flags):
                then(nc.vector.tensor_tensor(t4, flags, order, ALU.mult))
                then(nc.vector.tensor_reduce(top, t4, AX.X, ALU.max))
                then(nc.vector.tensor_tensor(dst, t4, wide(top), ALU.is_equal))

            dve.wait_ge(logit_done, 1)
            then(nc.vector.tensor_tensor(lg, k.psum[:, 0:NT, 0:20], bias.unsqueeze(1).to_broadcast([P, NT, 20]), ALU.add))
            then(nc.vector.tensor_reduce(gmax, lg[:, :, 0:4], AX.X, ALU.max))
            then(nc.vector.tensor_tensor(rel, lg[:, :, 0:4], wide(gmax), ALU.subtract))
            then(nc.vector.tensor_scalar(d1, rel, 0.0, None, ALU.is_ge))
            first_of(one_g, d1)
            then(nc.vector.tensor_tensor(sel, lg[:, :, 4:20].rearrange("p n (g j) -> p n g j", g=4),
                                         one_g.unsqueeze(3).to_broadcast([P, NT, 4, 4]), ALU.mult))
            then(nc.vector.tensor_reduce(le, sel.rearrange("p n g j -> p n j g"), AX.X, ALU.add))
            then(nc.vector.tensor_reduce(m1, le, AX.X, ALU.max))
            then(nc.vector.tensor_tensor(d1, le, wide(m1), ALU.subtract))
            then(nc.vector.tensor_scalar(d2, d1, 0.0, None, ALU.is_ge))
            first_of(one1, d2)
            then(nc.vector.scalar_tensor_tensor(d2, one1, -BIG, d1, ALU.mult, ALU.add))
            then(nc.vector.tensor_reduce(m2, d2, AX.X, ALU.max))
            assert n[0] == SECOND
            then(nc.vector.tensor_tensor(d1, d2, wide(m2), ALU.is_ge))
            first_of(one2, d1)
            for i, one in enumerate((one1, one2)):
                then(nc.vector.tensor_tensor(pick[:, i].rearrange("p n (g j) -> p n g j", g=NG),
                                             one_g.unsqueeze(3).to_broadcast([P, NT, 4, 4]),
                                             one.unsqueeze(2).to_broadcast([P, NT, 4, 4]), ALU.mult))
            nc.vector.tensor_tensor(both.rearrange("p (n e) -> p n e", n=NT), pick[:, 0], pick[:, 1], ALU.add).then_inc(chosen, 1)
            dve.wait_ge(ranked, 1)
            total = k.psum[:, 7, 3 * NE:4 * NE]
            then(nc.vector.tensor_scalar(over, total, float(P) + 0.5, None, ALU.is_ge))
            then(nc.vector.tensor_scalar(over_at, total, 2.0 * P + 0.5, None, ALU.is_ge))
            then(nc.vector.tensor_tensor(over, over, over_at, ALU.add))
            then(nc.vector.tensor_tensor_scan(over_sum, over, over, 0.0, ALU.add, ALU.max))
            then(nc.vector.tensor_tensor(over_at, over_sum, over, ALU.subtract))
            then(nc.vector.tensor_tensor(flags, count[:, 0:OVER].unsqueeze(2).to_broadcast([P, OVER, NE]),
                                         over_at.unsqueeze(1).to_broadcast([P, OVER, NE]), ALU.is_ge))
            then(nc.vector.tensor_reduce(found, flags, AX.X, ALU.add))
            then(nc.vector.tensor_scalar(k.overflow_expert[:], found, -1.0, None, ALU.add))
            then(nc.vector.tensor_copy(rank, k.psum[:, 7, 0:NT * NE].rearrange("p (n e) -> p n e", n=NT)))
            then(nc.vector.tensor_scalar(part, rank, float(P), None, ALU.is_ge))
            then(nc.vector.tensor_scalar(high, rank, 2.0 * P, None, ALU.is_ge))
            then(nc.vector.tensor_tensor(high, high, part, ALU.add))
            then(nc.vector.scalar_tensor_tensor(pos, high, -float(P), rank, ALU.mult, ALU.add))
            then(nc.vector.tensor_scalar(over_sum, over_at, NE - 1.0, None, ALU.add))
            then(nc.vector.tensor_tensor(over_sum, over_sum, count[:, 0:NE], ALU.subtract))
            then(nc.vector.tensor_tensor(blk, high, over_sum.unsqueeze(1).to_broadcast([P, NT, NE]), ALU.add))
            then(nc.vector.tensor_tensor(blk, blk, part, ALU.mult))
            then(nc.vector.tensor_tensor(blk, blk, count[:, 0:NE].unsqueeze(1).to_broadcast([P, NT, NE]), ALU.add))
            for src, dst in ((pos, pos_f), (blk, blk_f)):
                for i in range(2):
                    then(nc.vector.tensor_tensor(part, pick[:, i], src, ALU.mult))
                    then(nc.vector.tensor_reduce(dst[:, i], part, AX.X, ALU.add))
            pf, bf = pos_f.rearrange("p k n -> p (k n)"), blk_f.rearrange("p k n -> p (k n)")
            then(nc.vector.tensor_tensor(in_blk, count[:, 0:BLOCKS].unsqueeze(1).to_broadcast([P, 2 * NT, BLOCKS]),
                                         bf.unsqueeze(2).to_broadcast([P, 2 * NT, BLOCKS]), ALU.is_equal))
            for i in range(2):
                both_n = in_blk[:, NT * i:NT * i + NT, :]
                ins = nc.vector.tensor_tensor(both_n, both_n, token.unsqueeze(2).to_broadcast([P, NT, BLOCKS]), ALU.mult)
                if i:
                    ins.then_inc(placed, 1)
                else:
                    then(ins)
            nc.vector.tensor_tensor(in_pos, count.unsqueeze(1).to_broadcast([P, 2 * NT, P]),
                                    pf.unsqueeze(2).to_broadcast([P, 2 * NT, P]), ALU.is_equal).then_inc(placed, 1)
            then(nc.vector.scalar_tensor_tensor(slot_f.rearrange("p k n -> p (k n)"), bf, float(P), pf, ALU.mult, ALU.add))
            then(nc.vector.tensor_copy(k.slots[:], slot_f.rearrange("p k n -> p (k n)")))
            dve.wait_ge(exps, 2)
            then(nc.vector.tensor_reduce(gsum, gexp, AX.X, ALU.add))
            then(nc.vector.scalar_tensor_tensor(den, e2, 1.0, gsum, ALU.add, ALU.mult))
            then(nc.vector.reciprocal(weight[:, 0], den))
            then(nc.vector.tensor_tensor(weight[:, 1], weight[:, 0], e2, ALU.mult))
            dve.wait_ge(listed, 1)
            then(nc.vector.tensor_copy(k.block_tokens[:], k.psum[:, 0, 0:BLOCKS]))


SECOND = 17
WEIGHT_AT = 1184


def phase_moe(k, layer):
    nc, a = k.nc, k.a
    first = k.taken
    k.taken += 66
    names = ("gathered0", "gathered1", "y_out0", "y_out1", "turned", "turn_read", "h_done", "silu_ok", "hid_ok", "y_done", "y_half0", "y_half1")
    gathered0, gathered1, y_out0, y_out1, turned, turn_read, h_done, silu_ok, hid_ok, y_done, y_half0, y_half1 = (
        k.sem(f"moe{layer}_{n}") for n in names)
    gathered, y_out = (gathered0, gathered1), (y_out0, y_out1)
    rows = [k.slab[:, S_R, D * i:D * i + D] for i in range(2)]
    cols_ = [k.slab[:, S_PF, D * i:D * i + D].rearrange("p (c s) -> p c s", c=DC) for i in range(2)]
    ys = [k.slab[:, S_PB, D * i:D * i + D] for i in range(2)]
    silu = [k.ws[:, 2048 + 256 * i:2304 + 256 * i].rearrange("p (f s) -> p f s", f=2) for i in range(2)]
    hid = [k.ws[:, 3072 + 256 * i:3328 + 256 * i].rearrange("p (f s) -> p f s", f=2) for i in range(2)]

    def w1_at(b):
        return 3 * b - 1 if b else 0

    def w3_at(b):
        return 3 * b if b else 1

    def w2_at(b):
        return 3 * b + 4 if b < BLOCKS - 1 else 3 * BLOCKS - 1

    LOOPS = (BLOCKS - 5) // 2

    @k.block()
    def _(block):
        @block.tensor
        def _(pe):
            def arrived(i, place):
                pe.wait_ge(k.ring_in[place % NS], i * 16 + k.arrival[first + place])
                return k.ring[:, place % NS, :]

            def turn(i, b):
                pe.wait_ge(gathered[b % 2], 16 * i + 16 * (b // 2 + 1))
                if b:
                    pe.wait_ge(turn_read, 4 * i + 2 * b)
                for c in range(DC):
                    last = nc.tensor.transpose(k.psum[:, c // 4, P * (c % 4):P * (c % 4) + P],
                                               rows[b % 2][:, P * c:P * c + P], k.ident[:])
                last.then_inc(turned, 1)

            def inner(i, b):
                w1, w3 = piece_cols(arrived(i, w1_at(b))), piece_cols(arrived(i, w3_at(b)))
                pe.wait_ge(turn_read, 4 * i + (2 * b + 2))
                if b >= 2:
                    pe.wait_ge(hid_ok, 2 * i + (b - 1))
                for j, w in enumerate((w1, w3)):
                    for f in range(2):
                        for c in range(DC):
                            last = nc.tensor.matmul(k.psum[:, 2 + b % 2, P * (2 * j + f):P * (2 * j + f) + P],
                                                    w[:, c, P * f:P * f + P], cols_[b % 2][:, c, :], start=c == 0, stop=c == DC - 1)
                last.then_inc(h_done, 1)

            def outer(i, b):
                w2 = arrived(i, w2_at(b)).rearrange("p (f n) -> p f n", f=2)
                pe.wait_ge(hid_ok, 2 * i + (b + 1))
                if b >= 2:
                    pe.wait_ge(y_half0, 2 * i + (b - 1))
                    pe.wait_ge(y_half1, 2 * i + (b - 1))
                for half in range(2):
                    for f in range(2):
                        last = nc.tensor.matmul(k.psum[:, 4 + 2 * (b % 2) + half, :], hid[b % 2][:, f, :],
                                                w2[:, f, 512 * half:512 * half + 512], start=f == 0, stop=f == 1)
                last.then_inc(y_done, 1)

            turn(0, 0)
            inner(0, 0)
            turn(0, 1)
            inner(0, 1)
            turn(0, 2)
            outer(0, 0)
            inner(0, 2)
            turn(0, 3)
            outer(0, 1)
            with pe.Fori(0, LOOPS) as i:
                inner(i, 3)
                turn(i, 4)
                outer(i, 2)
                inner(i, 4)
                turn(i, 5)
                outer(i, 3)
            inner(0, BLOCKS - 2)
            turn(0, BLOCKS - 1)
            outer(0, BLOCKS - 3)
            inner(0, BLOCKS - 1)
            outer(0, BLOCKS - 2)
            outer(0, BLOCKS - 1)
            for b in range(BLOCKS):
                k.used[first + w1_at(b)] = k.used[first + w3_at(b)] = (h_done, b + 1)
                k.used[first + w2_at(b)] = (y_done, b + 1)

        @block.sync
        def _(sp):
            k.overflow = [sp.value_load(k.overflow_expert[0:1, j:j + 1], min_val=0, max_val=NE - 1) for j in range(OVER)]
            body = [(6, "moe_w3", 2, [(h_done, 1)]), (7, "moe_w2", 1, [(h_done, 1), (y_done, 0)]),
                    (8, "moe_w1", 3, [(h_done, 2)]), (9, "moe_w3", 3, [(h_done, 2)]),
                    (10, "moe_w2", 2, [(y_done, 1)]), (11, "moe_w1", 4, [(h_done, 3)])]
            def load(i, waits, place, name, e):
                for sem, value in waits:
                    sp.wait_ge(sem, i * 2 + value)
                src = a[name][layer][bass.ds(2 * i + e, 1)].rearrange("e r n -> (e r) n").rearrange("(c p) n -> p c n", p=P)
                dst = k.ring[:, place % NS, :].rearrange("p (c n) -> p c n", c=2 if name == "moe_w2" else DC)
                sp.dma_start(dst, src).then_inc(k.ring_in[place % NS], 16)

            for place, name, e, waits in body:
                load(0, waits[:1], place, name, e)
            with sp.Fori(0, 5) as i:
                for place, name, e, waits in body:
                    sp.wait_ge(h_done, 1)
                    load(i, [(sem, value + 2) for sem, value in waits], place, name, e + 2)
            prefetch(k, sp, first + 36, first + 66)

        @block.gpsimd
        def _(pool):
            def put(b):
                pool.wait_ge(y_half0, b + 1)
                pool.wait_ge(y_half1, b + 1)
                pool.dma_start(a["y_rows"][P * b:P * b + P, :], ys[b % 2]).then_inc(y_out[b % 2], 16)

            for b in range(BLOCKS):
                if b >= 2:
                    pool.wait_ge(turned, b - 1)
                nc.gpsimd.indirect_dma_start(rows[b % 2], None, a["h_rows"],
                                             bass.IndirectOffsetOnAxis(ap=k.block_tokens[:, b:b + 1], axis=0)).then_inc(gathered[b % 2], 16)
                if b >= 4:
                    put(b - 4)
            for b in range(BLOCKS - 4, BLOCKS):
                put(b)
            pool.wait_ge(y_out0, 16 * ((BLOCKS + 1) // 2))
            pool.wait_ge(y_out1, 16 * (BLOCKS // 2))

        @block.scalar
        def _(act):
            def turn_out(i, b):
                act.wait_ge(turned, 2 * i + (b + 1))
                if b >= 2:
                    act.wait_ge(h_done, 2 * i + (b - 1))
                for g in range(2):
                    nc.scalar.copy(cols_[b % 2][:, 4 * g:4 * g + 4, :], k.psum[:, g, :].rearrange("p (c s) -> p c s", c=4)).then_inc(turn_read, 1)

            def gate(i, b):
                act.wait_ge(h_done, 2 * i + (b + 1))
                if b >= 2:
                    act.wait_ge(hid_ok, 2 * i + (b - 1))
                nc.scalar.activation(silu[b % 2], k.psum[:, 2 + b % 2, 0:2 * P].rearrange("p (f s) -> p f s", f=2),
                                     ACT.Silu).then_inc(silu_ok, 1)

            def store(i, b):
                act.wait_ge(y_done, 2 * i + (b + 1))
                if b >= 2:
                    act.wait_ge(y_out[b % 2], 16 * i + 16 * (b // 2))
                nc.scalar.copy(ys[b % 2][:, 0:512], k.psum[:, 4 + 2 * (b % 2), :]).then_inc(y_half0, 1)

            turn_out(0, 0)
            gate(0, 0)
            turn_out(0, 1)
            gate(0, 1)
            turn_out(0, 2)
            store(0, 0)
            gate(0, 2)
            turn_out(0, 3)
            store(0, 1)
            with act.Fori(0, LOOPS) as i:
                gate(i, 3)
                turn_out(i, 4)
                store(i, 2)
                gate(i, 4)
                turn_out(i, 5)
                store(i, 3)
            gate(0, BLOCKS - 2)
            turn_out(0, BLOCKS - 1)
            store(0, BLOCKS - 3)
            gate(0, BLOCKS - 1)
            store(0, BLOCKS - 2)
            store(0, BLOCKS - 1)

        @block.vector
        def _(dve):
            def hidden(i, b):
                dve.wait_ge(silu_ok, 2 * i + (b + 1))
                if b >= 2:
                    dve.wait_ge(y_done, 2 * i + (b - 1))
                nc.vector.tensor_tensor(hid[b % 2], silu[b % 2], k.psum[:, 2 + b % 2, 2 * P:4 * P].rearrange("p (f s) -> p f s", f=2),
                                        ALU.mult).then_inc(hid_ok, 1)

            def store(i, b):
                dve.wait_ge(y_done, 2 * i + (b + 1))
                if b >= 2:
                    dve.wait_ge(y_out[b % 2], 16 * i + 16 * (b // 2))
                nc.vector.tensor_copy(ys[b % 2][:, 512:D], k.psum[:, 5 + 2 * (b % 2), :]).then_inc(y_half1, 1)

            hidden(0, 0)
            hidden(0, 1)
            store(0, 0)
            hidden(0, 2)
            store(0, 1)
            with dve.Fori(0, LOOPS) as i:
                hidden(i, 3)
                store(i, 2)
                hidden(i, 4)
                store(i, 3)
            hidden(0, BLOCKS - 2)
            store(0, BLOCKS - 3)
            hidden(0, BLOCKS - 1)
            store(0, BLOCKS - 2)
            store(0, BLOCKS - 1)


def phase_moe_out(k, layer, x_slab):
    nc, a = k.nc, k.a
    fetched = [k.sem(f"moe{layer}_fetched{n}") for n in range(NT)]
    weighed, summed, y_turned, x_added = (k.sem(f"moe{layer}_{n}") for n in ("weighed", "summed", "y_turned", "x_added"))
    got = [k.tok3(S_R), k.tok3(S_PF)]
    x = k.act3(x_slab)
    weight = k.ws[:, WEIGHT_AT:WEIGHT_AT + 2 * NT].rearrange("p (k n) -> p k n", k=2)

    @k.block()
    def _(block):
        @block.gpsimd
        def _(pool):
            for n in range(NT):
                for i in range(2):
                    nc.gpsimd.indirect_dma_start(got[i][:, n, :], None, a["y_rows"],
                                                 bass.IndirectOffsetOnAxis(ap=k.slots[:, NT * i + n:NT * i + n + 1], axis=0)).then_inc(fetched[n], 16)

        @block.tensor
        def _(pe):
            for n in range(NT):
                pe.wait_ge(summed, n + 1)
                for c in range(DC):
                    last = nc.tensor.transpose(k.psum[:, c, P * n:P * n + P], got[1][:, n, P * c:P * c + P], k.ident[:])
                    if n == NT - 1:
                        last.then_inc(y_turned, 1)

        @block.vector
        def _(dve):
            for n in range(NT):
                dve.wait_ge(fetched[n], 32)
                nc.vector.tensor_scalar(got[0][:, n, :], got[0][:, n, :], weight[:, 0, n:n + 1], None, ALU.mult).then_inc(weighed, 1)
                dve.wait_ge(weighed, n + 1)
                nc.vector.scalar_tensor_tensor(got[1][:, n, :], got[1][:, n, :], weight[:, 1, n:n + 1], got[0][:, n, :],
                                               ALU.mult, ALU.add).then_inc(summed, 1)
            for c in range(DC):
                dve.wait_ge(y_turned, c + 1)
                residual(k, dve, x, c, k.psum[:, c, 0:T], 40, x_added)


def phase_qkv(k):
    nc, a = k.nc, k.a
    first = k.taken
    k.taken += 12
    proj, read_out, kt_done, kt_ok, stored = (k.sem("qkv_" + n) for n in ("done", "read", "kt_done", "kt_ok", "stored"))
    padded, rpb_in, pad_out, cap_in, bias_in, capped = (
        k.sem("bias_" + n) for n in ("padded", "rpb_in", "pad_out", "cap_in", "in", "capped"))
    q_lat = k.sem("q_lat_ok")
    ctx_in, kc_done, kc_ok = (k.sem("ctx_" + n) for n in ("in", "kc_done", "kc_ok"))
    h, q3, k3, v3 = k.act3(S_Y), k.act3(S_PF), k.act3(S_PB), k.tok3(S_V)
    new_k = k.ws[:, 0:D]
    pad = k.ws[0:H, 1024:1024 + 15 * P].rearrange("h (r n) -> h r n", r=15)
    cap = k.ws[:, 3000:3064]
    MID = GRID - WIN_C
    slabs = k.slab[:, S_R:S_K + 1, :].rearrange("p s n -> p (s n)")
    bias = slabs[:, 0:H * 6 * GRID].rearrange("p (h e n) -> p h e n", h=H, e=6)
    k_tok, v_tok = k.slab[:, S_NKK, 0:D], k.slab[:, S_NKK, D:2 * D]
    kc = k.slab[:, S_NKK, 2 * D:3 * D].rearrange("p (c t) -> p c t", c=DC)

    def bank(o):
        return k.psum[:, o % 6, :]

    @k.block()
    def _(block):
        @block.tensor
        def _(pe):
            o = 0
            for j in range(12):
                w = piece_cols(take_piece(k, pe, first + j))
                for m in range(2 if j < 8 else NT):
                    if o >= 6:
                        pe.wait_ge(read_out, o - 5)
                    for c in range(DC):
                        if j < 8:
                            last = nc.tensor.matmul(bank(o)[:, 0:T], w[:, c, P * m:P * m + P], h[:, c, :], start=c == 0, stop=c == DC - 1)
                        else:
                            last = nc.tensor.matmul(bank(o)[:, 0:256], h[:, c, P * m:P * m + P], w[:, c, :], start=c == 0, stop=c == DC - 1)
                    last.then_inc(proj, 1)
                    o += 1
                k.used[first + j] = (proj, o)
                if j == 8:
                    pe.wait_ge(read_out, 16)
                    for c in range(DC):
                        last = nc.tensor.transpose(k.psum[:, 6 + c // 4, P * (c % 4):P * (c % 4) + P], k3[:, c, 0:CTX], k.ident[:])
                    last.then_inc(kt_done, 1)
            pe.wait_ge(kt_ok, 1)
            pe.wait_ge(ctx_in, 32)
            for c in range(DC):
                last = nc.tensor.transpose(k.psum[:, 6 + c // 4, P * (c % 4):P * (c % 4) + P], k_tok[:, P * c:P * c + P], k.ident[:])
            last.then_inc(kc_done, 1)

        @block.sync
        def _(sp):
            sp.dma_start(k_tok, a["cache_na_k"][0, 0].rearrange("t h d -> t (h d)")).then_inc(ctx_in, 16)
            sp.dma_start(v_tok, a["cache_na_v"][0, 0].rearrange("t h d -> t (h d)")).then_inc(ctx_in, 16)
            prefetch(k, sp, first, first + 12)
            sp.wait_ge(kt_ok, 1)
            sp.dma_start(a["new_k"][0, 0].rearrange("t h d -> t (h d)"), new_k).then_inc(stored, 16)
            sp.wait_ge(read_out, 28)
            sp.dma_start(a["new_v"][0, 0].rearrange("t h d -> t (h d)"), v3[:, 0, :]).then_inc(stored, 16)
            sp.wait_ge(stored, 32)

        @block.scalar
        def _(act):
            act.wait_ge(padded, 1)
            act.dma_start(pad[:, :, MID:MID + 31], a["na_rpb"][0]).then_inc(rpb_in, 16)
            act.wait_ge(rpb_in, 16)
            act.dma_start(a["scratch"], pad).then_inc(pad_out, 16)
            act.dma_start(cap, a["c_cap"]).then_inc(cap_in, 16)
            act.wait_ge(pad_out, 16)
            for half in range(2):
                for e in range(6):
                    row = e + 5 - half
                    src = bass.AP(tensor=a["scratch"].tensor, offset=row * P, ap=[[1, GRID], [15 * P, H], [1, GRID]])
                    act.dma_start(bias[64 * half:64 * half + 64, :, e, :], src).then_inc(bias_in, 16)
            for o in range(28):
                act.wait_ge(proj, o + 1)
                if o < 8:
                    nc.scalar.mul(q3[:, o, CTX:T].rearrange("p (r n) -> p r n", n=GRID),
                                  bank(o)[:, CTX:T].rearrange("p (r n) -> p r n", n=GRID)[:, :, ::-1], HD ** -0.5).then_inc(q_lat, 1)
                    nc.scalar.mul(q3[:, o, 0:CTX], bank(o)[:, 0:CTX], HD ** -0.5).then_inc(read_out, 1)
                elif o < 16:
                    nc.scalar.copy(k3[:, o - 8, :], bank(o)[:, 0:T]).then_inc(read_out, 1)
                else:
                    j, n = divmod(o - 16, NT)
                    nc.scalar.copy(v3[:, n, 256 * j:256 * j + 256], bank(o)[:, 0:256]).then_inc(read_out, 1)

        @block.vector
        def _(dve):
            nc.vector.memset(k.ws[0:H, 1024:1024 + 15 * P], 0.0).then_inc(padded, 1)
            dve.wait_ge(kt_done, 1)
            nc.vector.tensor_copy(new_k.rearrange("p (b n) -> p b n", b=2), k.psum[:, 6:8, :]).then_inc(kt_ok, 1)
            dve.wait_ge(bias_in, 192)
            dve.wait_ge(cap_in, 16)
            for g in range(4):
                part = bias[:, 4 * g:4 * g + 4].rearrange("p h e n -> p (h e) n")
                nc.vector.tensor_tensor(part, part, cap.unsqueeze(1).to_broadcast([P, 24, GRID]), ALU.min).then_inc(capped, 1)
            dve.wait_ge(kc_done, 1)
            nc.vector.tensor_copy(kc.rearrange("p c t -> p (c t)").rearrange("p (b n) -> p b n", b=2), k.psum[:, 6:8, :]).then_inc(kc_ok, 1)


def phase_attention(k):
    nc = k.nc
    staged, s_done, s_ok, m_ok, e_ok, pt_done, pt_ok, o_done, r_ok, o_ok = (
        k.sem("att_" + n) for n in ("staged", "s_done", "s_ok", "m_ok", "e_ok", "pt_done", "pt_ok", "o_done", "r_ok", "o_ok"))
    q3, k3, v3, o3 = k.act3(S_PF), k.act3(S_PB), k.tok3(S_V), k.tok3(S_AF)
    slabs = k.slab[:, S_R:S_K + 1, :].rearrange("p s n -> p (s n)")
    bias = slabs[:, 0:H * 6 * GRID].rearrange("p (h n) -> p h n", h=H)
    v_ctx = k.slab[:, S_NKK, D:2 * D]
    kc = k.slab[:, S_NKK, 2 * D:3 * D].rearrange("p (c t) -> p c t", c=DC)
    LK = LAT + CTX
    UNITS = [(0, 1), (1, 1), (0, 0), (0, 2), (1, 2), (1, 0)]
    PASSES = H // 2
    sets = [[k.ws[:, at + lo:at + hi] for lo, hi in ((0, T), (T, 2 * T), (2 * T, 2 * T + P))] for at in (0, 6600)]
    probs = [k.ws[:, 1024 + LK * i:1024 + LK * i + (LK if n else CTX)] for i, (e, n) in enumerate(UNITS)]
    turned = [k.ws[:, 4096 + LK * i:4096 + LK * i + (LK if n else CTX)] for i, (e, n) in enumerate(UNITS)]
    neg_max, total, inverse = (k.ws[:, 8000 + 8 * i:8006 + 8 * i] for i in range(3))

    def passes(eng, one):
        one(0, 0, first=True)
        with eng.Fori(0, PASSES // 2 - 1) as half:
            for odd in (1, 0):
                one(2 * half + (2 - odd), odd)
        one(PASSES - 1, 1, last=True)

    def ahead(c, i):
        return (c, i + 3) if i < 3 else (c + 1, i - 3)

    @k.block()
    def _(block):
        @block.tensor
        def _(pe):
            def scores(c, odd, i):
                e, n = UNITS[i]
                qs, ks, kcs = sets[odd]
                rows = slice(64 * e, 64 * e + 64)
                if i == 0:
                    pe.wait_ge(staged, 3 * c + 3)
                q, out = qs[rows, P * n:P * n + P], k.psum[:, i, :]
                if n:
                    nc.tensor.matmul(out[:, 0:LAT], q, ks[rows, CTX:T], start=True, stop=True)
                    nc.tensor.matmul(out[:, LAT:LK], q, kcs[rows, :], start=True, stop=True).then_inc(s_done, 1)
                else:
                    nc.tensor.matmul(out[:, 0:CTX], q, ks[rows, 0:CTX], start=True, stop=True).then_inc(s_done, 1)

            def values(c, i):
                e, n = UNITS[i]
                pe.wait_ge(pt_ok, 6 * c + (i + 1))
                out = k.psum[:, i, 448:512]
                tiles = [v3[:, 1], v3[:, 2], v_ctx] if n else [v3[:, 0]]
                for j, v in enumerate(tiles):
                    last = nc.tensor.matmul(out, turned[i][:, P * j:P * j + P], v[:, bass.ds(P * c + 64 * e, 64)],
                                            start=j == 0, stop=j == len(tiles) - 1)
                last.then_inc(o_done, 1)

            def one(c, odd, first=False, last=False):
                for i, (e, n) in enumerate(UNITS):
                    pe.wait_ge(e_ok, 6 * c + (i + 1))
                    if not first or i >= 2:
                        pe.wait_ge(pt_ok, 6 * c + (i - 1))
                    for j in range(3 if n else 1):
                        ins = nc.tensor.matmul(k.psum[:, 6 + i % 2, P * j:P * j + P], probs[i][:, P * j:P * j + P], k.ident[:],
                                               start=True, stop=True)
                    ins.then_inc(pt_done, 1)
                    if i:
                        values(c, i - 1)
                    elif not first:
                        values(c - 1, 5)
                    if i >= 3:
                        pe.wait_ge(o_ok, 6 * c + (i - 2))
                    if i < 3 or not last:
                        scores(ahead(c, i)[0], odd if i < 3 else 1 - odd, ahead(c, i)[1])
                if last:
                    values(c, 5)

            for i in range(3):
                scores(0, 0, i)
            passes(pe, one)

        @block.gpsimd
        def _(pool):
            def stage(c, odd):
                for dst, src in zip(sets[odd], (q3, k3, kc)):
                    nc.gpsimd.tensor_copy(dst, src[:, bass.ds(c, 1), :].squeeze(1)).then_inc(staged, 1)

            stage(0, 0)
            stage(1, 1)
            with pool.Fori(0, PASSES // 2 - 1) as half:
                for odd in range(2):
                    pool.wait_ge(s_done, 12 * half + (6 * odd + 6))
                    stage(2 * half + (2 + odd), odd)

        @block.scalar
        def _(act):
            def exponents(c, i):
                act.wait_ge(m_ok, 6 * c + (i + 1))
                src = probs[i] if UNITS[i][1] else k.psum[:, i, 0:CTX]
                nc.scalar.activation(probs[i], src, ACT.Exp, bias=neg_max[:, i:i + 1], accum_out=total[:, i:i + 1]).then_inc(e_ok, 1)

            def one(c, odd, first=False, last=False):
                for i, (e, n) in enumerate(UNITS):
                    act.wait_ge(pt_done, 6 * c + (i + 1))
                    nc.scalar.copy(turned[i], k.psum[:, 6 + i % 2, 0:LK if n else CTX]).then_inc(pt_ok, 1)
                    if i < 3 or not last:
                        exponents(*ahead(c, i))

            for i in range(3):
                exponents(0, i)
            passes(act, one)

        @block.vector
        def _(dve):
            def maxima(c, i):
                e, n = UNITS[i]
                src = k.psum[:, i, :]
                dve.wait_ge(s_done, 6 * c + (i + 1))
                if n:
                    lo = GRID * (2 - 2 * (n - 1))
                    nc.vector.tensor_tensor(probs[i][:, 0:LAT], src[:, 0:LAT],
                                            bias[:, bass.ds(2 * c + e, 1), lo:lo + LAT].squeeze(1), ALU.add).then_inc(s_ok, 1)
                    nc.vector.tensor_copy(probs[i][:, LAT:LK], src[:, LAT:LK]).then_inc(s_ok, 1)
                    dve.wait_ge(s_ok, 8 * c + 2 * sum(tile > 0 for _, tile in UNITS[:i + 1]))
                nc.vector.tensor_reduce(neg_max[:, i:i + 1], probs[i] if n else src[:, 0:CTX], AX.X, ALU.max, negate=True).then_inc(m_ok, 1)

            def normalise(c, i):
                e, n = UNITS[i]
                dve.wait_ge(o_done, 6 * c + (i + 1))
                dve.wait_ge(r_ok, 6 * c + (i + 1))
                nc.vector.tensor_scalar(o3[:, n, bass.ds(P * c + 64 * e, 64)], k.psum[:, i, 448:512], inverse[:, i:i + 1],
                                        None, ALU.mult).then_inc(o_ok, 1)

            def one(c, odd, first=False, last=False):
                for i in range(len(UNITS)):
                    if i:
                        normalise(c, i - 1)
                    elif not first:
                        normalise(c - 1, 5)
                    dve.wait_ge(e_ok, 6 * c + (i + 1))
                    nc.vector.reciprocal(inverse[:, i:i + 1], total[:, i:i + 1]).then_inc(r_ok, 1)
                    if i < 3 or not last:
                        maxima(*ahead(c, i))
                if last:
                    normalise(c, 5)

            for i in range(3):
                maxima(0, i)
            passes(dve, one)


def phase_na_out(k):
    nc = k.nc
    first = k.taken
    k.taken += 6
    o_turned, o_read, done, added = (k.sem("na_out_" + n) for n in ("turned", "read", "done", "added"))
    o3, ot, x = k.tok3(S_AF), k.act3(S_Y), k.act3(S_AB)

    @k.block()
    def _(block):
        @block.tensor
        def _(pe):
            for c in range(DC):
                if c >= 4:
                    pe.wait_ge(o_read, 2 * (c - 3))
                for n in range(NT):
                    last = nc.tensor.transpose(k.psum[:, c % 4, P * n:P * n + P], o3[:, n, P * c:P * c + P], k.ident[:])
                last.then_inc(o_turned, 1)
            for m in range(DC):
                if m % 2 == 0:
                    w = piece_cols(take_piece(k, pe, first + m // 2))
                if m >= 4:
                    pe.wait_ge(added, 2 * (m - 3))
                for c in range(DC):
                    pe.wait_ge(o_read, 2 * (c + 1))
                    last = nc.tensor.matmul(k.psum[:, 4 + m % 4, 0:T], w[:, c, P * (m % 2):P * (m % 2) + P], ot[:, c, :],
                                            start=c == 0, stop=c == DC - 1)
                last.then_inc(done, 1)
                k.used[first + m // 2] = (done, m + 1)

        @block.sync
        def _(sp):
            prefetch(k, sp, first, first + 6)

        @block.scalar
        def _(act):
            for c in range(DC):
                act.wait_ge(o_turned, c + 1)
                nc.scalar.copy(ot[:, c, 0:CTX], k.psum[:, c % 4, 0:CTX]).then_inc(o_read, 1)
                nc.scalar.copy(ot[:, c, CTX:T].rearrange("p (r n) -> p r n", n=GRID),
                               k.psum[:, c % 4, CTX:T].rearrange("p (r n) -> p r n", n=GRID)[:, :, ::-1]).then_inc(o_read, 1)

        @block.vector
        def _(dve):
            for m in range(DC):
                dve.wait_ge(done, m + 1)
                residual(k, dve, x, m, k.psum[:, 4 + m % 4, 0:T], 16, added)


def phase_store(k, y_slab, out_slab):
    nc = k.nc
    turned, read_out, stored = (k.sem("store_" + n) for n in ("turned", "read", "stored"))
    y, out = k.act3(y_slab), k.tok3(out_slab)

    @k.block()
    def _(block):
        @block.tensor
        def _(pe):
            for n in range(NT):
                for g in range(2):
                    for c in range(4):
                        last = nc.tensor.transpose(k.psum[:, 2 * n + g, P * c:P * c + P], y[:, 4 * g + c, P * n:P * n + P], k.ident[:])
                    last.then_inc(turned, 1)

        @block.vector
        def _(dve):
            for n in range(NT):
                for g in range(2):
                    dve.wait_ge(turned, 2 * n + g + 1)
                    nc.vector.tensor_copy(out[:, n, 512 * g:512 * g + 512], k.psum[:, 2 * n + g, :]).then_inc(read_out, 1)

        @block.sync
        def _(sp):
            for n in range(NT):
                sp.wait_ge(read_out, 2 * n + 2)
                dst = k.a["y_prompt"][0] if n == 0 else k.a["y_sample"][0, P * (n - 1):P * n, :]
                sp.dma_start(dst, out[:, n, :]).then_inc(stored, 16)
            sp.wait_ge(stored, 48)


INPUTS = ["x_prompt", "x_sample", "c", "state_rwkv", "cache_na_k", "cache_na_v", "c_ctx", "norm_mix", "norm_ffn",
          "ada_w", "ada_b", "rwkv_mu", "rwkv_w_r", "rwkv_w_k", "rwkv_w_v", "rwkv_w_o", "rwkv_w0", "rwkv_w1", "rwkv_w2",
          "rwkv_a0", "rwkv_a1", "rwkv_a2", "rwkv_g1", "rwkv_g2", "rwkv_k_k", "rwkv_k_a", "rwkv_r_k", "rwkv_lnx_g",
          "rwkv_lnx_b", "na_w_qkv", "na_w_o", "na_rpb", "moe_w_grp", "moe_b_grp", "moe_w_exp", "moe_b_exp",
          "moe_w1", "moe_w3", "moe_w2", "final_norm"]
OUTPUTS = [("y_prompt", (1, CTX, D)), ("y_sample", (1, LAT, D)), ("new_state", (1, 1, 2, H, HD, HD)),
           ("new_k", (1, 1, CTX, H, HD)), ("new_v", (1, 1, CTX, H, HD))]


def program(nc, a, ctx):
    k = Kernel(nc, a, ctx)
    add_pieces(k)
    steps = [
        lambda: phase_inputs(k),
        lambda: phase_ada(k, 0),
        lambda: phase_norm(k, "mix0", S_Y, S_PF, S_NKK, V_NMIX, 0),
        lambda: phase_rwkv_project(k),
        lambda: phase_rwkv_rates(k),
        lambda: phase_scan(k),
        lambda: phase_rwkv_out(k),
        lambda: phase_norm(k, "ffn0", S_AB, S_Y, S_PF, V_NFFN, 24, router=0),
        lambda: phase_router(k, 0, S_Y),
        lambda: phase_moe(k, 0),
        lambda: phase_moe_out(k, 0, S_AB),
        lambda: phase_ada(k, 1),
        lambda: phase_norm(k, "mix1", S_AB, S_Y, S_PF, V_NMIX + 8, 0),
        lambda: phase_qkv(k),
        lambda: phase_attention(k),
        lambda: phase_na_out(k),
        lambda: phase_norm(k, "ffn1", S_AB, S_Y, S_PF, V_NFFN + 8, 24, router=1),
        lambda: phase_router(k, 1, S_Y),
        lambda: phase_moe(k, 1),
        lambda: phase_moe_out(k, 1, S_AB),
        lambda: phase_norm(k, "final", S_AB, S_Y, S_PF, V_FIN, None),
        lambda: phase_store(k, S_Y, S_PF),
    ]
    for s in steps:
        s()
    return k


def kernel(**inputs):
    import concourse.bacc as bacc
    from concourse.bass_utils import run_bass_kernel_spmd

    nc = bacc.Bacc("TRN2", target_bir_lowering=False, num_devices=1)
    arrays, a = {}, {}
    given = {n: np.ascontiguousarray(inputs[n]) for n in INPUTS}
    for n, x in {**given, **constants()}.items():
        arrays[n] = x
        a[n] = nc.dram_tensor(n, x.shape, F32, kind="ExternalInput").ap()
    for n, shape in OUTPUTS:
        a[n] = nc.dram_tensor(n, shape, F32, kind="ExternalOutput").ap()
    a["h_rows"] = nc.dram_tensor("h_rows", (T, D), F32, kind="Internal").ap()
    a["y_rows"] = nc.dram_tensor("y_rows", (BLOCKS * P, D), F32, kind="Internal").ap()
    a["scratch"] = nc.dram_tensor("scratch", (H, 15, P), F32, kind="Internal").ap()
    with ExitStack() as ctx:
        program(nc, a, ctx)
    got = run_bass_kernel_spmd(nc, [arrays], core_ids=[0]).results[0]
    return tuple(got[n] for n, _ in OUTPUTS)
```
